# Optimizing a Trainium2 kernel written in Bass

```python
import jax
import jax.numpy as jnp
from jax import lax
import numpy as np
import math
import jax, jax.numpy as jnp

D_MODEL = 1024
BATCH = 1
SEQ = 512
DEPTH = 1

GRID_W = 64
CTX_LEN = 256
D_MIX = D_MODEL
D_MLSTM = D_MIX // 2
D_CONV = D_MIX - D_MLSTM
M_HEADS = 4
V_DIM = D_MLSTM // M_HEADS
QK_DIM = V_DIM // 2
D_QK = M_HEADS * QK_DIM
N_GATES = 4 * M_HEADS
CHUNK = 128
CONV_WIDTH = 31
N_EXPERTS = 64
TOP_K = 8
D_EXPERT = D_MODEL // 4
D_SHARED = D_EXPERT
ROUTE_SCALE = 2.5
EXPERT_BLOCK = 128
EPS = 1e-6
IN_SPLITS = (D_QK, 2 * D_QK, 2 * D_QK + D_MLSTM, 2 * D_QK + 2 * D_MLSTM,
             2 * D_QK + 2 * D_MLSTM + N_GATES, 2 * D_QK + 2 * D_MLSTM + N_GATES + D_CONV)
D_IN = 2 * D_QK + 2 * D_MLSTM + N_GATES + 2 * D_CONV


def _rms_norm(x, g):
    xf = x.astype(jnp.float32)
    y = xf * lax.rsqrt(jnp.mean(xf * xf, axis=-1, keepdims=True) + EPS)
    return (y * g.astype(jnp.float32)).astype(x.dtype)

def _layer_norm(x, g, b):
    xf = x.astype(jnp.float32)
    mu = jnp.mean(xf, axis=-1, keepdims=True)
    xc = xf - mu
    y = xc * lax.rsqrt(jnp.mean(xc * xc, axis=-1, keepdims=True) + EPS)
    return (y * g.astype(jnp.float32) + b.astype(jnp.float32)).astype(x.dtype)

def _modulate(h, shift, scale):
    return h * (1.0 + scale) + shift

def _heads(t, n):
    B, T, _ = t.shape
    return t.reshape(B, T, n, -1).transpose(0, 2, 1, 3).astype(jnp.float32)

def _mlstm_chunk_states(k, v, log_i, log_f, state0):
    B, H, T, dk = k.shape
    dv = v.shape[-1]
    nc = T // CHUNK
    kc = k.reshape(B, H, nc, CHUNK, dk)
    vc = v.reshape(B, H, nc, CHUNK, dv)
    li = log_i.reshape(B, H, nc, CHUNK)
    b = jnp.cumsum(log_f.reshape(B, H, nc, CHUNK), axis=-1)
    b_tot = b[..., -1]
    g = b_tot[..., None] - b + li
    m_loc = jnp.max(g, axis=-1)
    w = jnp.exp(g - m_loc[..., None])
    C_loc = jnp.einsum('bhcs,bhcsv,bhcsk->bhcvk', w, vc, kc)
    n_loc = jnp.einsum('bhcs,bhcsk->bhck', w, kc)

    def step(state, xs):
        C, n, m = state
        bt, ml, Cl, nl = xs
        m_new = jnp.maximum(bt + m, ml)
        a = jnp.exp(bt + m - m_new)
        e = jnp.exp(ml - m_new)
        C_new = a[..., None, None] * C + e[..., None, None] * Cl
        n_new = a[..., None] * n + e[..., None] * nl
        return (C_new, n_new, m_new), (C, n, m)

    xs = (jnp.moveaxis(b_tot, 2, 0), jnp.moveaxis(m_loc, 2, 0),
          jnp.moveaxis(C_loc, 2, 0), jnp.moveaxis(n_loc, 2, 0))
    final, prev = lax.scan(step, state0, xs)
    prev = (jnp.moveaxis(prev[0], 0, 2), jnp.moveaxis(prev[1], 0, 2), jnp.moveaxis(prev[2], 0, 2))
    return prev, final

def _mlstm_chunk_outputs(q, k, v, log_i, log_f, prev):
    C_prev, n_prev, m_prev = prev
    B, H, T, dk = q.shape
    dv = v.shape[-1]
    nc = T // CHUNK
    qc = q.reshape(B, H, nc, CHUNK, dk)
    kc = k.reshape(B, H, nc, CHUNK, dk)
    vc = v.reshape(B, H, nc, CHUNK, dv)
    li = log_i.reshape(B, H, nc, CHUNK)
    b = jnp.cumsum(log_f.reshape(B, H, nc, CHUNK), axis=-1)
    lower = jnp.tril(jnp.ones((CHUNK, CHUNK), dtype=bool))
    log_d = jnp.where(lower, b[..., :, None] - b[..., None, :] + li[..., None, :], -jnp.inf)
    a = b + m_prev[..., None]
    m_t = jnp.maximum(a, jnp.max(log_d, axis=-1))
    s = jnp.einsum('bhctk,bhcsk->bhcts', qc, kc) * jnp.exp(log_d - m_t[..., None])
    e_int = jnp.exp(a - m_t)
    num = (jnp.einsum('bhcts,bhcsv->bhctv', s, vc)
           + e_int[..., None] * jnp.einsum('bhcvk,bhctk->bhctv', C_prev, qc))
    den = jnp.sum(s, axis=-1) + e_int * jnp.einsum('bhck,bhctk->bhct', n_prev, qc)
    h = num / jnp.maximum(jnp.abs(den), jnp.exp(-m_t))[..., None]
    return h.reshape(B, H, T, dv)

def _mlstm_direction(q, k, v, log_i, log_f, state0, reverse, want_out):
    if reverse:
        q, k, v = jnp.flip(q, 2), jnp.flip(k, 2), jnp.flip(v, 2)
        log_i, log_f = jnp.flip(log_i, 2), jnp.flip(log_f, 2)
    prev, final = _mlstm_chunk_states(k, v, log_i, log_f, state0)
    h = None
    if want_out:
        h = _mlstm_chunk_outputs(q, k, v, log_i, log_f, prev)
        if reverse:
            h = jnp.flip(h, 2)
    return h, final

def _mlstm_bidir(q, k, v, gates, states0, want_out):
    h_f, s_f = _mlstm_direction(q, k, v, gates[:, 0], jax.nn.log_sigmoid(gates[:, 1]),
                                states0[0], False, want_out)
    h_b, s_b = _mlstm_direction(q, k, v, gates[:, 2], jax.nn.log_sigmoid(gates[:, 3]),
                                states0[1], True, want_out)
    h = h_f + h_b if want_out else None
    return h, (s_f, s_b)

def _project(h, w_in, b_in, b_gate):
    B, T, _ = h.shape
    z = h @ w_in + b_in
    q, k, v, o, gt, ga, gb = jnp.split(z, IN_SPLITS, axis=-1)
    q = _heads(q, M_HEADS)
    k = _heads(k, M_HEADS) * (QK_DIM ** -0.5)
    v = _heads(v, M_HEADS)
    gates = (gt.reshape(B, T, 4, M_HEADS).transpose(0, 2, 3, 1).astype(jnp.float32)
             + b_gate.astype(jnp.float32)[None, :, :, None])
    u = ga * jax.nn.sigmoid(gb)
    return (q, k, v, gates), o, u

def _mlstm_group_out(h, o, norm_g):
    B, H, T, dv = h.shape
    hn = h * lax.rsqrt(jnp.mean(h * h, axis=-1, keepdims=True) + EPS) * norm_g.astype(jnp.float32)[:, None, :]
    return hn.transpose(0, 2, 1, 3).reshape(B, T, H * dv).astype(o.dtype) * jax.nn.sigmoid(o)

def _conv_group_out(u, conv_w, conv_b, ln_g, ln_b, rows):
    B, T, C = u.shape
    lhs = u.reshape(B * rows, T // rows, C)
    y = lax.conv_general_dilated(lhs, conv_w.astype(u.dtype)[:, None, :], (1,), 'SAME',
                                 dimension_numbers=('NWC', 'WIO', 'NWC'), feature_group_count=C)
    y = y.reshape(B, T, C) + conv_b
    return jax.nn.silu(_layer_norm(y, ln_g, ln_b))

def _token_mixer(hx, hc, w_in, b_in, b_gate, norm_g, conv_w, conv_b, ln_g, ln_b, w_out, b_out, ctx_out):
    B = hx.shape[0]
    rows = hx.shape[1] // GRID_W
    mx_in, ox, ux = _project(hx, w_in, b_in, b_gate)
    mc_in, oc, uc = _project(hc, w_in, b_in, b_gate)
    zero = (jnp.zeros((B, M_HEADS, V_DIM, QK_DIM), jnp.float32),
            jnp.zeros((B, M_HEADS, QK_DIM), jnp.float32),
            jnp.zeros((B, M_HEADS), jnp.float32))
    hc_m, ctx_states = _mlstm_bidir(*mc_in, (zero, zero), ctx_out)
    hx_m, _ = _mlstm_bidir(*mx_in, ctx_states, True)
    yx = jnp.concatenate([_mlstm_group_out(hx_m, ox, norm_g),
                          _conv_group_out(ux, conv_w, conv_b, ln_g, ln_b, rows)], axis=-1) @ w_out + b_out
    yc = None
    if ctx_out:
        yc = jnp.concatenate([_mlstm_group_out(hc_m, oc, norm_g),
                              _conv_group_out(uc, conv_w, conv_b, ln_g, ln_b, 1)], axis=-1) @ w_out + b_out
    return yx, yc

def _moe_ffn(h, w_router, b_router, we_gate, we_up, we_down, ws_gate, ws_up, ws_down):
    B, T, D = h.shape
    hf = h.reshape(-1, D)
    nt = hf.shape[0]
    s = jax.nn.sigmoid((hf @ w_router).astype(jnp.float32))
    _, idx = lax.top_k(s + b_router.astype(jnp.float32), TOP_K)
    s_sel = jnp.take_along_axis(s, idx, axis=-1)
    wts = s_sel / jnp.sum(s_sel, axis=-1, keepdims=True) * ROUTE_SCALE
    n_assign = nt * TOP_K
    e_flat = idx.reshape(-1)
    tok_flat = jnp.repeat(jnp.arange(nt, dtype=jnp.int32), TOP_K)
    order = jnp.argsort(e_flat)
    e_s, tok_s, w_s = e_flat[order], tok_flat[order], wts.reshape(-1)[order]
    counts = jnp.bincount(e_flat, length=N_EXPERTS)
    starts = jnp.cumsum(counts) - counts
    padded = (counts + EXPERT_BLOCK - 1) // EXPERT_BLOCK * EXPERT_BLOCK
    pend = jnp.cumsum(padded)
    pstarts = pend - padded
    dest = pstarts[e_s] + (jnp.arange(n_assign, dtype=jnp.int32) - starts[e_s])
    n_rows = -(-(n_assign + N_EXPERTS * (EXPERT_BLOCK - 1)) // EXPERT_BLOCK) * EXPERT_BLOCK
    n_blocks = n_rows // EXPERT_BLOCK
    row_tok = jnp.full((n_rows,), nt, jnp.int32).at[dest].set(tok_s)
    row_w = jnp.zeros((n_rows,), jnp.float32).at[dest].set(w_s)
    block_e = jnp.minimum(jnp.searchsorted(pend, jnp.arange(n_blocks) * EXPERT_BLOCK, side='right'),
                          N_EXPERTS - 1)
    hpad = jnp.concatenate([hf, jnp.zeros((1, D), hf.dtype)], axis=0)

    def body(acc, xs):
        rows, rw, e = xs
        xb = hpad[rows]
        y = (jax.nn.silu(xb @ we_gate[e]) * (xb @ we_up[e])) @ we_down[e]
        return acc.at[rows].add(y * rw[:, None].astype(y.dtype)), None

    acc, _ = lax.scan(body, jnp.zeros((nt + 1, D), hf.dtype),
                      (row_tok.reshape(n_blocks, EXPERT_BLOCK), row_w.reshape(n_blocks, EXPERT_BLOCK), block_e))
    shared = (jax.nn.silu(hf @ ws_gate) * (hf @ ws_up)) @ ws_down
    return (acc[:nt] + shared).reshape(B, T, D)

def first_inputs(seed: int = 0) -> dict:
    key = jax.random.key(seed)
    ks = jax.random.split(key, 32)

    def nrm(k, shape, scale):
        return jax.random.normal(k, shape, jnp.float32) * scale

    D = D_MODEL
    b_gate = jnp.stack([nrm(ks[12], (DEPTH, M_HEADS), 0.1),
                        3.0 + 3.0 * jax.random.uniform(ks[13], (DEPTH, M_HEADS), jnp.float32),
                        nrm(ks[14], (DEPTH, M_HEADS), 0.1),
                        3.0 + 3.0 * jax.random.uniform(ks[15], (DEPTH, M_HEADS), jnp.float32)], axis=1)
    return {
        "x": nrm(ks[0], (BATCH, SEQ, D), 1.0),
        "c": nrm(ks[1], (BATCH, D), 1.0),
        "ctx": nrm(ks[2], (BATCH, CTX_LEN, D), 1.0),
        "c_ctx": nrm(ks[3], (D,), 1.0),
        "w_ada": nrm(ks[4], (DEPTH, D, 6 * D), 0.5 * D ** -0.5),
        "b_ada": nrm(ks[5], (DEPTH, 6 * D), 0.02),
        "g_pre_mix": 1.0 + nrm(ks[6], (DEPTH, D), 0.1),
        "g_post_mix": 1.0 + nrm(ks[7], (DEPTH, D), 0.1),
        "g_pre_ffn": 1.0 + nrm(ks[8], (DEPTH, D), 0.1),
        "g_post_ffn": 1.0 + nrm(ks[9], (DEPTH, D), 0.1),
        "w_in": nrm(ks[10], (DEPTH, D, D_IN), D ** -0.5),
        "b_in": nrm(ks[11], (DEPTH, D_IN), 0.02),
        "b_gate": b_gate,
        "mlstm_norm_g": 1.0 + nrm(ks[16], (DEPTH, M_HEADS, V_DIM), 0.1),
        "conv_w": nrm(ks[17], (DEPTH, CONV_WIDTH, D_CONV), CONV_WIDTH ** -0.5),
        "conv_b": nrm(ks[18], (DEPTH, D_CONV), 0.02),
        "conv_ln_g": 1.0 + nrm(ks[19], (DEPTH, D_CONV), 0.1),
        "conv_ln_b": nrm(ks[20], (DEPTH, D_CONV), 0.02),
        "w_out": nrm(ks[21], (DEPTH, D_MIX, D), D_MIX ** -0.5),
        "b_out": nrm(ks[22], (DEPTH, D), 0.02),
        "w_router": nrm(ks[23], (DEPTH, D, N_EXPERTS), D ** -0.5),
        "b_router": nrm(ks[24], (DEPTH, N_EXPERTS), 0.01),
        "we_gate": nrm(ks[25], (DEPTH, N_EXPERTS, D, D_EXPERT), D ** -0.5),
        "we_up": nrm(ks[26], (DEPTH, N_EXPERTS, D, D_EXPERT), D ** -0.5),
        "we_down": nrm(ks[27], (DEPTH, N_EXPERTS, D_EXPERT, D), D_EXPERT ** -0.5),
        "ws_gate": nrm(ks[28], (DEPTH, D, D_SHARED), D ** -0.5),
        "ws_up": nrm(ks[29], (DEPTH, D, D_SHARED), D ** -0.5),
        "ws_down": nrm(ks[30], (DEPTH, D_SHARED, D), D_SHARED ** -0.5),
    }

def first_block(x, c, ctx, c_ctx, w_ada, b_ada, g_pre_mix, g_post_mix, g_pre_ffn, g_post_ffn,
              w_in, b_in, b_gate, mlstm_norm_g, conv_w, conv_b, conv_ln_g, conv_ln_b, w_out, b_out,
              w_router, b_router, we_gate, we_up, we_down, ws_gate, ws_up, ws_down):
    for l in range(DEPTH):
        ctx_out = l < DEPTH - 1
        mx = [t[:, None, :] for t in jnp.split(jax.nn.silu(c) @ w_ada[l] + b_ada[l], 6, axis=-1)]
        mc = jnp.split(jax.nn.silu(c_ctx) @ w_ada[l] + b_ada[l], 6, axis=-1)
        hx = _modulate(_rms_norm(x, g_pre_mix[l]), mx[0], mx[1])
        hc = _modulate(_rms_norm(ctx, g_pre_mix[l]), mc[0], mc[1])
        yx, yc = _token_mixer(hx, hc, w_in[l], b_in[l], b_gate[l], mlstm_norm_g[l], conv_w[l], conv_b[l],
                              conv_ln_g[l], conv_ln_b[l], w_out[l], b_out[l], ctx_out)
        x = x + mx[2] * _rms_norm(yx, g_post_mix[l])
        hx = _modulate(_rms_norm(x, g_pre_ffn[l]), mx[3], mx[4])
        x = x + mx[5] * _rms_norm(_moe_ffn(hx, w_router[l], b_router[l], we_gate[l], we_up[l], we_down[l],
                                           ws_gate[l], ws_up[l], ws_down[l]), g_post_ffn[l])
        if ctx_out:
            ctx = ctx + mc[2] * _rms_norm(yc, g_post_mix[l])
            hc = _modulate(_rms_norm(ctx, g_pre_ffn[l]), mc[3], mc[4])
            ctx = ctx + mc[5] * _rms_norm(_moe_ffn(hc, w_router[l], b_router[l], we_gate[l], we_up[l], we_down[l],
                                                 ws_gate[l], ws_up[l], ws_down[l]), g_post_ffn[l])
    return x


DEPTH_2 = 2

HEAD_DIM = 64
N_HEADS_MOBA = 8
N_HEADS_DIL = 8
N_HEADS_EVEN = N_HEADS_MOBA + N_HEADS_DIL
EVEN_WIDTH = N_HEADS_EVEN * HEAD_DIM
MOBA_BLOCK = 256
MOBA_TOPK = 3
MOBA_Q_CHUNK = 32
DIL_PAIRS = ((128, 1), (512, 4), (2048, 16))
N_HEADS_DIFF = 8
DIFF_HEAD_DIM = 64
DIFF_WIDTH = N_HEADS_DIFF * 2 * DIFF_HEAD_DIM
DIFF_Q_BLOCK = 128
DIFF_EPS = 1e-5
D_FF = 2816
CONV_WIDTH_2 = 3
ROPE_THETA = 10000.0
NORM_EPS = 1e-6
N_EVEN = (DEPTH_2 + 1) // 2
N_ODD = DEPTH_2 // 2


f32 = jnp.float32

def rms_norm(x, g, eps=NORM_EPS):
    xf = x.astype(f32)
    y = xf * lax.rsqrt(jnp.mean(xf * xf, axis=-1, keepdims=True) + eps)
    return (y * g.astype(f32)).astype(x.dtype)

def rope(t):
    S, dim = t.shape[-2], t.shape[-1]
    half = dim // 2
    inv = 1.0 / (ROPE_THETA ** (jnp.arange(half, dtype=f32) * 2.0 / dim))
    ang = jnp.arange(S, dtype=f32)[:, None] * inv[None, :]
    cos, sin = jnp.cos(ang), jnp.sin(ang)
    tf = t.astype(f32)
    t1, t2 = tf[..., :half], tf[..., half:]
    return jnp.concatenate([t1 * cos - t2 * sin, t2 * cos + t1 * sin], axis=-1).astype(t.dtype)

def moba_attention(q, k, v):
    B, H, S, hd = q.shape
    nb = -(-S // MOBA_BLOCK)
    Sp = nb * MOBA_BLOCK
    pad = ((0, 0), (0, 0), (0, Sp - S), (0, 0))
    kb = jnp.pad(k, pad).reshape(B, H, nb, MOBA_BLOCK, hd)
    vb = jnp.pad(v, pad).reshape(B, H, nb, MOBA_BLOCK, hd)
    kmean = jnp.mean(kb.astype(f32), axis=3)
    n_sel = min(MOBA_TOPK, nb - 1)
    scale = hd ** -0.5
    n_chunks = S // MOBA_Q_CHUNK

    def chunk(c):
        q0 = c * MOBA_Q_CHUNK
        qc = lax.dynamic_slice_in_dim(q, q0, MOBA_Q_CHUNK, axis=2)
        blk = q0 // MOBA_BLOCK
        qpos = q0 + jnp.arange(MOBA_Q_CHUNK)
        own_k = lax.dynamic_index_in_dim(kb, blk, axis=2, keepdims=False)
        own_v = lax.dynamic_index_in_dim(vb, blk, axis=2, keepdims=False)
        kpos = blk * MOBA_BLOCK + jnp.arange(MOBA_BLOCK)
        s_own = jnp.einsum('bhqd,bhkd->bhqk', qc, own_k).astype(f32) * scale
        s_own = jnp.where(kpos[None, :] <= qpos[:, None], s_own, -jnp.inf)
        if n_sel == 0:
            p = jax.nn.softmax(s_own, axis=-1)
            return jnp.einsum('bhqk,bhkd->bhqd', p.astype(v.dtype), own_v)
        gate = jnp.einsum('bhqd,bhnd->bhqn', qc.astype(f32), kmean)
        gate = jnp.where(jnp.arange(nb) < blk, gate, -jnp.inf)
        _, idx = lax.top_k(gate, n_sel)
        valid = jnp.arange(n_sel) < blk
        take = jax.vmap(jax.vmap(lambda tb, ib: tb[ib]))
        sel_k = take(kb, idx)
        sel_v = take(vb, idx)
        s_sel = jnp.einsum('bhqd,bhqjkd->bhqjk', qc, sel_k).astype(f32) * scale
        s_sel = jnp.where(valid[:, None], s_sel, -jnp.inf)
        s_all = jnp.concatenate(
            [s_own, s_sel.reshape(B, H, MOBA_Q_CHUNK, n_sel * MOBA_BLOCK)], axis=-1)
        p = jax.nn.softmax(s_all, axis=-1).astype(v.dtype)
        p_own = p[..., :MOBA_BLOCK]
        p_sel = p[..., MOBA_BLOCK:].reshape(B, H, MOBA_Q_CHUNK, n_sel, MOBA_BLOCK)
        return (jnp.einsum('bhqk,bhkd->bhqd', p_own, own_v)
                + jnp.einsum('bhqjk,bhqjkd->bhqd', p_sel, sel_v))

    out = lax.map(chunk, jnp.arange(n_chunks))
    return out.transpose(1, 2, 0, 3, 4).reshape(B, H, S, hd)

def dilated_window_attention(q, k, v, window, dilation):
    B, H, S, hd = q.shape
    n = window // dilation
    L = S // dilation
    nblk = -(-L // n)
    Lp = nblk * n

    def to_residue(t):
        t = t.reshape(B, H, L, dilation, hd).transpose(0, 1, 3, 2, 4)
        return jnp.pad(t, ((0, 0), (0, 0), (0, 0), (0, Lp - L), (0, 0)))

    def band(t):
        own = t.reshape(B, H, dilation, nblk, n, hd)
        prev = jnp.pad(t, ((0, 0), (0, 0), (0, 0), (n, 0), (0, 0)))[..., :Lp, :]
        prev = prev.reshape(B, H, dilation, nblk, n, hd)
        return jnp.concatenate([prev, own], axis=-2)

    qb = to_residue(q).reshape(B, H, dilation, nblk, n, hd)
    kw = band(to_residue(k))
    vw = band(to_residue(v))
    s = jnp.einsum('bhrnqd,bhrnkd->bhrnqk', qb, kw).astype(f32) * (hd ** -0.5)
    i = jnp.arange(n)[:, None]
    j = jnp.arange(2 * n)[None, :]
    blk = jnp.arange(nblk)[:, None, None]
    dist = n + i - j
    kidx = (blk - 1) * n + j
    mask = (dist >= 0) & (dist <= n) & (kidx >= 0)
    s = jnp.where(mask, s, -jnp.inf)
    m = jnp.max(s, axis=-1, keepdims=True)
    p = jnp.exp(s - m)
    den = jnp.sum(p, axis=-1, keepdims=True)
    o = jnp.einsum('bhrnqk,bhrnkd->bhrnqd', (p / den).astype(v.dtype), vw)
    lse = (m + jnp.log(den))[..., 0]
    o = o.reshape(B, H, dilation, Lp, hd)[:, :, :, :L, :]
    o = o.transpose(0, 1, 3, 2, 4).reshape(B, H, S, hd)
    lse = lse.reshape(B, H, dilation, Lp)[:, :, :, :L].transpose(0, 1, 3, 2).reshape(B, H, S)
    return o, lse

def dilated_mixture(q, k, v):
    results = [dilated_window_attention(q, k, v, w, r) for (w, r) in DIL_PAIRS]
    outs = jnp.stack([o for (o, _) in results]).astype(f32)
    lses = jnp.stack([l for (_, l) in results])
    wts = jax.nn.softmax(lses, axis=0)
    return jnp.einsum('gbhs,gbhsd->bhsd', wts, outs).astype(q.dtype)

def even_mixer(h, w_in, w_out):
    B, S, _ = h.shape
    qkv = (h @ w_in).reshape(B, S, 3, N_HEADS_EVEN, HEAD_DIM).transpose(2, 0, 3, 1, 4)
    q, k, v = rope(qkv[0]), rope(qkv[1]), qkv[2]
    na = N_HEADS_MOBA
    a = moba_attention(q[:, :na], k[:, :na], v[:, :na])
    b = dilated_mixture(q[:, na:], k[:, na:], v[:, na:])
    o = jnp.concatenate([a, b], axis=1).transpose(0, 2, 1, 3).reshape(B, S, EVEN_WIDTH)
    return o @ w_out

def diff_attention(q, k, v, lam):
    B, H, _, S, d = q.shape
    nq = S // DIFF_Q_BLOCK
    scale = d ** -0.5
    qb = q.reshape(B, H, 2, nq, DIFF_Q_BLOCK, d).transpose(3, 0, 1, 2, 4, 5)
    kpos = jnp.arange(S)

    def block(args):
        qblk, bi = args
        qpos = bi * DIFF_Q_BLOCK + jnp.arange(DIFF_Q_BLOCK)
        s = jnp.einsum('bhcqd,bhckd->bhcqk', qblk, k).astype(f32) * scale
        s = jnp.where(kpos[None, :] <= qpos[:, None], s, -jnp.inf)
        p = jax.nn.softmax(s, axis=-1)
        a = p[:, :, 0] - lam * p[:, :, 1]
        return jnp.einsum('bhqk,bhkd->bhqd', a.astype(v.dtype), v)

    out = lax.map(block, (qb, jnp.arange(nq)))
    return out.transpose(1, 2, 0, 3, 4).reshape(B, H, S, 2 * d)

def diff_mixer(h, w_qkv, lq1, lk1, lq2, lk2, subln, w_out, lambda_init):
    B, S, _ = h.shape
    H, d = N_HEADS_DIFF, DIFF_HEAD_DIM
    qkv = h @ w_qkv
    q = qkv[..., :2 * H * d].reshape(B, S, H, 2, d).transpose(0, 2, 3, 1, 4)
    k = qkv[..., 2 * H * d:4 * H * d].reshape(B, S, H, 2, d).transpose(0, 2, 3, 1, 4)
    v = qkv[..., 4 * H * d:].reshape(B, S, H, 2 * d).transpose(0, 2, 1, 3)
    q, k = rope(q), rope(k)
    lam = (jnp.exp(jnp.sum(lq1.astype(f32) * lk1.astype(f32)))
           - jnp.exp(jnp.sum(lq2.astype(f32) * lk2.astype(f32))) + lambda_init)
    o = diff_attention(q, k, v, lam)
    o = rms_norm(o, subln, DIFF_EPS) * (1.0 - lambda_init)
    return o.transpose(0, 2, 1, 3).reshape(B, S, DIFF_WIDTH) @ w_out

def causal_depthwise_conv(u, w, b):
    C = u.shape[-1]
    y = lax.conv_general_dilated(
        u, w[:, None, :].astype(u.dtype), window_strides=(1,),
        padding=((CONV_WIDTH_2 - 1, 0),), dimension_numbers=('NWC', 'WIO', 'NWC'),
        feature_group_count=C)
    return y + b

def conv_ffn(h, w_up, conv_w, conv_b, w_down):
    u = causal_depthwise_conv(h @ w_up, conv_w, conv_b)
    gate, val = u[..., :D_FF], u[..., D_FF:]
    return (jax.nn.silu(gate) * val) @ w_down

def second_inputs(seed: int = 0) -> dict:
    key = jax.random.key(seed)
    ks = jax.random.split(key, 18)

    def nrm(kk, shape, scale):
        return jax.random.normal(kk, shape, f32) * scale

    d = DIFF_HEAD_DIM
    return {
        'x': nrm(ks[0], (BATCH, SEQ, D_MODEL), 1.0),
        'even_norm': 1.0 + nrm(ks[1], (N_EVEN, D_MODEL), 0.1),
        'even_w_in': nrm(ks[2], (N_EVEN, D_MODEL, 3 * EVEN_WIDTH), D_MODEL ** -0.5),
        'even_w_out': nrm(ks[3], (N_EVEN, EVEN_WIDTH, D_MODEL), EVEN_WIDTH ** -0.5),
        'odd_norm': 1.0 + nrm(ks[4], (N_ODD, D_MODEL), 0.1),
        'odd_w_qkv': nrm(ks[5], (N_ODD, D_MODEL, 3 * DIFF_WIDTH), D_MODEL ** -0.5),
        'odd_lambda_q1': nrm(ks[6], (N_ODD, d), 0.1),
        'odd_lambda_k1': nrm(ks[7], (N_ODD, d), 0.1),
        'odd_lambda_q2': nrm(ks[8], (N_ODD, d), 0.1),
        'odd_lambda_k2': nrm(ks[9], (N_ODD, d), 0.1),
        'odd_subln': 1.0 + nrm(ks[10], (N_ODD, 2 * d), 0.1),
        'odd_w_out': nrm(ks[11], (N_ODD, DIFF_WIDTH, D_MODEL), DIFF_WIDTH ** -0.5),
        'ffn_norm': 1.0 + nrm(ks[12], (DEPTH_2, D_MODEL), 0.1),
        'ffn_w_up': nrm(ks[13], (DEPTH_2, D_MODEL, 2 * D_FF), D_MODEL ** -0.5),
        'ffn_conv_w': nrm(ks[14], (DEPTH_2, CONV_WIDTH_2, 2 * D_FF), CONV_WIDTH_2 ** -0.5),
        'ffn_conv_b': nrm(ks[15], (DEPTH_2, 2 * D_FF), 0.02),
        'ffn_w_down': nrm(ks[16], (DEPTH_2, D_FF, D_MODEL), D_FF ** -0.5),
        'final_norm': 1.0 + nrm(ks[17], (D_MODEL,), 0.1),
    }

def second_block(x, even_norm, even_w_in, even_w_out, odd_norm, odd_w_qkv,
              odd_lambda_q1, odd_lambda_k1, odd_lambda_q2, odd_lambda_k2, odd_subln,
              odd_w_out, ffn_norm, ffn_w_up, ffn_conv_w, ffn_conv_b, ffn_w_down,
              final_norm):
    for layer in range(DEPTH_2):
        i = layer // 2
        if layer % 2 == 0:
            x = x + even_mixer(rms_norm(x, even_norm[i]), even_w_in[i], even_w_out[i])
        else:
            lambda_init = 0.8 - 0.6 * math.exp(-0.3 * layer)
            x = x + diff_mixer(rms_norm(x, odd_norm[i]), odd_w_qkv[i],
                               odd_lambda_q1[i], odd_lambda_k1[i],
                               odd_lambda_q2[i], odd_lambda_k2[i],
                               odd_subln[i], odd_w_out[i], lambda_init)
        x = x + conv_ffn(rms_norm(x, ffn_norm[layer]), ffn_w_up[layer],
                         ffn_conv_w[layer], ffn_conv_b[layer], ffn_w_down[layer])
    return rms_norm(x, final_norm)


def setup_inputs(seed=0):
    out = dict(first_inputs(seed))
    for name, value in second_inputs(seed + 1).items():
        if name != "x":
            out[name + "_2"] = value
    return out


def reference(
    x, c, ctx, c_ctx, w_ada, b_ada, g_pre_mix, g_post_mix, g_pre_ffn, g_post_ffn, w_in, b_in,
    b_gate, mlstm_norm_g, conv_w, conv_b, conv_ln_g, conv_ln_b, w_out, b_out, w_router,
    b_router, we_gate, we_up, we_down, ws_gate, ws_up, ws_down, even_norm_2, even_w_in_2,
    even_w_out_2, odd_norm_2, odd_w_qkv_2, odd_lambda_q1_2, odd_lambda_k1_2, odd_lambda_q2_2,
    odd_lambda_k2_2, odd_subln_2, odd_w_out_2, ffn_norm_2, ffn_w_up_2, ffn_conv_w_2,
    ffn_conv_b_2, ffn_w_down_2, final_norm_2,
):
    x = first_block(
        x, c, ctx, c_ctx, w_ada, b_ada, g_pre_mix, g_post_mix, g_pre_ffn, g_post_ffn, w_in,
        b_in, b_gate, mlstm_norm_g, conv_w, conv_b, conv_ln_g, conv_ln_b, w_out, b_out,
        w_router, b_router, we_gate, we_up, we_down, ws_gate, ws_up, ws_down,
    )
    return second_block(
        x, even_norm_2, even_w_in_2, even_w_out_2, odd_norm_2, odd_w_qkv_2, odd_lambda_q1_2,
        odd_lambda_k1_2, odd_lambda_q2_2, odd_lambda_k2_2, odd_subln_2, odd_w_out_2, ffn_norm_2,
        ffn_w_up_2, ffn_conv_w_2, ffn_conv_b_2, ffn_w_down_2, final_norm_2,
    )


_drawn_inputs = setup_inputs


def setup_inputs(seed=0):
    import zlib

    import numpy as np

    out = dict(_drawn_inputs(seed))
    spreads = {}
    factors = {'conv_ln_b': 2.89, 'odd_lambda_q1_2': 2.777, 'ffn_conv_b_2': 2.751}
    for name, (base, spread) in spreads.items():
        noise = np.random.default_rng([zlib.crc32(name.encode()), seed]).standard_normal(out[name].shape)
        drawn = base * np.exp(spread * noise) if base else spread * noise
        out[name] = jnp.asarray(drawn.astype(out[name].dtype))
    for name, factor in factors.items():
        out[name] = (out[name] * factor).astype(out[name].dtype)
    return out
```

```python
from contextlib import ExitStack

import concourse.bass as bass
import numpy as np
from concourse import mybir

F32 = mybir.dt.float32
I32 = mybir.dt.int32
F32R = mybir.dt.float32r
ALU = mybir.AluOpType
ACT = mybir.ActivationFunctionType

P = 128
D = 1024
KT = D // P
SEQ = 512
CTX = 256
TT = SEQ // P
ALLT = SEQ + CTX
H_M = 4
QK = 64
DV = 128
D_QK = H_M * QK
D_ML = H_M * DV
D_CONV = 512
CW = 31
GRID = 64
ROWS = SEQ // GRID
HALO = CW // 2
N_EXP = 64
TOP_K = 8
D_EXP = 256
MAX_BLOCKS = (SEQ * TOP_K + N_EXP * (P - 1)) // P
ROUTE_SCALE = 2.5
D_FF = 2816
FT = D_FF // P
HD = 64
N_PAIR = 8
EPS = 1e-6
DIFF_EPS = 1e-5
NEG = -1.0e30
LAMBDA_INIT = 0.8 - 0.6 * float(np.exp(-0.3))


class Columns:

    def __init__(self, sizes):
        self.at, self.n = {}, 0
        for name, n in sizes:
            self.at[name] = (self.n, n)
            self.n += n

    def of(self, tile, name, j=0, n=None):
        a, size = self.at[name]
        n = size - j if n is None else n
        return tile[:, a + j:a + j + n]


VEC = Columns([
    ("c", KT * 2), ("b_ada", 48 * 2),
    ("g_pre_mix", KT), ("g_post_mix", KT), ("g_pre_ffn", KT), ("g_post_ffn", KT),
    ("b_q", 2), ("b_k", 2), ("b_ga", 4), ("b_gb", 4), ("b_gates", 2),
    ("conv_w", 4 * CW), ("conv_b", 4), ("ln_g", 4), ("ln_b", 4), ("b_out", KT),
    ("even_norm", KT), ("odd_norm", KT), ("ffn_norm", 2 * KT), ("final_norm", KT),
    ("ffn_conv", 2 * FT * 8), ("subln", 1), ("lambda", 4),
])
ROWV = Columns([("b_v", D_ML), ("b_o", D_ML), ("norm_g", D_ML), ("b_router", N_EXP)])
CONST = Columns([
    ("ident", P), ("ones", P), ("inv_d", P), ("inv_c", P), ("inv_v", P), ("before", P), ("slot", P),
    ("neg_block", P), ("eps", 1), ("diff_eps", 1), ("part", 1), ("token", TT), ("one", 1),
    ("mask_fwd", ALLT), ("mask_bwd", ALLT),
])
W_IN_TILES = [("gb", D_CONV), ("ga", D_CONV), ("q", D_QK), ("k", D_QK), ("gates", 16), ("v", D_ML), ("o", D_ML)]
W_IN = Columns([(n, KT * w) for n, w in W_IN_TILES])


def _cols(v, pad=P):
    return np.ascontiguousarray(np.asarray(v).reshape(-1, P).T)


def _kmaj(w):
    return w.reshape(-1, P, w.shape[1]).transpose(1, 0, 2)


def _flat(a):
    return np.ascontiguousarray(a).reshape(P, -1)


def constants():
    f = np.float32
    p = np.arange(P)[:, None]
    j = np.arange(P)[None, :]
    one = np.ones((P, P), f)
    fwd = np.zeros((P, ALLT), f)
    fwd[:, ALLT - P:] = np.where(j <= p, 0, NEG)
    bwd = np.zeros((P, ALLT), f)
    bwd[:, :P] = np.where(j >= p, 0, NEG)
    token = p + P * np.arange(TT)[None, :]
    parts = {
        "ident": np.eye(P), "ones": one, "inv_d": one / D, "inv_c": one / D_CONV, "inv_v": one / P,
        "before": (p < j), "slot": np.broadcast_to(j, (P, P)),
        "neg_block": np.broadcast_to(-P * j, (P, P)), "eps": np.full((P, 1), EPS),
        "diff_eps": np.full((P, 1), DIFF_EPS), "part": p, "token": token, "one": np.ones((P, 1)),
        "mask_fwd": fwd, "mask_bwd": bwd,
    }
    const = np.concatenate([np.asarray(parts[n], f) for n in CONST.at], axis=1)
    sel = np.zeros((16, 2, H_M, 2, P), f)
    for h in range(H_M):
        sel[h, 0, h, 0] = 1
        sel[4 + h, 0, h, 1] = -1
        sel[8 + h, 1, h, 0] = 1
        sel[12 + h, 1, h, 1] = 1
    d = p + (SEQ - P) - np.arange(SEQ)[None, :]
    count = (d <= 128).astype(f) + (d % 4 == 0) + (d % 16 == 0)
    plain = np.where(d >= 0, 0, NEG)
    mixed = np.where((d >= 0) & (count > 0), np.log(np.maximum(count, 1)) * HD ** 0.5, NEG)
    amask = np.stack([plain, plain, mixed, mixed], 1).astype(f)
    half = HD // 2
    inv = (1.0 / (np.float32(10000.0) ** (np.arange(half, dtype=f) * f(2.0) / f(HD)))).astype(f)
    ang = (np.arange(SEQ, dtype=f)[None, :] * inv[:, None]).astype(f)
    cos, sin = np.cos(ang).astype(f), np.sin(ang).astype(f)
    rope = np.stack([np.tile(cos, (4, 1)), np.concatenate([sin, -sin, sin, -sin])], 1)
    return {"const": const, "sel": sel.reshape(16, -1), "amask": _flat(amask), "rope": _flat(rope)}


def layouts(x, c, ctx, c_ctx, w_ada, b_ada, g_pre_mix, g_post_mix, g_pre_ffn, g_post_ffn, w_in, b_in,
            b_gate, mlstm_norm_g, conv_w, conv_b, conv_ln_g, conv_ln_b, w_out, b_out, w_router,
            b_router, we_gate, we_up, we_down, ws_gate, ws_up, ws_down, even_norm_2, even_w_in_2,
            even_w_out_2, odd_norm_2, odd_w_qkv_2, odd_lambda_q1_2, odd_lambda_k1_2, odd_lambda_q2_2,
            odd_lambda_k2_2, odd_subln_2, odd_w_out_2, ffn_norm_2, ffn_w_up_2, ffn_conv_w_2,
            ffn_conv_b_2, ffn_w_down_2, final_norm_2):
    def pad(v):
        out = np.zeros((P,), np.float32)
        out[:len(v)] = v
        return out[:, None]

    cuts = np.cumsum([D_QK, D_QK, D_ML, D_ML, 16, D_CONV])
    names = ("q", "k", "v", "o", "gates", "ga", "gb")
    wi = dict(zip(names, np.split(w_in[0], cuts, axis=1)))
    bi = dict(zip(names, np.split(b_in[0], cuts)))
    taps = np.concatenate([ffn_conv_w_2, ffn_conv_b_2[:, None]], 1)
    taps = taps.reshape(2, 4, 2, FT, P).transpose(4, 0, 3, 2, 1)
    vec = {
        "c": _flat(np.stack([_cols(c[0]), _cols(c_ctx)], 2)),
        "b_ada": _flat(np.broadcast_to(_cols(b_ada[0])[:, :, None], (P, 48, 2))),
        "g_pre_mix": _cols(g_pre_mix[0]), "g_post_mix": _cols(g_post_mix[0]),
        "g_pre_ffn": _cols(g_pre_ffn[0]), "g_post_ffn": _cols(g_post_ffn[0]),
        "b_q": _cols(bi["q"]), "b_k": _cols(bi["k"]), "b_ga": _cols(bi["ga"]), "b_gb": _cols(bi["gb"]),
        "b_gates": np.concatenate([pad(bi["gates"]), pad(b_gate[0].reshape(-1))], 1),
        "conv_w": _flat(conv_w[0].reshape(CW, 4, P).transpose(2, 1, 0)),
        "conv_b": _cols(conv_b[0]), "ln_g": _cols(conv_ln_g[0]), "ln_b": _cols(conv_ln_b[0]),
        "b_out": _cols(b_out[0]), "even_norm": _cols(even_norm_2[0]), "odd_norm": _cols(odd_norm_2[0]),
        "ffn_norm": _cols(ffn_norm_2.reshape(-1)), "final_norm": _cols(final_norm_2),
        "ffn_conv": _flat(taps), "subln": _cols(odd_subln_2[0]),
        "lambda": np.concatenate([pad(v[0]) for v in (odd_lambda_q1_2, odd_lambda_k1_2,
                                                      odd_lambda_q2_2, odd_lambda_k2_2)], 1),
    }
    row = {"b_v": bi["v"], "b_o": bi["o"], "norm_g": mlstm_norm_g[0].reshape(-1), "b_router": b_router[0]}
    qkv = {}
    for name, w in (("w_even", even_w_in_2[0]), ("w_odd", odd_w_qkv_2[0])):
        w = _kmaj(w).reshape(P, KT, 3, N_PAIR, P)
        qkv[name] = np.ascontiguousarray(w.transpose(3, 0, 2, 1, 4)).reshape(N_PAIR, P, -1)
    up = _kmaj(ffn_w_up_2[0]), _kmaj(ffn_w_up_2[1])
    up = np.stack([u.reshape(P, KT, 2, FT, P).transpose(3, 0, 2, 1, 4) for u in up])
    down = np.stack([_kmaj(w).reshape(P, FT, KT, P).transpose(2, 0, 1, 3) for w in ffn_w_down_2])
    gu = np.stack([we_gate[0], we_up[0]], 2).reshape(N_EXP, KT, P, 2 * D_EXP).transpose(0, 2, 1, 3)
    return {
        "x": _flat(_kmaj(np.concatenate([x[0], ctx[0]]).T)),
        "vec": np.concatenate([vec[n] for n in VEC.at], axis=1),
        "rowv": np.ascontiguousarray(np.broadcast_to(np.concatenate([row[n] for n in ROWV.at])[None], (P, ROWV.n))),
        "w_ada": np.ascontiguousarray(_kmaj(w_ada[0]).reshape(P, KT, 12, 512).transpose(2, 0, 1, 3)).reshape(12, P, -1),
        "w_in": np.concatenate([_flat(_kmaj(wi[n])) for n, _ in W_IN_TILES], axis=1),
        "w_out": _flat(_kmaj(w_out[0])), "w_router": _flat(_kmaj(w_router[0])),
        "w_gu": np.ascontiguousarray(gu).reshape(N_EXP, P, -1),
        "w_dn": np.ascontiguousarray(we_down[0].reshape(N_EXP, 2, P, D).transpose(0, 2, 1, 3)).reshape(N_EXP, P, -1),
        "ws_gu": _flat(_kmaj(np.concatenate([ws_gate[0], ws_up[0]], 1))), "ws_dn": _flat(_kmaj(ws_down[0])),
        **qkv,
        "w_eo": _flat(_kmaj(even_w_out_2[0])), "w_oo": _flat(_kmaj(odd_w_out_2[0])),
        "w_up": np.ascontiguousarray(up).reshape(2, FT, P, -1),
        "w_down": np.ascontiguousarray(down).reshape(2, KT, P, -1),
    }


class Steps:

    def __init__(self, sem):
        self.sem, self.n = sem, 0

    def __call__(self, eng, ins):
        self.n += 1
        ins.then_inc(self.sem, 1)
        eng.wait_ge(self.sem, self.n)


class Machine:

    def __init__(self, nc, stack):
        self.nc, self.stack, self.stage = nc, stack, 0

    def open(self, stack=None):
        self.stage += 1
        nc, stack, n, sems = self.nc, stack or ExitStack(), self.stage, []

        def clear():
            if sems:
                nc.clear_and_free_semaphores(sems)
                nc.all_engine_barrier()
        stack.callback(clear)

        def sb(name, shape, dt=F32):
            return stack.enter_context(self.nc.sbuf_tensor(f"{name}_{n}", shape, dt))

        def sem(name):
            sems.append(nc.alloc_semaphore(f"{name}_{n}"))
            return sems[-1]
        return stack, sb, sem


def load_and_modulation(m, d):
    nc, ps = m.nc, m.ps
    stack, sb, sem = m.open()
    N_AB = 6 * D // 512
    with stack:
        w = [sb(f"w_ada{s}", [P, KT, 512]) for s in range(2)]
        cs = sb("silu_c", [P, KT, 2])
        row = [sb(f"row{s}", [2, 512]) for s in range(2)]
        small_in, x_in, w_in = sem("small_in"), m.x_in, [sem("w_in0"), sem("w_in1")]
        silu_done, w_used, row_copied, turned, added, seen = (
            sem(s) for s in ("silu_done", "w_used", "row_copied", "turned", "added", "seen"))
        with nc.Block() as block:
            @block.sync
            def _(sp):
                sp.dma_start(m.vec[:], d["vec"]).then_inc(small_in, 16)
                for s in range(2):
                    sp.dma_start(w[s][:].rearrange("p k n -> p (k n)"), d["w_ada"][s]).then_inc(w_in[s], 16)
                sp.dma_start(m.const[:], d["const"]).then_inc(small_in, 16)
                sp.dma_start(m.rowv[:], d["rowv"]).then_inc(small_in, 16)
                sp.dma_start(m.x[:].rearrange("p k t -> p (k t)"), d["x"]).then_inc(x_in, 16)
                with sp.Fori(1, N_AB // 2) as g:
                    for s in range(2):
                        sp.wait_ge(w_used, 2 * g - 1 + s)
                        sp.dma_start(w[s][:].rearrange("p k n -> p (k n)"), d["w_ada"][2 * g + s]).then_inc(w_in[s], 16)
                sp.wait_ge(small_in, 48)
                sp.wait_ge(x_in, 16)

            @block.tensor
            def _(pe):
                ident = CONST.of(m.const, "ident")[0:2, 0:2]

                def product(n, s, loads):
                    pe.wait_ge(w_in[s], loads)
                    pe.wait_ge(row_copied, n + 1)
                    for k in range(KT):
                        mm = pe.matmul(ps[0:2, s, :], cs[:, k, :], w[s][:, k, :], start=(k == 0), stop=(k == KT - 1))
                    mm.then_inc(w_used, 1)

                def turn(n, s):
                    pe.wait_ge(row_copied, n + 3)
                    pe.wait_ge(added, n + 1)
                    pe.sem_inc(seen, 1)
                    for a in range(4):
                        mm = pe.transpose(ps[:, 2 + s, 2 * a:2 * a + 2], row[s][:, a * P:(a + 1) * P], ident)
                    mm.then_inc(turned, 1)

                pe.wait_ge(silu_done, 1)
                product(0, 0, 16)
                with pe.Fori(0, N_AB // 2 - 1) as g:
                    product(2 * g + 1, 1, 16 * g + 16)
                    turn(2 * g, 0)
                    product(2 * g + 2, 0, 16 * g + 32)
                    turn(2 * g + 1, 1)
                product(N_AB - 1, 1, 8 * N_AB)
                turn(N_AB - 2, 0)
                turn(N_AB - 1, 1)

            @block.scalar
            def _(act):
                act.wait_ge(small_in, 48)
                act.activation(cs[:].rearrange("p k c -> p (k c)"), VEC.of(m.vec, "c"), ACT.Silu).then_inc(silu_done, 1)
                act.sem_inc(row_copied, 2)
                with act.Fori(0, N_AB // 2) as g:
                    for s in range(2):
                        act.wait_ge(w_used, 2 * g + s + 1)
                        act.wait_ge(added, 2 * g + s + 1)
                        act.activation(row[s][:], ps[0:2, s, :], ACT.Copy).then_inc(row_copied, 1)

            @block.vector
            def _(dve):
                dve.sem_inc(added, 2)
                dve.wait_ge(small_in, 48)
                b_ada = VEC.of(m.vec, "b_ada")
                with dve.Fori(0, N_AB // 2) as g:
                    for s in range(2):
                        dve.wait_ge(turned, 2 * g + s + 1)
                        at = bass.ds(16 * g + 8 * s, 8)
                        dve.tensor_tensor(m.mod[:, at], ps[:, 2 + s, 0:8], b_ada[:, at], ALU.add).then_inc(added, 1)


class Split:

    def __init__(self, sb, name, shape):
        self.high, self.low = sb(name + "_high", shape, F32R), sb(name + "_low", shape, F32R)

    def passes(self, other):
        return (self.high, other.high), (self.high, other.low), (self.low, other.high)


def rms_norm(m, src, dst, groups, gain, shift=None, out=None):
    nc, ps, eps = m.nc, m.ps, CONST.of(m.const, "eps")
    inv_d = CONST.of(m.const, "inv_d")
    tokens = sum(n for _, n in groups)
    stack, sb, sem = m.open()
    with stack:
        sq = sb("sq", [P, KT, tokens])
        std, rstd = sb("std", [P, tokens]), sb("rstd", [P, tokens])
        sq_done, ms_done, std_done, rstd_done, scaled, shifted, rounded, stored = (
            sem(s) for s in ("sq_done", "ms_done", "std_done", "rstd_done", "scaled", "shifted", "rounded", "stored"))
        split = isinstance(dst, Split)
        in_sq = shift or split
        with nc.Block() as block:
            @block.scalar
            def _(act):
                for k in range(KT):
                    act.activation(sq[:, k, :], src[:, k, 0:tokens], ACT.Square).then_inc(sq_done, 1)
                for g, (t, n) in enumerate(groups):
                    act.wait_ge(ms_done, g + 1)
                    act.activation(std[:, t:t + n], ps[:, g, 0:n], ACT.Sqrt, bias=eps).then_inc(std_done, 1)
                if shift:
                    for g, (t, n) in enumerate(groups):
                        for k in range(KT):
                            act.wait_ge(scaled, g * KT + k + 1)
                            to = sq if split else dst
                            act.activation(to[:, k, t:t + n], sq[:, k, t:t + n], ACT.Identity, bias=shift(k, g)).then_inc(shifted, 1)
                if split:
                    for g, (t, n) in enumerate(groups):
                        for k in range(KT):
                            act.wait_ge(shifted if shift else scaled, g * KT + k + 1)
                            act.activation(dst.high[:, k, t:t + n], sq[:, k, t:t + n], ACT.Copy).then_inc(rounded, 1)

            @block.tensor
            def _(pe):
                for k in range(KT):
                    pe.wait_ge(sq_done, k + 1)
                    for g, (t, n) in enumerate(groups):
                        mm = pe.matmul(ps[:, g, 0:n], inv_d, sq[:, k, t:t + n], start=(k == 0), stop=(k == KT - 1))
                        if k == KT - 1:
                            mm.then_inc(ms_done, 1)

            @block.vector
            def _(dve):
                for g, (t, n) in enumerate(groups):
                    dve.wait_ge(std_done, g + 1)
                    dve.reciprocal(rstd[:, t:t + n], std[:, t:t + n]).then_inc(rstd_done, 1)
                for g, (t, n) in enumerate(groups):
                    dve.wait_ge(rstd_done, g + 1)
                    dve.wait_ge(ms_done, g + 1)
                    for k in range(KT):
                        to = sq if in_sq else dst
                        dve.scalar_tensor_tensor(to[:, k, t:t + n], src[:, k, t:t + n], gain(k, g), rstd[:, t:t + n],
                                                 ALU.mult, ALU.mult).then_inc(scaled, 1)
                if split:
                    for g, (t, n) in enumerate(groups):
                        for k in range(KT):
                            dve.wait_ge(rounded, g * KT + k + 1)
                            dve.tensor_tensor(dst.low[:, k, t:t + n], sq[:, k, t:t + n], dst.high[:, k, t:t + n].bitcast(F32),
                                              ALU.subtract)

            @block.sync
            def _(sp):
                if out is not None:
                    for k in range(KT):
                        sp.wait_ge(scaled, k + 1)
                        sp.dma_start(out[:, k, :], dst[:, k, 0:tokens]).then_inc(stored, 16)
                    sp.wait_ge(stored, 16 * KT)


def add_normed(m, y, gain):
    nc, ps = m.nc, m.ps
    stack, sb, sem = m.open()
    with stack:
        sq = sb("sq", [P, KT, SEQ])
        std, rstd = sb("std", [P, SEQ]), sb("rstd", [P, SEQ])
        sq_done, ms_done, std_done, rstd_done, scaled = (
            sem(s) for s in ("sq_done", "ms_done", "std_done", "rstd_done", "scaled"))
        with nc.Block() as block:
            @block.scalar
            def _(act):
                for k in range(KT):
                    act.activation(sq[:, k, :], y[:, k, :], ACT.Square).then_inc(sq_done, 1)
                act.wait_ge(ms_done, 1)
                act.activation(std[:], ps[:, 0, :], ACT.Sqrt, bias=CONST.of(m.const, "eps")).then_inc(std_done, 1)

            @block.tensor
            def _(pe):
                for k in range(KT):
                    pe.wait_ge(sq_done, k + 1)
                    mm = pe.matmul(ps[:, 0, :], CONST.of(m.const, "inv_d"), sq[:, k, :], start=(k == 0), stop=(k == KT - 1))
                mm.then_inc(ms_done, 1)

            @block.vector
            def _(dve):
                dve.wait_ge(std_done, 1)
                dve.reciprocal(rstd[:], std[:]).then_inc(rstd_done, 1)
                dve.wait_ge(rstd_done, 1)
                for k in range(KT):
                    dve.scalar_tensor_tensor(sq[:, k, :], y[:, k, :], gain(k), rstd[:], ALU.mult, ALU.mult).then_inc(scaled, 1)
                for k in range(KT):
                    dve.wait_ge(scaled, k + 1)
                    dve.tensor_tensor(m.x[:, k, 0:SEQ], sq[:, k, :], m.x[:, k, 0:SEQ], ALU.add)


def modulation_gain(m, name, part):
    nc = m.nc
    stack, sb, sem = m.open()
    with stack:
        with nc.Block() as block:
            @block.vector
            def _(dve):
                mod = m.mod[:].rearrange("p (j c) -> p j c", c=2)
                for c in range(2):
                    dve.scalar_tensor_tensor(m.gain[:, :, c], mod[:, KT * part:KT * part + KT, c], 1.0,
                                             VEC.of(m.vec, name), ALU.add, ALU.mult)


def gate_gain(m, name, part):
    nc = m.nc
    with nc.Block() as block:
        @block.vector
        def _(dve):
            mod = m.mod[:].rearrange("p (j c) -> p j c", c=2)
            dve.tensor_tensor(m.gain[:, :, 0], mod[:, KT * part:KT * part + KT, 0], VEC.of(m.vec, name), ALU.mult)


def project_in(m, d, mix):
    nc, ps = m.nc, m.ps
    stack, sb, sem = m.open()
    with stack:
        w_first = W_IN.n - 2 * KT * D_ML
        w = sb("w_in", [P, w_first])
        gb, u = sb("gate_b", [P, 4, SEQ]), sb("u", [P, 4, ROWS, GRID + 2 * HALO])
        acc = mix[:, 4:8, :]
        centre = u[:].rearrange("p j r t -> p (j r t)")[:, 0:4 * SEQ].rearrange("p (j t) -> p j t", j=4)
        stat = sb("conv_stat", [P, 2, SEQ])
        w_in = [sem(f"w_in_{n}") for n, _ in W_IN_TILES]
        bank_full, act_free, dve_free, sig, u_ready, dve_own, conv_sq, mean_done, centred, var_done, std_done, normed = (
            sem(s) for s in ("bank_full", "act_free", "dve_free", "sig", "u_ready", "dve_own", "conv_sq", "mean_done",
                             "centred", "var_done", "std_done", "normed"))

        def wt(name):
            a, n = W_IN.at[name]
            a -= w_first if name in ("v", "o") else 0
            return w[:, a:a + n].rearrange("p (k n) -> p k n", k=KT)

        x_, c_ = (0, SEQ), (SEQ, CTX)
        jobs = [("gb", j, x_, "act") for j in range(4)] + [("ga", j, x_, "dve") for j in range(4)]
        jobs += [("q", j, x_, "dve") for j in range(2)]
        jobs += [("k", j, t, "dve") for j in range(2) for t in (x_, c_)]
        jobs += [("gates", 0, t, "dve") for t in (x_, c_)]
        jobs += [("v", None, i, "act") for i in range(ALLT // P)] + [("o", None, i, "act") for i in range(TT)]
        NB = 6
        CB, VB = 6, 7

        def done_before(n, reader):
            return sum(1 for j in jobs[:n] if j[3] == reader)

        with nc.Block() as block:
            @block.sync
            def _(sp):
                for i, (name, _) in enumerate(W_IN_TILES):
                    a, n = W_IN.at[name]
                    if name in ("v", "o"):
                        sp.wait_ge(bank_full, 4 if name == "v" else 8)
                    sp.dma_start(wt(name).rearrange("p k n -> p (k n)"), d["w_in"][:, a:a + n]).then_inc(w_in[i], 16)

            @block.tensor
            def _(pe):
                seen = set()
                for n, (name, j, t, reader) in enumerate(jobs):
                    if n >= NB:
                        pe.wait_ge(act_free if jobs[n - NB][3] == "act" else dve_free,
                                   done_before(n - NB + 1, jobs[n - NB][3]))
                    i = [x for x, _ in W_IN_TILES].index(name)
                    if name not in seen:
                        pe.wait_ge(w_in[i], 16)
                        seen.add(name)
                    bank = ps[:, n % NB, :]
                    for k in range(KT):
                        if j is None:
                            mm = pe.matmul(bank, m.h[:, k, t * P:t * P + P], wt(name)[:, k, :], start=(k == 0), stop=False)
                        else:
                            cols = min(P, W_IN.at[name][1] // KT)
                            mm = pe.matmul(bank[0:cols, 0:t[1]], wt(name)[:, k, j * P:j * P + cols],
                                           m.h[:, k, t[0]:t[0] + t[1]], start=(k == 0), stop=(k == KT - 1))
                    if j is None:
                        mm = pe.matmul(bank, CONST.of(m.const, "ones")[0:1, :], ROWV.of(m.rowv, "b_" + name)[0:1, :],
                                       start=False, stop=True)
                    mm.then_inc(bank_full, 1)
                inv_c = CONST.of(m.const, "inv_c")
                pe.wait_ge(u_ready, 1)
                for j in range(4):
                    mm = pe.matmul(ps[:, CB, :], inv_c, acc[:, j, :], start=(j == 0), stop=(j == 3))
                mm.then_inc(mean_done, 1)
                for j in range(4):
                    pe.wait_ge(conv_sq, j + 1)
                    mm = pe.matmul(ps[:, VB, :], inv_c, gb[:, j, :], start=(j == 0), stop=(j == 3))
                mm.then_inc(var_done, 1)

            @block.scalar
            def _(act):
                for n, (name, j, t, reader) in enumerate(jobs):
                    if reader != "act":
                        continue
                    act.wait_ge(bank_full, n + 1)
                    bank = ps[:, n % NB, :]
                    if name == "gb":
                        act.activation(gb[:, j, :], bank, ACT.Sigmoid, bias=VEC.of(m.vec, "b_gb", j, 1)).then_inc(act_free, 1)
                    elif name == "o":
                        act.activation(m.so[:, t, :], bank, ACT.Sigmoid).then_inc(act_free, 1)
                    else:
                        act.activation(m.v[:, t, :], bank, ACT.Copy).then_inc(act_free, 1)
                for j in range(4):
                    act.wait_ge(centred, j + 1)
                    act.activation(gb[:, j, :], centre[:, j, :], ACT.Square).then_inc(conv_sq, 1)
                act.wait_ge(var_done, 1)
                act.activation(stat[:, 0, :], ps[:, VB, :], ACT.Sqrt, bias=CONST.of(m.const, "eps")).then_inc(std_done, 1)
                for j in range(4):
                    act.wait_ge(normed, j + 1)
                    act.activation(acc[:, j, :], acc[:, j, :], ACT.Silu, scale=VEC.of(m.vec, "ln_g", j, 1),
                                   bias=VEC.of(m.vec, "ln_b", j, 1))

            @block.vector
            def _(dve):
                own = Steps(dve_own)
                own(dve, dve.memset(u[:], 0.0))
                for n, (name, j, t, reader) in enumerate(jobs):
                    if reader != "dve":
                        continue
                    dve.wait_ge(bank_full, n + 1)
                    bank = ps[:, n % NB, :]
                    if name == "ga":
                        if j == 0:
                            dve.wait_ge(act_free, 4)
                        dve.scalar_tensor_tensor(
                            u[:, j, :, HALO:HALO + GRID], bank.rearrange("p (r t) -> p r t", t=GRID),
                            VEC.of(m.vec, "b_ga", j, 1), gb[:, j, :].rearrange("p (r t) -> p r t", t=GRID),
                            ALU.add, ALU.mult).then_inc(dve_free, 1)
                    elif name == "q":
                        dve.tensor_scalar(m.q[:, j, :], bank, VEC.of(m.vec, "b_q", j, 1), None, ALU.add).then_inc(dve_free, 1)
                    elif name == "k":
                        scale = QK ** -0.5
                        b = VEC.of(m.vec, "b_k", j, 1)
                        if t is x_:
                            dve.tensor_scalar(m.k[:, j, CTX:CTX + SEQ], bank, b, scale, ALU.add, ALU.mult).then_inc(dve_free, 1)
                        else:
                            dve.tensor_scalar(m.k[:, j, 0:CTX], bank[:, 0:CTX], b, scale, ALU.add, ALU.mult)
                            dve.tensor_scalar(m.k[:, j, CTX + SEQ:], bank[:, 0:CTX], b, scale, ALU.add, ALU.mult).then_inc(dve_free, 1)
                    else:
                        dve.tensor_scalar(m.gates[:, t[0]:t[0] + t[1]], bank[0:16, 0:t[1]],
                                          VEC.of(m.vec, "b_gates", 0, 1)[0:16], VEC.of(m.vec, "b_gates", 1, 1)[0:16],
                                          ALU.add, ALU.add).then_inc(dve_free, 1)
                dve.wait_ge(dve_free, sum(1 for j in jobs if j[3] == "dve"))
                for tap in range(CW):
                    for j in range(4):
                        src = u[:, j, :, tap:tap + GRID]
                        to = acc[:, j, :].rearrange("p (r t) -> p r t", t=GRID)
                        w_tap = VEC.of(m.vec, "conv_w", j * CW + tap, 1)
                        if tap == 0:
                            ins = dve.tensor_scalar(to, src, w_tap, VEC.of(m.vec, "conv_b", j, 1), ALU.mult, ALU.add)
                        else:
                            ins = dve.scalar_tensor_tensor(to, src, w_tap, to, ALU.mult, ALU.add)
                    own(dve, ins)
                dve.tensor_copy(m.scratch1[:, 0:1], acc[:, 0, 0:1]).then_inc(u_ready, 1)
                dve.wait_ge(mean_done, 1)
                for j in range(4):
                    dve.tensor_tensor(centre[:, j, :], acc[:, j, :], ps[:, CB, :], ALU.subtract).then_inc(centred, 1)
                dve.wait_ge(std_done, 1)
                own(dve, dve.reciprocal(stat[:, 1, :], stat[:, 0, :]))
                dve.wait_ge(centred, 4)
                for j in range(4):
                    dve.tensor_tensor(acc[:, j, :], centre[:, j, :], stat[:, 1, :], ALU.mult).then_inc(normed, 1)


def mlstm(m, d, mix):
    nc, ps = m.nc, m.ps
    M_LEAST = -60.0
    stack, sb, sem = m.open()
    L = CTX + SEQ + CTX
    with stack:
        sel = sb("sel", [16, 2, H_M, 2, P])
        lsig, tmp, zero = sb("lsig", [16, ALLT]), sb("lsig_tmp", [16, ALLT]), sb("zero", [16, SEQ])
        run = [sb(f"run{i}", [16, ALLT]) for i in range(2)]
        a_col = sb("a_col", [P, TT, 2, 16])
        r_row = sb("r_row", [P, 2, H_M, ALLT])
        t_sb = [sb(f"logits{i}", [P, ALLT]) for i in range(2)]
        p_sb = [sb(f"decay{i}", [P, ALLT]) for i in range(2)]
        s_sb = [sb(f"scores{i}", [P, ALLT]) for i in range(2)]
        st_sb = [sb(f"scores_t{i}", [P, ALLT]) for i in range(2)]
        cols = [sb(f"row_cols{i}", [P, 8, 2]) for i in range(2)]
        hout = sb("hout", [P, TT, D_ML])
        ss, rs = sb("ss", [P, TT * H_M]), sb("rs", [P, 2, TT * H_M])
        (sel_in, l_abs, l_exp, l_ln, own_s, run_done, rr_done, rr_copied, ac_done, ac_copied, qk_done, qk_free, t_done,
         p_done, s_done, tr_done, st_done, pv_done, h_done, thr_done, ss_done, rs_done, mixed, mt_done) = (
            sem(s) for s in ("sel_in", "l_abs", "l_exp", "l_ln", "own", "run_done", "rr_done", "rr_copied", "ac_done",
                             "ac_copied", "qk_done", "qk_free", "t_done", "p_done", "s_done", "tr_done", "st_done",
                             "pv_done", "h_done", "thr_done", "ss_done", "rs_done", "mixed", "mt_done"))
        units = [(h, i) for h in range(H_M) for i in range(TT)]
        subs = [(h, i, r) for h, i in units for r in range(2)]

        def keys(i, r):
            return (0, CTX + P * (i + 1)) if r == 0 else (CTX + P * i, SEQ - P * i + CTX)

        with nc.Block() as block:
            @block.sync
            def _(sp):
                sp.dma_start(sel[:].rearrange("p a b c n -> p (a b c n)"), d["sel"]).then_inc(sel_in, 16)

            @block.scalar
            def _(act):
                act.wait_ge(l_abs, 1)
                act.activation(tmp[:], tmp[:], ACT.Exp, scale=-1.0).then_inc(l_exp, 1)
                act.wait_ge(l_exp, 1)
                act.activation(tmp[:], tmp[:], ACT.Ln, bias=1.0).then_inc(l_ln, 1)
                for n in range(2 * H_M):
                    r, h = divmod(n, H_M)
                    act.wait_ge(rr_done, n + 1)
                    b = 2 * (n % 2)
                    act.activation(r_row[:, r, h, 0:SEQ], ps[:, b, :], ACT.Copy)
                    act.activation(r_row[:, r, h, SEQ:], ps[:, b + 1, 0:CTX], ACT.Copy).then_inc(rr_copied, 1)
                act.wait_ge(ac_done, 1)
                act.activation(a_col[:].rearrange("p i r g -> p (i r g)"), ps[:, 4, 0:TT * 32], ACT.Copy).then_inc(ac_copied, 1)

                def copy_t(n):
                    h, i, r = subs[n]
                    k0, w = keys(i, r)
                    act.wait_ge(tr_done, n + 1)
                    if n >= 2:
                        act.wait_ge(pv_done, n - 1)
                    act.activation(st_sb[n % 2][:, 0:min(w, SEQ)], ps[:, 4, 0:min(w, SEQ)], ACT.Copy)
                    if w > SEQ:
                        act.activation(st_sb[n % 2][:, SEQ:w], ps[:, 5, 0:w - SEQ], ACT.Copy)
                    act.activation(m.scratch2[:, 0:1], m.scratch2[:, 1:2], ACT.Copy).then_inc(st_done, 1)

                for n, (h, i, r) in enumerate(subs):
                    k0, w = keys(i, r)
                    act.wait_ge(t_done, n + 1)
                    c = cols[n % 2]
                    if n >= 2:
                        act.wait_ge(s_done, n - 1)
                        act.wait_ge(h_done, n - 1)
                    act.activation(p_sb[n % 2][:, 0:w], t_sb[n % 2][:, 0:w], ACT.Exp, bias=c[:, 2, 0:1]).then_inc(p_done, 1)
                    act.activation(c[:, 3, 0:1], c[:, 1, 0:1], ACT.Exp, scale=-1.0).then_inc(thr_done, 1)
                    if n >= 1:
                        copy_t(n - 1)
                copy_t(len(subs) - 1)
                act.wait_ge(ss_done, 1)
                act.activation(rs[:, 0, :], ss[:], ACT.Sqrt, scale=1.0 / DV, bias=CONST.of(m.const, "eps")).then_inc(rs_done, 1)
                for j in range(4):
                    act.wait_ge(mt_done, j + 1)
                    act.activation(mix[:, j, :], ps[:, j, :], ACT.Copy)

            @block.vector
            def _(dve):
                own = Steps(own_s)
                dve.memset(zero[:], 0.0)
                dve.memset(m.scratch2[:, 0:2], 0.0)
                own(dve, dve.tensor_scalar(lsig[:], m.gates[:], -1.0, None, ALU.mult))
                dve.tensor_tensor(tmp[:], lsig[:], m.gates[:], ALU.max).then_inc(l_abs, 1)
                dve.wait_ge(l_ln, 1)
                own(dve, dve.scalar_tensor_tensor(lsig[:], m.gates[:], 0.0, tmp[:], ALU.min, ALU.subtract))
                x, c = slice(0, SEQ), slice(SEQ, ALLT)
                own(dve, dve.tensor_tensor_scan(run[0][:, c], lsig[:, c], zero[:, 0:CTX], 0.0, ALU.add, ALU.add))
                own(dve, dve.tensor_tensor_scan(run[0][:, x], lsig[:, x], zero[:], run[0][:, ALLT - 1:ALLT], ALU.add, ALU.add))
                own(dve, dve.tensor_tensor_scan(tmp[:, x], lsig[:, x], zero[:], 0.0, ALU.add, ALU.add))
                own(dve, dve.tensor_tensor_scan(tmp[:, c], lsig[:, c], zero[:, 0:CTX], tmp[:, SEQ - 1:SEQ], ALU.add, ALU.add))
                dve.tensor_tensor(run[1][:], tmp[:], lsig[:], ALU.subtract).then_inc(run_done, 1)
                dve.wait_ge(rr_copied, 2 * H_M)
                dve.wait_ge(ac_copied, 1)

                def finish(n):
                    h, i, r = subs[n]
                    c = cols[n % 2]
                    dve.wait_ge(thr_done, n + 1)
                    own(dve, dve.tensor_scalar(c[:, 5, 0:1], c[:, 4, 0:1], -1.0, None, ALU.mult))
                    own(dve, dve.tensor_tensor(c[:, 5, 0:1], c[:, 5, 0:1], c[:, 4, 0:1], ALU.max))
                    own(dve, dve.tensor_tensor(c[:, 5, 0:1], c[:, 5, 0:1], c[:, 3, 0:1], ALU.max))
                    own(dve, dve.reciprocal(c[:, 6, 0:1], c[:, 5, 0:1]))
                    dve.wait_ge(pv_done, n + 1)
                    to, pv = hout[:, i, h * DV:(h + 1) * DV], ps[:, 6, 0:DV]
                    if r == 0:
                        ins = dve.tensor_scalar(to, pv, c[:, 6, 0:1], None, ALU.mult)
                    else:
                        ins = dve.scalar_tensor_tensor(to, pv, c[:, 6, 0:1], to, ALU.mult, ALU.add)
                    ins.then_inc(h_done, 1)
                    dve.wait_ge(h_done, n + 1)

                def scores(n):
                    h, i, r = subs[n]
                    k0, w = keys(i, r)
                    dve.wait_ge(p_done, n + 1)
                    dve.wait_ge(qk_done, n // 2 + 1)
                    if n >= 2:
                        dve.wait_ge(tr_done, n - 1)
                    b = 2 * ((n // 2) % 2)
                    qk = ps[:, b:b + 2, :].rearrange("p b n -> p (b n)")[:, k0:k0 + w]
                    dve.tensor_tensor_reduce(s_sb[n % 2][:, 0:w], p_sb[n % 2][:, 0:w], qk, 1.0, 0.0, ALU.mult, ALU.add,
                                             cols[n % 2][:, 4, 0:1]).then_inc(s_done, 1)
                    dve.wait_ge(s_done, n + 1)

                for n, (h, i, r) in enumerate(subs):
                    k0, w = keys(i, r)
                    c = cols[n % 2]
                    if n >= 2:
                        finish(n - 2)
                    row = r_row[:, r, h, :]
                    mask = CONST.of(m.const, "mask_fwd")[:, ALLT - w:] if r == 0 else CONST.of(m.const, "mask_bwd")[:, 0:w]
                    src = row[:, 0:w] if r == 0 else row[:, k0 - CTX:]
                    own(dve, dve.tensor_tensor_reduce(t_sb[n % 2][:, 0:w], src, mask, 1.0, NEG, ALU.add, ALU.max, c[:, 0, 0:1]))
                    gate = (4 + h) if r == 0 else (12 + h)
                    a = a_col[:, i, r, gate:gate + 1]
                    if r == 0:
                        own(dve, dve.tensor_scalar(c[:, 1, 0:1], c[:, 0, 0:1], a, M_LEAST, ALU.add, ALU.max))
                        dve.tensor_tensor(c[:, 2, 0:1], a, c[:, 1, 0:1], ALU.subtract).then_inc(t_done, 1)
                    else:
                        own(dve, dve.tensor_scalar(c[:, 1, 0:1], c[:, 0, 0:1], a, M_LEAST, ALU.subtract, ALU.max))
                        own(dve, dve.tensor_tensor(c[:, 7, 0:1], a, c[:, 1, 0:1], ALU.add))
                        dve.tensor_scalar(c[:, 2, 0:1], c[:, 7, 0:1], -1.0, None, ALU.mult).then_inc(t_done, 1)
                    if n >= 1:
                        scores(n - 1)
                last = len(subs) - 1
                scores(last)
                finish(last - 1)
                finish(last)
                for i in range(TT):
                    for h in range(H_M):
                        hh = hout[:, i, h * DV:(h + 1) * DV]
                        ins = dve.tensor_tensor_reduce(t_sb[0][:, 0:DV], hh, hh, 1.0, 0.0, ALU.mult, ALU.add,
                                                       ss[:, i * H_M + h:i * H_M + h + 1])
                        own(dve, ins)
                dve.tensor_copy(m.scratch1[:, 0:1], m.scratch1[:, 0:1]).then_inc(ss_done, 1)
                dve.wait_ge(rs_done, 1)
                own(dve, dve.reciprocal(rs[:, 1, :], rs[:, 0, :]))
                for i in range(TT):
                    for h in range(H_M):
                        hh = hout[:, i, h * DV:(h + 1) * DV]
                        ins = dve.scalar_tensor_tensor(hh, hh, rs[:, 1, i * H_M + h:i * H_M + h + 1],
                                                       ROWV.of(m.rowv, "norm_g", h * DV, DV), ALU.mult, ALU.mult)
                    own(dve, ins)
                    dve.tensor_tensor(hout[:, i, :], hout[:, i, :], m.so[:, i, :], ALU.mult).then_inc(mixed, 1)

            @block.tensor
            def _(pe):
                pe.wait_ge(sel_in, 16)
                pe.wait_ge(run_done, 1)
                for n in range(2 * H_M):
                    r, h = divmod(n, H_M)
                    if n >= 2:
                        pe.wait_ge(rr_copied, n - 1)
                    b = 2 * (n % 2)
                    order = [(SEQ, CTX, 0), (0, CTX, CTX), (CTX, CTX, SEQ)] if r == 0 else [(0, SEQ, 0), (SEQ, CTX, SEQ)]
                    for t, w, at in order:
                        to = ps[:, b + at // SEQ, at % SEQ:at % SEQ + w]
                        pe.matmul(to, sel[:, r, h, 0, :], m.gates[:, t:t + w], start=True, stop=False)
                        mm = pe.matmul(to, sel[:, r, h, 1, :], run[r][:, t:t + w], start=False, stop=True)
                    mm.then_inc(rr_done, 1)
                for i in range(TT):
                    for r in range(2):
                        at = (2 * i + r) * 16
                        mm = pe.transpose(ps[:, 4, at:at + 16], run[r][:, i * P:(i + 1) * P], CONST.of(m.const, "ident")[0:16, 0:16])
                mm.then_inc(ac_done, 1)
                pe.wait_ge(rr_copied, 2 * H_M)
                pe.wait_ge(ac_copied, 1)
                ident = CONST.of(m.const, "ident")

                def qk(u):
                    h, i = units[u]
                    if u >= 2:
                        pe.wait_ge(s_done, 2 * (u - 1))
                    rows = slice(QK * (h % 2), QK * (h % 2) + QK)
                    b = 2 * (u % 2)
                    for c in range(2):
                        mm = pe.matmul(ps[:, b + c, :], m.q[rows, h // 2, i * P:(i + 1) * P],
                                       m.k[rows, h // 2, c * SEQ:(c + 1) * SEQ], start=True, stop=True)
                    mm.then_inc(qk_done, 1)

                def turn(n):
                    h, i, r = subs[n]
                    k0, w = keys(i, r)
                    pe.wait_ge(s_done, n + 1)
                    if n >= 1:
                        pe.wait_ge(st_done, n)
                    for t in range(w // P):
                        mm = pe.transpose(ps[:, 4 + t // 4, (t % 4) * P:(t % 4 + 1) * P],
                                          s_sb[n % 2][:, t * P:(t + 1) * P], ident)
                    mm.then_inc(tr_done, 1)

                def pv(n):
                    h, i, r = subs[n]
                    k0, w = keys(i, r)
                    pe.wait_ge(st_done, n + 1)
                    if n >= 1:
                        pe.wait_ge(h_done, n)
                    for t in range(w // P):
                        tile = (k0 // P + t + 4) % 6
                        mm = pe.matmul(ps[:, 6, 0:DV], st_sb[n % 2][:, t * P:(t + 1) * P],
                                       m.v[:, tile, h * DV:(h + 1) * DV], start=(t == 0), stop=(t == w // P - 1))
                    mm.then_inc(pv_done, 1)

                qk(0)
                for n in range(len(subs)):
                    if n % 2 == 0 and n // 2 + 1 < len(units):
                        qk(n // 2 + 1)
                    turn(n)
                    pv(n)
                for i in range(TT):
                    pe.wait_ge(mixed, i + 1)
                for j in range(4):
                    for i in range(TT):
                        mm = pe.transpose(ps[:, j, i * P:(i + 1) * P], hout[:, i, j * P:(j + 1) * P], ident)
                    mm.then_inc(mt_done, 1)


def project_out(m, w_dram, src, bias=None, dst=None):
    nc, ps = m.nc, m.ps
    stack, sb, sem = m.open()
    with stack:
        w = sb("w_out", [P, KT, D])
        w_in, done, own_s = sem("w_in"), sem("done"), sem("own")
        with nc.Block() as block:
            @block.sync
            def _(sp):
                sp.dma_start(w[:].rearrange("p k n -> p (k n)"), w_dram).then_inc(w_in, 16)

            @block.tensor
            def _(pe):
                pe.wait_ge(w_in, 16)
                for j in range(KT):
                    for k in range(KT):
                        mm = pe.matmul(ps[:, j, :], w[:, k, j * P:(j + 1) * P], src[:, k, 0:SEQ], start=(k == 0), stop=(k == KT - 1))
                    mm.then_inc(done, 1)

            @block.vector
            def _(dve):
                for j in range(KT):
                    dve.wait_ge(done, j + 1)
                    if dst is None:
                        dve.tensor_tensor(m.x[:, j, 0:SEQ], ps[:, j, :], m.x[:, j, 0:SEQ], ALU.add)
                    else:
                        dve.tensor_scalar(dst[:, j, :], ps[:, j, :], VEC.of(m.vec, bias, j, 1), None, ALU.add)


def route(m, d, scratch, y):
    nc, ps = m.nc, m.ps
    stack, sb, sem = m.open()
    TE = TT * N_EXP
    with stack:
        wr, wgu, wdn = sb("w_router", [P, KT, N_EXP]), sb("ws_gu", [P, KT, 2 * D_EXP]), sb("ws_dn", [P, 2, D])
        rows = [sb(f"rows{i}", [P, D]) for i in range(2)]
        s, biased, rest = sb("s", [P, TT, N_EXP]), sb("biased", [P, TT, N_EXP]), sb("rest", [P, TT, N_EXP])
        mask, top, sums = sb("mask", [P, TT, N_EXP]), sb("top", [P, TT, 8]), sb("sums", [P, 2, TT])
        held, nblk = sb("held", [P, TT, N_EXP]), sb("nblk", [P, 2, N_EXP])
        ends, base, zero = sb("ends", [P, N_EXP]), sb("base", [P, N_EXP]), sb("zero", [P, N_EXP])
        owner, owner_i, pairs = sb("owner", [P, 3]), sb("owner_i", [P, 1], I32), sb("pairs", [P, 2])
        sg, hs = sb("shared_gate", [P, 2, SEQ]), sb("shared_h", [P, 2, SEQ])
        stored = [sem("stored0"), sem("stored1")]
        (w_in, logits, s_done, own_s, tr_done, tr_copied, mask_done, rank_done, owner_done, owner_out,
         gu_done, sg_done, hs_done, y_done) = (
            sem(n) for n in ("w_in", "logits", "s_done", "own", "tr_done", "tr_copied", "mask_done", "rank_done",
                             "owner_done", "owner_out", "gu_done", "sg_done", "hs_done", "y_done"))
        with nc.Block() as block:
            @block.sync
            def _(sp):
                for to, name in ((wr, "w_router"), (wgu, "ws_gu"), (wdn, "ws_dn")):
                    sp.dma_start(to[:].rearrange("p k n -> p (k n)"), d[name]).then_inc(w_in, 16)
                for i in range(TT):
                    sp.wait_ge(tr_copied, i + 1)
                    sp.dma_start(scratch["h_rows"][i * P:(i + 1) * P, :], rows[i % 2][:]).then_inc(stored[i % 2], 16)
                sp.wait_ge(owner_done, 1)
                sp.dma_start(scratch["block_expert"], owner_i[:]).then_inc(owner_out, 16)
                sp.wait_ge(owner_out, 16)
                sp.dma_start(m.owner_row[:], scratch["block_expert"].rearrange("p o -> o p")).then_inc(owner_out, 16)
                sp.wait_ge(owner_out, 32)
                for q in stored:
                    sp.wait_ge(q, 16 * (TT // 2))

            @block.tensor
            def _(pe):
                ident = CONST.of(m.const, "ident")
                pe.wait_ge(w_in, 48)
                for i in range(TT):
                    for k in range(KT):
                        mm = pe.matmul(ps[:, 0, i * N_EXP:(i + 1) * N_EXP], m.h[:, k, i * P:(i + 1) * P], wr[:, k, :],
                                       start=(k == 0), stop=(k == KT - 1))
                mm.then_inc(logits, 1)
                for i in range(TT):
                    if i >= 1:
                        pe.wait_ge(tr_copied, i)
                    for k in range(KT):
                        mm = pe.transpose(ps[:, 1 + k // 4, (k % 4) * P:(k % 4 + 1) * P], m.h[:, k, i * P:(i + 1) * P], ident)
                    mm.then_inc(tr_done, 1)
                for j in range(4):
                    for k in range(KT):
                        mm = pe.matmul(ps[:, 3 + j, :], wgu[:, k, j * P:(j + 1) * P], m.h[:, k, 0:SEQ],
                                       start=(k == 0), stop=(k == KT - 1))
                    mm.then_inc(gu_done, 1)
                pe.wait_ge(mask_done, 1)
                for i in range(TT):
                    to = ps[:, 0, i * N_EXP:(i + 1) * N_EXP]
                    pe.matmul(to, CONST.of(m.const, "before"), mask[:, i, :], start=True, stop=(i == 0))
                    for j in range(i):
                        pe.matmul(to, CONST.of(m.const, "ones"), mask[:, j, :], start=False, stop=(j == i - 1))
                for i in range(TT):
                    mm = pe.matmul(ps[:, 0, TE:TE + N_EXP], CONST.of(m.const, "ones"), mask[:, i, :],
                                   start=(i == 0), stop=(i == TT - 1))
                mm.then_inc(rank_done, 1)
                for j in range(KT):
                    if j == 0:
                        pe.wait_ge(hs_done, 2)
                        pe.wait_ge(tr_copied, TT)
                    if j >= 2:
                        pe.wait_ge(y_done, j - 1)
                    for k in range(2):
                        mm = pe.matmul(ps[:, 1 + j % 2, :], wdn[:, k, j * P:(j + 1) * P], hs[:, k, :], start=(k == 0), stop=(k == 1))
                    mm.then_inc(gu_done, 1)

            @block.scalar
            def _(act):
                act.wait_ge(logits, 1)
                act.activation(s[:].rearrange("p i e -> p (i e)"), ps[:, 0, 0:TE], ACT.Sigmoid).then_inc(s_done, 1)
                for i in range(TT):
                    act.wait_ge(tr_done, i + 1)
                    if i >= 2:
                        act.wait_ge(stored[i % 2], 16 * (i // 2))
                    act.activation(rows[i % 2][:, 0:512], ps[:, 1, :], ACT.Copy)
                    act.activation(rows[i % 2][:, 512:], ps[:, 2, :], ACT.Copy).then_inc(tr_copied, 1)
                for j in range(2):
                    act.wait_ge(gu_done, j + 1)
                    act.activation(sg[:, j, :], ps[:, 3 + j, :], ACT.Silu).then_inc(sg_done, 1)
                for j in range(KT):
                    act.wait_ge(gu_done, 5 + j)
                    act.activation(y[:, j, :], ps[:, 1 + j % 2, :], ACT.Copy).then_inc(y_done, 1)

            @block.vector
            def _(dve):
                own = Steps(own_s)
                own(dve, dve.memset(zero[:], 0.0))
                dve.wait_ge(s_done, 1)
                for i in range(TT):
                    ins = dve.tensor_tensor(biased[:, i, :], s[:, i, :], ROWV.of(m.rowv, "b_router"), ALU.add)
                own(dve, ins)
                for i in range(TT):
                    ins = dve.max(top[:, i, :], biased[:, i, :])
                own(dve, ins)
                for i in range(TT):
                    ins = dve.match_replace(rest[:, i, :], top[:, i, :], biased[:, i, :], NEG)
                own(dve, ins)
                ins = dve.tensor_tensor(mask[:], rest[:], biased[:], ALU.not_equal)
                ins.then_inc(mask_done, 1)
                dve.wait_ge(mask_done, 1)
                for i in range(TT):
                    ins = dve.tensor_tensor_reduce(biased[:, i, :], s[:, i, :], mask[:, i, :], 1.0, 0.0, ALU.mult, ALU.add,
                                                   sums[:, 0, i:i + 1])
                own(dve, ins)
                own(dve, dve.reciprocal(sums[:, 1, :], sums[:, 0, :]))
                token = CONST.of(m.const, "token")
                for i in range(TT):
                    dve.tensor_scalar(m.moved[:, i, :, 1], biased[:, i, :], sums[:, 1, i:i + 1], ROUTE_SCALE, ALU.mult, ALU.mult)
                    dve.tensor_scalar(m.moved[:, i, :, 0], mask[:, i, :], 0.0, token[:, i:i + 1], ALU.mult, ALU.add)
                    ins = dve.tensor_tensor_scan(held[:, i, :], mask[:, i, :], zero[:], 0.0, ALU.add, ALU.add)
                own(dve, ins)
                for i in range(TT):
                    ins = dve.tensor_scalar(rest[:, i, :], held[:, i, :], float(SEQ), token[:, i:i + 1], ALU.mult, ALU.add)
                own(dve, ins)
                for i in range(TT):
                    dve.tensor_scalar(m.moved[:, i, :, 2], rest[:, i, :], float(1 - SEQ), None, ALU.add)
                dve.wait_ge(rank_done, 1)
                count = ps[:, 0, TE:TE + N_EXP]
                own(dve, dve.tensor_scalar(nblk[:, 0, :], count, 0.0, None, ALU.is_gt))
                for j in range(1, TT):
                    own(dve, dve.scalar_tensor_tensor(nblk[:, j % 2, :], count, float(P * j), nblk[:, (j + 1) % 2, :],
                                                      ALU.is_gt, ALU.add))
                n_of = nblk[:, (TT - 1) % 2, :]
                own(dve, dve.tensor_tensor_scan(ends[:], n_of, zero[:], 0.0, ALU.add, ALU.add))
                own(dve, dve.tensor_tensor(base[:], ends[:], n_of, ALU.subtract))
                own(dve, dve.tensor_scalar(base[:], base[:], float(P), 1.0, ALU.mult, ALU.add))
                for i in range(TT):
                    ins = dve.tensor_tensor(rest[:, i, :], ps[:, 0, i * N_EXP:(i + 1) * N_EXP], base[:], ALU.add)
                own(dve, ins)
                own(dve, dve.tensor_tensor(held[:], rest[:], mask[:], ALU.mult))
                dve.tensor_scalar(m.dest[:], held[:], 1.0, None, ALU.subtract)
                own(dve, dve.tensor_scalar(nblk[:, 0, :], ends[:], CONST.of(m.const, "part"), None, ALU.is_le))
                own(dve, dve.reduce_sum(owner[:, 0:1], nblk[:, 0, :], mybir.AxisListType.X))
                own(dve, dve.tensor_scalar(owner[:, 1:2], owner[:, 0:1], float(N_EXP - 1), None, ALU.min))
                dve.tensor_copy(owner_i[:], owner[:, 1:2]).then_inc(owner_done, 1)
                own(dve, dve.tensor_scalar(nblk[:, 0, :], CONST.of(m.const, "slot", 0, N_EXP), 2.0, ends[:, N_EXP - 1:N_EXP],
                                           ALU.mult, ALU.is_lt))
                own(dve, dve.reduce_sum(pairs[:, 0:1], nblk[:, 0, :], mybir.AxisListType.X))
                dve.tensor_copy(m.pairs_i[:], pairs[:, 0:1])
                for j in range(2):
                    dve.wait_ge(sg_done, j + 1)
                    dve.wait_ge(gu_done, 3 + j)
                    dve.tensor_tensor(hs[:, j, :], sg[:, j, :], ps[:, 5 + j, :], ALU.mult).then_inc(hs_done, 1)


def experts(m, d, scratch):
    nc, ps = m.nc, m.ps
    stack, sb, sem = m.open()
    GU, BI, BT, BG, BU, BA, BY = KT * 2 * D_EXP, 0, 1, 3, 4, 5, 6
    with stack:
        gu = [sb(f"w_gu{s}", [P, KT, 2 * D_EXP]) for s in range(2)]
        dn = [sb(f"w_dn{s}", [P, 2, D]) for s in range(2)]
        pick, cols = sb("pick", [P, TT, P]), sb("cols", [P, TT, 3])
        raw = [sb(f"raw{s}", [P, 3]) for s in range(2)]
        token_i, target, target_i = sb("token_i", [P, 1], I32), sb("target", [P, 2]), sb("target_i", [P, 1], I32)
        xg, xt = sb("x_rows", [P, D]), sb("x_t", [P, KT, P])
        sg, a, at = sb("silu_gate", [P, D_EXP]), sb("act", [P, D_EXP]), sb("act_t", [P, 2, P])
        yb, spare = sb("y_block", [P, D]), sb("spare", [P, 2])
        gu_in, dn_in = [sem("gu_in0"), sem("gu_in1")], [sem("dn_in0"), sem("dn_in1")]
        (picked, found, listed, gathered, xt_turned, xt_done, gate_done, up_done, sg_done,
         a_done, a_turned, at_done, y_made, y_out, scattered, target_done, own_s, issued) = (
            sem(n) for n in ("picked", "found", "listed", "gathered", "xt_turned", "xt_done",
                             "gate_done", "up_done", "sg_done", "a_done", "a_turned", "at_done", "y_made", "y_out",
                             "scattered", "target_done", "own", "issued"))
        least, last = SEQ * TOP_K // P // 2, (MAX_BLOCKS + 1) // 2

        with nc.Block() as block:
            @block.sync
            def _(sp):
                pairs = sp.value_load(m.pairs_i[0:1, 0:1], min_val=least, max_val=last)

                def load(n, s, used):
                    e = sp.value_load(m.owner_row[0:1, bass.ds(n, 1)], min_val=0, max_val=N_EXP - 1)
                    if used is not None:
                        sp.wait_ge(up_done, used)
                    sp.dma_start(gu[s][:].rearrange("p k n -> p (k n)"), d["w_gu"][e]).then_inc(gu_in[s], 16)
                    if used is not None:
                        sp.wait_ge(y_made, 2 * used)
                    sp.dma_start(dn[s][:].rearrange("p k n -> p (k n)"), d["w_dn"][e]).then_inc(dn_in[s], 16)

                load(0, 0, None)
                load(1, 1, None)
                with sp.Fori(1, pairs) as g:
                    for s in range(2):
                        load(2 * g + s, s, 2 * g + s - 1)

            @block.tensor
            def _(pe):
                ident = CONST.of(m.const, "ident")
                pairs = pe.value_load(m.pairs_i[0:1, 0:1], min_val=least, max_val=last)

                def find(n):
                    pe.wait_ge(picked, n + 1)
                    for i in range(TT):
                        mm = pe.matmul(ps[:, BI, 0:3], pick[:, i, :], cols[:, i, :], start=(i == 0), stop=(i == TT - 1))
                    mm.then_inc(found, 1)

                def turn(half):
                    for k in range(4):
                        mm = pe.transpose(ps[:, BT + half, k * P:(k + 1) * P], xg[:, (4 * half + k) * P:(4 * half + k + 1) * P], ident)
                    mm.then_inc(xt_turned, 1)

                find(0)
                pe.wait_ge(gathered, 16)
                turn(0)
                turn(1)
                with pe.Fori(0, pairs) as g:
                    for s in range(2):
                        b = 2 * g + s
                        find(b + 1)
                        pe.wait_ge(xt_done, 2 * b + 2)
                        pe.wait_ge(gu_in[s], 16 * g + 16)
                        pe.wait_ge(sg_done, b + 1)
                        for k in range(KT):
                            mm = pe.matmul(ps[:, BG, 0:D_EXP], xt[:, k, :], gu[s][:, k, 0:D_EXP], start=(k == 0), stop=(k == KT - 1))
                        mm.then_inc(gate_done, 1)
                        pe.wait_ge(a_done, b + 1)
                        for k in range(KT):
                            mm = pe.matmul(ps[:, BU, 0:D_EXP], xt[:, k, :], gu[s][:, k, D_EXP:], start=(k == 0), stop=(k == KT - 1))
                        mm.then_inc(up_done, 1)
                        pe.wait_ge(gathered, 16 * b + 32)
                        turn(0)
                        pe.wait_ge(a_done, b + 2)
                        for j in range(2):
                            mm = pe.transpose(ps[:, BA, j * P:(j + 1) * P], a[:, j * P:(j + 1) * P], ident)
                        mm.then_inc(a_turned, 1)
                        turn(1)
                        pe.wait_ge(at_done, b + 1)
                        pe.wait_ge(dn_in[s], 16 * g + 16)
                        for n in range(2):
                            pe.wait_ge(y_out, 2 * b + n + 1)
                            for j in range(2):
                                mm = pe.matmul(ps[:, BY + n, :], at[:, j, :], dn[s][:, j, n * 512:(n + 1) * 512],
                                               start=(j == 0), stop=(j == 1))
                            mm.then_inc(y_made, 1)

            @block.scalar
            def _(act):
                pairs = act.value_load(m.pairs_i[0:1, 0:1], min_val=least, max_val=last)
                act.sem_inc(sg_done, 1)
                act.sem_inc(y_out, 2)

                def copy_x(n):
                    for half in range(2):
                        act.wait_ge(xt_turned, n + half + 1)
                        act.activation(xt[:, 4 * half:4 * half + 4, :].rearrange("p k t -> p (k t)"), ps[:, BT + half, :],
                                       ACT.Copy).then_inc(xt_done, 1)

                copy_x(0)
                with act.Fori(0, pairs) as g:
                    for s in range(2):
                        b = 2 * g + s
                        act.wait_ge(a_done, b + 1)
                        act.wait_ge(gate_done, b + 1)
                        act.activation(sg[:], ps[:, BG, 0:D_EXP], ACT.Silu).then_inc(sg_done, 1)
                        act.wait_ge(up_done, b + 1)
                        act.wait_ge(xt_turned, 2 * b + 3)
                        act.activation(xt[:, 0:4, :].rearrange("p k t -> p (k t)"), ps[:, BT, :], ACT.Copy).then_inc(xt_done, 1)
                        act.wait_ge(a_turned, b + 1)
                        act.activation(at[:].rearrange("p j t -> p (j t)"), ps[:, BA, 0:2 * P], ACT.Copy).then_inc(at_done, 1)
                        act.wait_ge(xt_turned, 2 * b + 4)
                        act.activation(xt[:, 4:8, :].rearrange("p k t -> p (k t)"), ps[:, BT + 1, :], ACT.Copy).then_inc(xt_done, 1)
                        for n in range(2):
                            act.wait_ge(scattered, 16 * b + 16)
                            act.wait_ge(y_made, 2 * b + n + 1)
                            act.activation(yb[:, n * 512:(n + 1) * 512], ps[:, BY + n, :], ACT.Copy).then_inc(y_out, 1)

            @block.vector
            def _(dve):
                pairs = dve.value_load(m.pairs_i[0:1, 0:1], min_val=least, max_val=last)
                dve.sem_inc(a_done, 1)
                slot, neg_block = CONST.of(m.const, "slot"), CONST.of(m.const, "neg_block")

                def choose(n):
                    e = dve.value_load(m.owner_row[0:1, bass.ds(n, 1)], min_val=0, max_val=N_EXP - 1)
                    for i in range(TT):
                        dve.tensor_scalar(pick[:, i, :], slot, m.dest[:, i, bass.ds(e, 1)], neg_block[:, bass.ds(n, 1)],
                                          ALU.subtract, ALU.is_equal)
                    dve.tensor_copy(cols[:], m.moved[:, :, bass.ds(e, 1), :].rearrange("p i o c -> p i (o c)")).then_inc(picked, 1)

                def read_tokens(n, s):
                    dve.wait_ge(found, n + 1)
                    dve.tensor_copy(token_i[:], ps[:, BI, 0:1])
                    dve.tensor_copy(raw[s][:], ps[:, BI, 0:3]).then_inc(listed, 1)

                choose(0)
                read_tokens(0, 0)
                choose(1)
                with dve.Fori(0, pairs) as g:
                    for s in range(2):
                        b = 2 * g + s
                        dve.wait_ge(a_done, b + 1)
                        dve.wait_ge(gathered, 16 * b + 16)
                        read_tokens(b + 1, 1 - s)
                        choose(b + 2)
                        dve.wait_ge(up_done, b + 1)
                        dve.wait_ge(sg_done, b + 2)
                        dve.wait_ge(listed, b + 1)
                        dve.scalar_tensor_tensor(a[:], ps[:, BU, 0:D_EXP], raw[s][:, 1:2], sg[:], ALU.mult, ALU.mult).then_inc(a_done, 1)
                        dve.tensor_scalar(target[:, 0:1], raw[s][:, 2:3], 0.0, 1.0e6, ALU.is_equal, ALU.mult).then_inc(own_s, 1)
                        dve.wait_ge(own_s, 2 * b + 1)
                        dve.tensor_tensor(target[:, 1:2], target[:, 0:1], raw[s][:, 2:3], ALU.add).then_inc(own_s, 1)
                        dve.wait_ge(own_s, 2 * b + 2)
                        dve.wait_ge(scattered, 16 * b + 16)
                        dve.tensor_scalar(target_i[:], target[:, 1:2], 1.0, None, ALU.subtract).then_inc(target_done, 1)
                        dve.wait_ge(target_done, b + 1)

            @block.gpsimd
            def _(pool):
                pairs = pool.value_load(m.pairs_i[0:1, 0:1], min_val=least, max_val=last)

                def gather():
                    pool.indirect_dma_start(xg[:], None, scratch["h_rows"], bass.IndirectOffsetOnAxis(ap=token_i[:, 0:1], axis=0),
                                            bounds_check=SEQ - 1, oob_is_err=False).then_inc(gathered, 16)

                pool.dma_start(spare[:], d["const"][:, 0:2]).then_inc(scattered, 16)
                pool.wait_ge(listed, 1)
                gather()
                with pool.Fori(0, pairs) as g:
                    for s in range(2):
                        b = 2 * g + s
                        pool.wait_ge(listed, b + 2)
                        pool.wait_ge(xt_turned, 2 * b + 2)
                        pool.sem_inc(issued, 1)
                        gather()
                        pool.wait_ge(target_done, b + 1)
                        pool.wait_ge(y_out, 2 * b + 4)
                        pool.sem_inc(issued, 1)
                        pool.indirect_dma_start(scratch["y_rows"], bass.IndirectOffsetOnAxis(ap=target_i[:, 0:1], axis=0), yb[:], None,
                                                bounds_check=TOP_K * SEQ - 1, oob_is_err=False).then_inc(scattered, 16)
                pool.wait_ge(gathered, 32 * pairs + 16)
                pool.sem_inc(issued, 1)
                pool.wait_ge(scattered, 32 * pairs + 16)
                pool.sem_inc(issued, 1)


def combine(m, scratch, y):
    nc, ps = m.nc, m.ps
    stack, sb, sem = m.open()
    with stack:
        rows = [sb(f"expert_rows{i}", [P, TOP_K, D]) for i in range(2)]
        rows_in = [sem("rows_in0"), sem("rows_in1")]
        turned, added = sem("turned"), sem("added")
        src = scratch["y_rows"].rearrange("(c i p) n -> i p c n", c=TOP_K, p=P)
        with nc.Block() as block:
            @block.sync
            def _(sp):
                for i in range(TT):
                    if i >= 2:
                        sp.wait_ge(turned, 2 * (i - 1))
                    sp.dma_start(rows[i % 2][:], src[i]).then_inc(rows_in[i % 2], 16)

            @block.tensor
            def _(pe):
                for i in range(TT):
                    pe.wait_ge(rows_in[i % 2], 16 * (i // 2) + 16)
                    for half in range(2):
                        n = 2 * i + half
                        if n >= 4:
                            pe.wait_ge(added, n - 3)
                        for k in range(4):
                            at = (4 * half + k) * P
                            for c in range(TOP_K):
                                mm = pe.matmul(ps[:, n % 4, k * P:(k + 1) * P], rows[i % 2][:, c, at:at + P],
                                               CONST.of(m.const, "ident"), start=(c == 0), stop=(c == TOP_K - 1), is_transpose=True)
                        mm.then_inc(turned, 1)

            @block.vector
            def _(dve):
                for i in range(TT):
                    for half in range(2):
                        n = 2 * i + half
                        to = y[:, 4 * half:4 * half + 4, i * P:(i + 1) * P]
                        dve.wait_ge(turned, n + 1)
                        dve.tensor_tensor(to, ps[:, n % 4, :].rearrange("p (k t) -> p k t", k=4), to, ALU.add).then_inc(added, 1)


def attention(m, d, w_name, o, diff):
    nc, ps = m.nc, m.ps
    stack, sb, sem = m.open()
    BT, BO, BP = 4, 6, 7
    U = 1 if diff else 2
    with stack:
        w = [sb(f"w_qkv{s}", [P, 3, KT, P]) for s in range(2)]
        rope, amask = sb("rope", [P, 2, SEQ]), sb("amask", [P, 4, SEQ])
        q, k = [sb(f"q{s}", [P, SEQ]) for s in range(2)], [sb(f"k{s}", [P, SEQ]) for s in range(2)]
        v = [sb(f"v{s}", [P, TT, P]) for s in range(2)]
        mask_now = sb("mask_now", [P, SEQ])
        straight, crossed = sb("straight", [P, SEQ]), sb("crossed", [P, SEQ])
        sm = [sb(f"scores{u}", [P, TT, SEQ]) for u in range(2)]
        pt = sb("scores_t", [P, TT, SEQ])
        low = [sb(f"least{u}", [P, TT]) for u in range(2)]
        den = [sb(f"den{u}", [P, 3, TT]) for u in range(2)]
        w_in, tables_in = [sem("w_in0"), sem("w_in1")], sem("tables_in")
        (q_made, k_made, v_made, q_ready, k_ready, v_ready, s_made, masked, e_done, p_ready, turned, pt_done, o_made,
         o_copied, own_s, own_p, own_rope, seen, mask_set) = (
            sem(n) for n in ("q_made", "k_made", "v_made", "q_ready", "k_ready", "v_ready", "s_made", "masked", "e_done",
                             "p_ready", "turned", "pt_done", "o_made", "o_copied", "own", "own_p", "own_rope", "seen", "mask_set"))

        def weights(s):
            return w[s][:].rearrange("p c k n -> p (c k n)")

        def steps(eng, emit):
            with eng.Fori(0, 3) as g:
                for s in range(2):
                    emit(2 * g + s, s, g, True)
            for s in range(2):
                emit(6 + s, s, 3, s == 0)

        def width(i):
            return P * (i + 1)

        with nc.Block() as block:
            @block.sync
            def _(sp):
                for s in range(2):
                    sp.dma_start(weights(s), d[w_name][s]).then_inc(w_in[s], 16)
                sp.dma_start(rope[:].rearrange("p a t -> p (a t)"), d["rope"]).then_inc(tables_in, 16)
                sp.dma_start(amask[:].rearrange("p a t -> p (a t)"), d["amask"]).then_inc(tables_in, 16)
                with sp.Fori(1, 4) as g:
                    for s in range(2):
                        sp.wait_ge(v_made, 2 * g - 1 + s)
                        sp.dma_start(weights(s), d[w_name][2 * g + s]).then_inc(w_in[s], 16)

            @block.tensor
            def _(pe):
                ident = CONST.of(m.const, "ident")

                def project(j, s, part, first=False):
                    if part == 0:
                        pe.wait_ge(w_in[s], 16 * (j // 2) + 16 if isinstance(j, int) else 8 * (j - s) + 16)
                        if not first:
                            pe.wait_ge(v_ready, j)
                    else:
                        pe.wait_ge(q_ready if part == 1 else k_ready, j + 1)
                    if part < 2:
                        for kk in range(KT):
                            mm = pe.matmul(ps[:, BP, :], w[s][:, part, kk, :], m.h[:, kk, :], start=(kk == 0), stop=(kk == KT - 1))
                    else:
                        for i in range(TT):
                            for kk in range(KT):
                                mm = pe.matmul(ps[:, BP, i * P:(i + 1) * P], m.h[:, kk, i * P:(i + 1) * P], w[s][:, 2, kk, :],
                                               start=(kk == 0), stop=(kk == KT - 1))
                    mm.then_inc((q_made, k_made, v_made)[part], 1)

                def scores(j, s, u):
                    if u == 0:
                        pe.wait_ge(k_ready, j + 1)
                    pe.wait_ge(masked, 8 * j + 4 * u + 4)
                    rows = slice(HD * u, HD * u + HD)
                    for i in range(TT):
                        mm = pe.matmul(ps[:, i, 0:width(i)], q[s][rows, i * P:(i + 1) * P], k[s][rows, 0:width(i)],
                                       start=True, stop=True)
                    mm.then_inc(s_made, 1)

                def turn(n, of):
                    pe.wait_ge(p_ready, n + 1)
                    for t in range(TT):
                        pe.wait_ge(pt_done, 4 * n + t + 1)
                        for i in range(t, TT):
                            mm = pe.transpose(ps[:, BT + t % 2, (i - t) * P:(i - t + 1) * P], sm[of][:, i, t * P:(t + 1) * P], ident)
                        mm.then_inc(turned, 1)

                def product(j, n, s, u):
                    rows = slice(0, P) if diff else slice(HD * u, HD * u + HD)
                    if u == 0:
                        pe.wait_ge(o_copied, j + 1)
                        pe.wait_ge(v_ready, j + 1)
                    for t in range(TT):
                        pe.wait_ge(pt_done, 4 * n + t + 3)
                        mm = pe.matmul(ps[rows, BO, t * P:], v[s][:, t, rows], pt[:, t, 0:SEQ - t * P], start=(t == 0), stop=(t == TT - 1))
                    mm.then_inc(o_made, 1)

                def step(j, s, g, more):
                    scores(j, s, 0)
                    if more:
                        project(j + 1, 1 - s, 0)
                    scores(j, s, 1)
                    if not diff:
                        turn(2 * j, 0)
                    if more:
                        project(j + 1, 1 - s, 1)
                    if not diff:
                        product(j, 2 * j, s, 0)
                        turn(2 * j + 1, 1)
                    else:
                        turn(j, 0)
                    if more:
                        project(j + 1, 1 - s, 2)
                    product(j, 2 * j + 1 if not diff else j, s, 1 if not diff else 0)

                pe.sem_inc(turned, 8)
                pe.sem_inc(o_made, 1)
                for part in range(3):
                    project(0, 0, part, True)
                steps(pe, step)

            @block.scalar
            def _(act):
                act.sem_inc(pt_done, 2)

                def exps(j, u):
                    for i in range(TT):
                        act.wait_ge(masked, 8 * j + 4 * u + i + 5)
                        act.activation(sm[u][:, i, 0:width(i)], sm[u][:, i, 0:width(i)], ACT.Exp, scale=-1.0,
                                       bias=low[u][:, i:i + 1], accum_out=den[u][:, 0, i:i + 1]).then_inc(e_done, 1)

                def copy_t(n):
                    act.wait_ge(o_made, n + 1)
                    for t in range(TT):
                        act.wait_ge(turned, 4 * n + t + 9)
                        act.activation(pt[:, t, 0:SEQ - t * P], ps[:, BT + t % 2, 0:SEQ - t * P], ACT.Copy).then_inc(pt_done, 1)

                def copy_v(j, s):
                    act.wait_ge(v_made, j + 1)
                    act.activation(v[s][:].rearrange("p i n -> p (i n)"), ps[:, BP, :], ACT.Copy).then_inc(v_ready, 1)

                def step(j, s, g, more):
                    exps(j, 0)
                    if not diff:
                        copy_t(2 * j)
                    exps(j, 1)
                    copy_t(j if diff else 2 * j + 1)
                    if more:
                        copy_v(j + 1, 1 - s)

                copy_v(0, 0)
                steps(act, step)

            @block.vector
            def _(dve):
                dve.sem_inc(masked, 4)
                dve.sem_inc(o_copied, 1)

                def rotate(j, s, part):
                    dve.wait_ge((q_made, k_made)[part], j + 1)
                    src, to, ready = ps[:, BP, :], (q, k)[part][s], (q_ready, k_ready)[part]
                    dve.tensor_tensor(straight[:], src, rope[:, 0, :], ALU.mult)
                    for a in range(4):
                        b = a ^ 1
                        ins = dve.tensor_tensor(crossed[32 * b:32 * b + 32, :], src[32 * a:32 * a + 32, :],
                                                rope[32 * a:32 * a + 32, 1, :], ALU.mult)
                    ins.then_inc(own_rope, 1)
                    dve.wait_ge(own_rope, 2 * j + part + 1)
                    dve.tensor_tensor(to[:], straight[:], crossed[:], ALU.add).then_inc(ready, 1)
                    dve.wait_ge(ready, j + 1)

                def mask(j, g, u):
                    if diff:
                        dve.wait_ge(*((turned, 4 * j + 8) if u == 0 else (own_p, j + 1)))
                    else:
                        dve.wait_ge(turned, 8 * j + 4 * u + 4)
                    dve.wait_ge(s_made, 2 * j + u + 1)
                    dve.sem_inc(seen, 1)
                    for i in range(TT):
                        dve.tensor_tensor_reduce(sm[u][:, i, 0:width(i)], ps[:, i, 0:width(i)], mask_now[:, SEQ - width(i):],
                                                 -HD ** -0.5, 3.0e38, ALU.add, ALU.min, low[u][:, i:i + 1]).then_inc(masked, 1)

                def normalise(j, u):
                    dve.wait_ge(e_done, 8 * j + 4 * u + 4)
                    dve.reciprocal(den[u][:, 1, :], den[u][:, 0, :]).then_inc(own_s, 1)
                    n = (3 if diff else 2) * j + u + 1
                    dve.wait_ge(own_s, n)
                    if diff and u == 1:
                        dve.tensor_scalar(den[1][:, 2, :], den[1][:, 1, :], m.neg_lambda[:, 0:1], None, ALU.mult).then_inc(own_s, 1)
                        dve.wait_ge(own_s, n + 1)
                    for i in range(TT):
                        p0 = sm[0][:, i, 0:width(i)]
                        if diff and u == 1:
                            ins = dve.scalar_tensor_tensor(p0, sm[1][:, i, 0:width(i)], den[1][:, 2, i:i + 1], p0, ALU.mult, ALU.add)
                        else:
                            pu = sm[u][:, i, 0:width(i)]
                            ins = dve.tensor_scalar(pu, pu, den[u][:, 1, i:i + 1], None, ALU.mult)
                    if not diff or u == 1:
                        ins.then_inc(p_ready, 1)
                    else:
                        ins.then_inc(own_p, 1)
                        dve.wait_ge(own_p, j + 1)

                def step(j, s, g, more):
                    if s == 0 and not diff:
                        dve.wait_ge(masked, 8 * j + 4)
                        dve.tensor_copy(mask_now[:], amask[:, bass.ds(g, 1), :].rearrange("p a t -> p (a t)")).then_inc(mask_set, 1)
                        dve.wait_ge(mask_set, g + 1)
                    mask(j, g, 0)
                    normalise(j, 0)
                    if more:
                        rotate(j + 1, 1 - s, 0)
                    mask(j, g, 1)
                    normalise(j, 1)
                    if more:
                        rotate(j + 1, 1 - s, 1)
                    dve.wait_ge(o_made, U * (j + 1) + 1)
                    dve.tensor_copy(o[:, bass.ds(j, 1), :].rearrange("p a t -> p (a t)"), ps[:, BO, :]).then_inc(o_copied, 1)

                dve.wait_ge(tables_in, 32)
                if diff:
                    dve.tensor_copy(mask_now[:], amask[:, 0, :]).then_inc(mask_set, 1)
                    dve.wait_ge(mask_set, 1)
                rotate(0, 0, 0)
                rotate(0, 0, 1)
                steps(dve, step)


def lambda_value(m):
    nc, ps = m.nc, m.ps
    stack, sb, sem = m.open()
    with stack:
        prod, e = sb("prod", [P, 2]), sb("e", [P, 2])
        prod_done, dot_done, e_done, own_s = sem("prod_done"), sem("dot_done"), sem("e_done"), sem("own")
        with nc.Block() as block:
            @block.vector
            def _(dve):
                own = Steps(own_s)
                vec = VEC.of(m.vec, "lambda")
                dve.tensor_tensor(prod[:], vec[:, 0::2], vec[:, 1::2], ALU.mult).then_inc(prod_done, 1)
                dve.wait_ge(e_done, 1)
                own(dve, dve.tensor_tensor(prod[:, 0:1], e[:, 1:2], e[:, 0:1], ALU.subtract))
                dve.tensor_scalar(m.neg_lambda[:], prod[:, 0:1], LAMBDA_INIT, None, ALU.subtract)

            @block.tensor
            def _(pe):
                pe.wait_ge(prod_done, 1)
                pe.matmul(ps[:, 0, 0:2], CONST.of(m.const, "ones"), prod[:], start=True, stop=True).then_inc(dot_done, 1)

            @block.scalar
            def _(act):
                act.wait_ge(dot_done, 1)
                act.activation(e[:], ps[:, 0, 0:2], ACT.Exp).then_inc(e_done, 1)


def head_norm(m, o):
    nc, ps = m.nc, m.ps
    stack, sb, sem = m.open()
    with stack:
        sq = [sb(f"sq{i}", [P, SEQ]) for i in range(2)]
        std = [sb(f"std{i}", [P, SEQ]) for i in range(2)]
        g = sb("g", [P, 1])
        sq_done, ms_done, std_done, rstd_done, out_done = (
            sem(n) for n in ("sq_done", "ms_done", "std_done", "rstd_done", "out_done"))
        with nc.Block() as block:
            @block.scalar
            def _(act):
                for j in range(N_PAIR + 1):
                    if j < N_PAIR:
                        if j >= 2:
                            act.wait_ge(ms_done, j - 1)
                        act.activation(sq[j % 2][:], o[:, j, :], ACT.Square).then_inc(sq_done, 1)
                    if j >= 1:
                        i = j - 1
                        act.wait_ge(ms_done, i + 1)
                        if i >= 2:
                            act.wait_ge(out_done, i - 1)
                        act.activation(std[i % 2][:], ps[:, i % 4, :], ACT.Sqrt, bias=CONST.of(m.const, "diff_eps")).then_inc(std_done, 1)

            @block.tensor
            def _(pe):
                for j in range(N_PAIR):
                    pe.wait_ge(sq_done, j + 1)
                    if j >= 4:
                        pe.wait_ge(std_done, j - 3)
                    pe.matmul(ps[:, j % 4, :], CONST.of(m.const, "inv_v"), sq[j % 2][:], start=True, stop=True).then_inc(ms_done, 1)

            @block.vector
            def _(dve):
                dve.tensor_scalar(g[:], VEC.of(m.vec, "subln"), 1.0 - LAMBDA_INIT, None, ALU.mult).then_inc(rstd_done, 1)
                for j in range(N_PAIR):
                    dve.wait_ge(std_done, j + 1)
                    dve.reciprocal(std[j % 2][:], std[j % 2][:]).then_inc(rstd_done, 1)
                    dve.wait_ge(rstd_done, j + 2)
                    dve.scalar_tensor_tensor(o[:, j, :], o[:, j, :], g[:, 0:1], std[j % 2][:], ALU.mult, ALU.mult).then_inc(out_done, 1)


def conv_ffn(m, d, layer):
    nc, ps = m.nc, m.ps
    stack, sb, sem = m.open()
    base = VEC.at["ffn_conv"][0] + layer * FT * 8
    PARTS = [(0, 12), (12, FT)]
    W = 2 * KT * P
    with stack:
        raw = [sb(f"raw{s}", [P, W]) for s in range(2)]
        w = [Split(sb, f"w{s}", [P, W]) for s in range(2)]
        hid = Split(sb, "hidden", [P, 12, SEQ])
        y = [sb(f"conv{s}", [P, 2, SEQ]) for s in range(2)]
        gate = [sb(f"gate{s}", [P, SEQ]) for s in range(2)]
        raw_in = [sem("raw_in0"), sem("raw_in1")]
        (high_done, low_done, used, up_made, tap0, tap1, conv_done, gate_done, gate_free, prod_done, hid_high, hid_low,
         down_made, added) = (
            sem(n) for n in ("high_done", "low_done", "used", "up_made", "tap0", "tap1", "conv_done", "gate_done", "gate_free",
                             "prod_done", "hid_high", "hid_low", "down_made", "added"))
        n0 = [0, PARTS[0][1] + KT]
        JOBS = n0[1] + PARTS[1][1] - PARTS[1][0] + KT

        def tap(j, which, c):
            return m.vec[:, bass.ds(base + 8 * j + 4 * which + c, 1)]

        def loads(part):
            a, b = PARTS[part]
            return [(n0[part], b - a, W), (n0[part] + b - a, KT, (b - a) * P)]

        def size_after(n):
            for part in range(2):
                for first, count, cols in loads(part):
                    if first <= n < first + count:
                        return cols
            return 0

        def in_pairs(eng, emit):
            for part in range(2):
                for down, (first, count, cols) in enumerate(loads(part)):
                    with eng.Fori(0, count // 2 - 1) as g:
                        for s in range(2):
                            emit(part, down, first + 2 * g + s, 2 * g + s, s, cols)
                    for s in range(2):
                        n = first + count - 2 + s
                        emit(part, down, n, count - 2 + s, s, size_after(n + 1))

        with nc.Block() as block:
            @block.sync
            def _(sp):
                def load(part, down, n, j, s, first=False):
                    a, b = PARTS[part]
                    src = d["w_down"][layer][j][:, a * P:b * P] if down else d["w_up"][layer][a + j]
                    if not first:
                        sp.wait_ge(low_done, n - 1)
                    sp.dma_start(raw[s][:, 0:(b - a) * P] if down else raw[s][:], src).then_inc(raw_in[s], 16)

                for part in range(2):
                    for down, (first, count, _) in enumerate(loads(part)):
                        start = 1 if first == 0 else 0
                        if start:
                            load(0, 0, 0, 0, 0, True)
                            load(0, 0, 1, 1, 1, True)
                        with sp.Fori(start, count // 2) as g:
                            for s in range(2):
                                load(part, down, first + 2 * g + s, 2 * g + s, s)

            @block.tensor
            def _(pe):
                def job(part, down, n, j, s, _):
                    a, b = PARTS[part]
                    pe.wait_ge(low_done, n + 1)
                    if not down:
                        pe.wait_ge(conv_done, 2 * (PARTS[part][0] + j) + 2)
                        for c in range(2):
                            for k in range(KT):
                                at = (c * KT + k) * P
                                for i, (wp, hp) in enumerate(w[s].passes(m.hs)):
                                    mm = pe.matmul(ps[:, 2 * s + c, :], wp[:, at:at + P], hp[:, k, :],
                                                   start=(k == 0 and i == 0), stop=(k == KT - 1 and i == 2))
                            mm.then_inc(up_made if c == 0 else used, 1)
                    else:
                        pe.wait_ge(hid_low, PARTS[part][1])
                        pe.wait_ge(added, KT * part + j + 1)
                        for k in range(b - a):
                            for i, (wp, hp) in enumerate(w[s].passes(hid)):
                                mm = pe.matmul(ps[:, 4 + s, :], wp[:, k * P:(k + 1) * P], hp[:, k, :],
                                               start=(k == 0 and i == 0), stop=(k == b - a - 1 and i == 2))
                        mm.then_inc(used, 1)
                pe.sem_inc(used, 1)
                in_pairs(pe, job)

            @block.scalar
            def _(act):
                def high(n, s, cols, first=False):
                    if cols == 0:
                        return
                    act.wait_ge(raw_in[s], 8 * (n - s) + 16)
                    if not first:
                        act.wait_ge(used, n)
                    act.activation(w[s].high[:, 0:cols], raw[s][:, 0:cols], ACT.Copy).then_inc(high_done, 1)

                def job(part, down, n, j, s, cols):
                    high(n + 1, 1 - s, cols)
                    if down:
                        return
                    t = PARTS[part][0] + j
                    for c in range(2):
                        act.wait_ge(*((up_made, t + 1) if c == 0 else (used, n + 2)))
                        act.wait_ge(gate_free, t + 1)
                        act.activation(y[s][:, c, :], ps[:, 2 * s + c, :], ACT.Identity, scale=tap(t, c, 2),
                                       bias=tap(t, c, 3)).then_inc(tap0, 1)
                    act.wait_ge(conv_done, 2 * t + 5)
                    act.activation(gate[s][:], y[s][:, 0, :], ACT.Silu).then_inc(gate_done, 1)
                    act.wait_ge(prod_done, t + 1)
                    act.activation(hid.high[:, bass.ds(j, 1), :].rearrange("p a t -> p (a t)"), gate[s][:], ACT.Copy).then_inc(hid_high, 1)

                high(0, 0, W, True)
                in_pairs(act, job)

            @block.vector
            def _(dve):
                dve.sem_inc(conv_done, 4)
                dve.sem_inc(gate_free, 2)
                dve.sem_inc(added, 2)

                def low(n, s, cols):
                    if cols == 0:
                        return
                    dve.wait_ge(high_done, n + 1)
                    dve.tensor_tensor(w[s].low[:, 0:cols], raw[s][:, 0:cols], w[s].high[:, 0:cols].bitcast(F32),
                                      ALU.subtract).then_inc(low_done, 1)

                def job(part, down, n, j, s, cols):
                    low(n + 1, 1 - s, cols)
                    if down:
                        to = m.x[:, bass.ds(j, 1), 0:SEQ].rearrange("p a t -> p (a t)")
                        dve.wait_ge(used, n + 2)
                        dve.tensor_tensor(to, ps[:, 4 + s, :], to, ALU.add).then_inc(added, 1)
                        return
                    t = PARTS[part][0] + j
                    for c in range(2):
                        dve.wait_ge(tap0, 2 * t + c + 1)
                        src = ps[:, 2 * s + c, :]
                        dve.scalar_tensor_tensor(y[s][:, c, 1:], src[:, 0:SEQ - 1], tap(t, c, 1), y[s][:, c, 1:],
                                                 ALU.mult, ALU.add).then_inc(tap1, 1)
                        dve.wait_ge(tap1, 2 * t + c + 1)
                        dve.scalar_tensor_tensor(y[s][:, c, 2:], src[:, 0:SEQ - 2], tap(t, c, 0), y[s][:, c, 2:],
                                                 ALU.mult, ALU.add).then_inc(conv_done, 1)
                    dve.wait_ge(gate_done, t + 1)
                    dve.wait_ge(conv_done, 2 * t + 6)
                    dve.tensor_tensor(gate[s][:], gate[s][:], y[s][:, 1, :], ALU.mult).then_inc(prod_done, 1)
                    dve.wait_ge(hid_high, t + 1)
                    slot = bass.ds(j, 1)
                    dve.tensor_tensor(hid.low[:, slot, :].rearrange("p a t -> p (a t)"), gate[s][:],
                                      hid.high[:, slot, :].rearrange("p a t -> p (a t)").bitcast(F32), ALU.subtract).then_inc(hid_low, 1)
                    dve.wait_ge(hid_low, t + 1)
                    dve.sem_inc(gate_free, 1)

                low(0, 0, W)
                in_pairs(dve, job)


def program(nc, d, out, scratch):
    stack = ExitStack()
    m = Machine(nc, stack)
    with stack:
        _, sb, sem = m.open(stack)
        m.x_in = sem("x_in")
        m.ps = stack.enter_context(nc.psum_tensor("banks", [P, 8, 512], F32))
        m.vec, m.rowv, m.const = sb("vec", [P, VEC.n]), sb("rowv", [P, ROWV.n]), sb("const", [P, CONST.n])
        m.x = sb("x", [P, KT, ALLT])
        m.mod, m.gain = sb("mod", [P, 96]), sb("gain", [P, KT, 2])
        m.neg_lambda = sb("neg_lambda", [P, 1])
        m.scratch1, m.scratch2 = sb("scratch1", [P, 2]), sb("scratch2", [P, 2])

        def mod(part):
            return lambda k, g: m.mod[:, 2 * (KT * part + k) + g:2 * (KT * part + k) + g + 1]

        def gain(k, g=0):
            return m.gain[:, k, g:g + 1]

        def norm_gain(name, at):
            return lambda k, g: VEC.of(m.vec, name, at + k, 1)

        load_and_modulation(m, d)
        modulation_gain(m, "g_pre_mix", 1)
        s1, sb1, _ = m.open()
        with s1:
            mix = sb1("mix", [P, KT, SEQ])
            s2, sb2, _ = m.open()
            with s2:
                m.q, m.k = sb2("q", [P, 2, SEQ]), sb2("k", [P, 2, CTX + SEQ + CTX])
                m.v, m.so, m.gates = sb2("v", [P, ALLT // P, D_ML]), sb2("so", [P, TT, D_ML]), sb2("gates", [16, ALLT])
                s3, sb3, _ = m.open()
                with s3:
                    m.h = sb3("h", [P, KT, ALLT])
                    rms_norm(m, m.x, m.h, [(0, SEQ), (SEQ, CTX)], gain, mod(0))
                    project_in(m, d, mix)
                mlstm(m, d, mix)
            y = sb1("y", [P, KT, SEQ])
            project_out(m, d["w_out"], mix, "b_out", y)
            gate_gain(m, "g_post_mix", 2)
            add_normed(m, y, gain)
        modulation_gain(m, "g_pre_ffn", 4)
        s1, sb1, _ = m.open()
        with s1:
            y = sb1("y", [P, KT, SEQ])
            m.dest, m.moved = sb1("dest", [P, TT, N_EXP]), sb1("moved", [P, TT, N_EXP, 3])
            m.owner_row, m.pairs_i = sb1("owner_row", [1, P], I32), sb1("pairs_i", [P, 1], I32)
            s2, sb2, _ = m.open()
            with s2:
                m.h = sb2("h", [P, KT, SEQ])
                rms_norm(m, m.x, m.h, [(0, SEQ)], gain, mod(3))
                route(m, d, scratch, y)
            experts(m, d, scratch)
            combine(m, scratch, y)
            gate_gain(m, "g_post_ffn", 5)
            add_normed(m, y, gain)
        lambda_value(m)
        for layer in range(2):
            s1, sb1, _ = m.open()
            with s1:
                o = sb1("o", [P, KT, SEQ])
                s2, sb2, _ = m.open()
                with s2:
                    m.h = sb2("h", [P, KT, SEQ])
                    rms_norm(m, m.x, m.h, [(0, SEQ)], norm_gain(("even_norm", "odd_norm")[layer], 0))
                    attention(m, d, ("w_even", "w_odd")[layer], o, layer == 1)
                if layer == 1:
                    head_norm(m, o)
                project_out(m, d[("w_eo", "w_oo")[layer]], o)
            s1, sb1, _ = m.open()
            with s1:
                m.hs = Split(sb1, "h", [P, KT, SEQ])
                rms_norm(m, m.x, m.hs, [(0, SEQ)], norm_gain("ffn_norm", layer * KT))
                conv_ffn(m, d, layer)
        s1, sb1, _ = m.open()
        with s1:
            y = sb1("y", [P, KT, SEQ])
            rms_norm(m, m.x, y, [(0, SEQ)], norm_gain("final_norm", 0), out=out)


def kernel(**inputs):
    import concourse.bacc as bacc
    from concourse.bass_utils import run_bass_kernel_spmd as run

    nc = bacc.Bacc("TRN2", target_bir_lowering=False, num_devices=1)
    arrays = {**constants(), **layouts(**{k: np.asarray(v) for k, v in inputs.items()})}
    d = {name: nc.dram_tensor(f"in_{name}", a.shape, F32, kind="ExternalInput").ap() for name, a in arrays.items()}
    out = nc.dram_tensor("out", (P, KT, SEQ), F32, kind="ExternalOutput").ap()
    scratch = {
        "h_rows": nc.dram_tensor("h_rows", (SEQ, D), F32).ap(),
        "y_rows": nc.dram_tensor("y_rows", (TOP_K * SEQ, D), F32).ap(),
        "block_expert": nc.dram_tensor("block_expert", (P, 1), I32).ap(),
    }
    program(nc, d, out, scratch)
    r = run(nc, [{f"in_{name}": a for name, a in arrays.items()}], core_ids=[0])
    y = r.results[0]["out"]
    return np.ascontiguousarray(y.transpose(2, 1, 0)).reshape(1, SEQ, D)
```

```python
from contextlib import ExitStack

import concourse.bass as bass
import numpy as np
from concourse import mybir

F32 = mybir.dt.float32
I32 = mybir.dt.int32
F32R = mybir.dt.float32r
ALU = mybir.AluOpType
ACT = mybir.ActivationFunctionType

P = 128
D = 1024
KT = D // P
SEQ = 512
CTX = 256
TT = SEQ // P
ALLT = SEQ + CTX
H_M = 4
QK = 64
DV = 128
D_QK = H_M * QK
D_ML = H_M * DV
D_CONV = 512
CW = 31
GRID = 64
ROWS = SEQ // GRID
HALO = CW // 2
N_EXP = 64
TOP_K = 8
D_EXP = 256
MAX_BLOCKS = (SEQ * TOP_K + N_EXP * (P - 1)) // P
ROUTE_SCALE = 2.5
D_FF = 2816
FT = D_FF // P
HD = 64
N_PAIR = 8
EPS = 1e-6
DIFF_EPS = 1e-5
NEG = -1.0e30
LAMBDA_INIT = 0.8 - 0.6 * float(np.exp(-0.3))


class Columns:

    def __init__(self, sizes):
        self.at, self.n = {}, 0
        for name, n in sizes:
            self.at[name] = (self.n, n)
            self.n += n

    def of(self, tile, name, j=0, n=None):
        a, size = self.at[name]
        n = size - j if n is None else n
        return tile[:, a + j:a + j + n]


VEC = Columns([
    ("c", KT * 2), ("b_ada", 48 * 2),
    ("g_pre_mix", KT), ("g_post_mix", KT), ("g_pre_ffn", KT), ("g_post_ffn", KT),
    ("b_q", 2), ("b_k", 2), ("b_ga", 4), ("b_gb", 4), ("b_gates", 2),
    ("conv_w", 4 * CW), ("conv_b", 4), ("ln_g", 4), ("ln_b", 4), ("b_out", KT),
    ("even_norm", KT), ("odd_norm", KT), ("ffn_norm", 2 * KT), ("final_norm", KT),
    ("ffn_conv", 2 * FT * 8), ("subln", 1), ("lambda", 4),
])
ROWV = Columns([("b_v", D_ML), ("b_o", D_ML), ("norm_g", D_ML), ("b_router", N_EXP)])
CONST = Columns([
    ("ident", P), ("ones", P), ("inv_d", P), ("inv_c", P), ("inv_v", P), ("before", P), ("slot", P),
    ("neg_block", P), ("eps", 1), ("diff_eps", 1), ("part", 1), ("token", TT), ("one", 1),
    ("mask_fwd", ALLT), ("mask_bwd", ALLT),
])
W_IN_TILES = [("gb", D_CONV), ("ga", D_CONV), ("q", D_QK), ("k", D_QK), ("gates", 16), ("v", D_ML), ("o", D_ML)]
W_IN = Columns([(n, KT * w) for n, w in W_IN_TILES])


def _cols(v, pad=P):
    return np.ascontiguousarray(np.asarray(v).reshape(-1, P).T)


def _kmaj(w):
    return w.reshape(-1, P, w.shape[1]).transpose(1, 0, 2)


def _flat(a):
    return np.ascontiguousarray(a).reshape(P, -1)


def constants():
    f = np.float32
    p = np.arange(P)[:, None]
    j = np.arange(P)[None, :]
    one = np.ones((P, P), f)
    fwd = np.zeros((P, ALLT), f)
    fwd[:, ALLT - P:] = np.where(j <= p, 0, NEG)
    bwd = np.zeros((P, ALLT), f)
    bwd[:, :P] = np.where(j >= p, 0, NEG)
    token = p + P * np.arange(TT)[None, :]
    parts = {
        "ident": np.eye(P), "ones": one, "inv_d": one / D, "inv_c": one / D_CONV, "inv_v": one / P,
        "before": (p < j), "slot": np.broadcast_to(j, (P, P)),
        "neg_block": np.broadcast_to(-P * j, (P, P)), "eps": np.full((P, 1), EPS),
        "diff_eps": np.full((P, 1), DIFF_EPS), "part": p, "token": token, "one": np.ones((P, 1)),
        "mask_fwd": fwd, "mask_bwd": bwd,
    }
    const = np.concatenate([np.asarray(parts[n], f) for n in CONST.at], axis=1)
    sel = np.zeros((64, 2, H_M, P), f)
    for h in range(H_M):
        sel[32 + h, 0, h] = 1
        sel[4 + h, 0, h] = -1
        sel[40 + h, 1, h] = 1
        sel[12 + h, 1, h] = 1
    d = p + (SEQ - P) - np.arange(SEQ)[None, :]
    count = (d <= 128).astype(f) + (d % 4 == 0) + (d % 16 == 0)
    plain = np.where(d >= 0, 0, NEG)
    mixed = np.where((d >= 0) & (count > 0), np.log(np.maximum(count, 1)) * HD ** 0.5, NEG)
    amask = np.stack([plain, plain, mixed, mixed], 1).astype(f)
    half = HD // 2
    inv = (1.0 / (np.float32(10000.0) ** (np.arange(half, dtype=f) * f(2.0) / f(HD)))).astype(f)
    ang = (np.arange(SEQ, dtype=f)[None, :] * inv[:, None]).astype(f)
    cos, sin = np.cos(ang).astype(f), np.sin(ang).astype(f)
    rope = np.stack([np.tile(cos, (4, 1)), np.concatenate([sin, -sin, sin, -sin])], 1)
    return {"const": const, "sel": sel.reshape(64, -1), "amask": _flat(amask), "rope": _flat(rope)}


def layouts(x, c, ctx, c_ctx, w_ada, b_ada, g_pre_mix, g_post_mix, g_pre_ffn, g_post_ffn, w_in, b_in,
            b_gate, mlstm_norm_g, conv_w, conv_b, conv_ln_g, conv_ln_b, w_out, b_out, w_router,
            b_router, we_gate, we_up, we_down, ws_gate, ws_up, ws_down, even_norm_2, even_w_in_2,
            even_w_out_2, odd_norm_2, odd_w_qkv_2, odd_lambda_q1_2, odd_lambda_k1_2, odd_lambda_q2_2,
            odd_lambda_k2_2, odd_subln_2, odd_w_out_2, ffn_norm_2, ffn_w_up_2, ffn_conv_w_2,
            ffn_conv_b_2, ffn_w_down_2, final_norm_2):
    def pad(v):
        out = np.zeros((P,), np.float32)
        out[:len(v)] = v
        return out[:, None]

    cuts = np.cumsum([D_QK, D_QK, D_ML, D_ML, 16, D_CONV])
    names = ("q", "k", "v", "o", "gates", "ga", "gb")
    wi = dict(zip(names, np.split(w_in[0], cuts, axis=1)))
    bi = dict(zip(names, np.split(b_in[0], cuts)))
    taps = np.concatenate([ffn_conv_w_2, ffn_conv_b_2[:, None]], 1)
    taps = taps.reshape(2, 4, 2, FT, P).transpose(4, 0, 3, 2, 1)
    vec = {
        "c": _flat(np.stack([_cols(c[0]), _cols(c_ctx)], 2)),
        "b_ada": _flat(np.broadcast_to(_cols(b_ada[0])[:, :, None], (P, 48, 2))),
        "g_pre_mix": _cols(g_pre_mix[0]), "g_post_mix": _cols(g_post_mix[0]),
        "g_pre_ffn": _cols(g_pre_ffn[0]), "g_post_ffn": _cols(g_post_ffn[0]),
        "b_q": _cols(bi["q"]), "b_k": _cols(bi["k"]), "b_ga": _cols(bi["ga"]), "b_gb": _cols(bi["gb"]),
        "b_gates": np.concatenate([pad(bi["gates"]), pad(b_gate[0].reshape(-1))], 1),
        "conv_w": _flat(conv_w[0].reshape(CW, 4, P).transpose(2, 1, 0)),
        "conv_b": _cols(conv_b[0]), "ln_g": _cols(conv_ln_g[0]), "ln_b": _cols(conv_ln_b[0]),
        "b_out": _cols(b_out[0]), "even_norm": _cols(even_norm_2[0]), "odd_norm": _cols(odd_norm_2[0]),
        "ffn_norm": _cols(ffn_norm_2.reshape(-1)), "final_norm": _cols(final_norm_2),
        "ffn_conv": _flat(taps), "subln": _cols(odd_subln_2[0]),
        "lambda": np.concatenate([pad(v[0]) for v in (odd_lambda_q1_2, odd_lambda_k1_2,
                                                      odd_lambda_q2_2, odd_lambda_k2_2)], 1),
    }
    row = {"b_v": bi["v"], "b_o": bi["o"], "norm_g": mlstm_norm_g[0].reshape(-1), "b_router": b_router[0]}
    qkv = {}
    for name, w in (("w_even", even_w_in_2[0]), ("w_odd", odd_w_qkv_2[0])):
        w = _kmaj(w).reshape(P, KT, 3, N_PAIR, P)
        qkv[name] = np.ascontiguousarray(w.transpose(3, 0, 2, 1, 4)).reshape(N_PAIR, P, -1)
    up = _kmaj(ffn_w_up_2[0]), _kmaj(ffn_w_up_2[1])
    up = np.stack([u.reshape(P, KT, 2, FT, P).transpose(3, 0, 2, 1, 4) for u in up])
    down = np.stack([_kmaj(w).reshape(P, FT, KT, P).transpose(2, 0, 1, 3) for w in ffn_w_down_2])
    gu = np.stack([we_gate[0], we_up[0]], 2).reshape(N_EXP, KT, P, 2 * D_EXP).transpose(0, 2, 1, 3)
    return {
        "x": _flat(_kmaj(np.concatenate([x[0], ctx[0]]).T)),
        "vec": np.concatenate([vec[n] for n in VEC.at], axis=1),
        "rowv": np.ascontiguousarray(np.broadcast_to(np.concatenate([row[n] for n in ROWV.at])[None], (P, ROWV.n))),
        "w_ada": np.ascontiguousarray(_kmaj(w_ada[0]).reshape(P, KT, 12, 512).transpose(2, 0, 1, 3)).reshape(12, P, -1),
        "w_in": np.concatenate([_flat(_kmaj(wi[n])) for n, _ in W_IN_TILES], axis=1),
        "w_out": _flat(_kmaj(w_out[0])), "w_router": _flat(_kmaj(w_router[0])),
        "w_gu": np.ascontiguousarray(gu).reshape(N_EXP, P, -1),
        "w_dn": np.ascontiguousarray(we_down[0].reshape(N_EXP, 2, P, D).transpose(0, 2, 1, 3)).reshape(N_EXP, P, -1),
        "ws_gu": _flat(_kmaj(np.concatenate([ws_gate[0], ws_up[0]], 1))), "ws_dn": _flat(_kmaj(ws_down[0])),
        **qkv,
        "w_eo": _flat(_kmaj(even_w_out_2[0])), "w_oo": _flat(_kmaj(odd_w_out_2[0])),
        "w_up": np.ascontiguousarray(up).reshape(2, FT, P, -1),
        "w_down": np.ascontiguousarray(down).reshape(2, KT, P, -1),
    }


class Steps:

    def __init__(self, sem):
        self.sem, self.n = sem, 0

    def __call__(self, eng, ins):
        self.n += 1
        ins.then_inc(self.sem, 1)
        eng.wait_ge(self.sem, self.n)


class Count:

    def __init__(self, reg, k=1, c=0):
        self.reg, self.k, self.c = reg, k, c

    def __add__(self, c):
        return Count(self.reg, self.k, self.c + c)

    def __sub__(self, c):
        return self + -c

    def __rmul__(self, n):
        return Count(self.reg, self.k * n, self.c * n)

    @property
    def value(self):
        return self.reg * self.k + self.c if self.c else self.reg * self.k


def value(n):
    return n.value if isinstance(n, Count) else n


class Machine:

    def __init__(self, nc, stack):
        self.nc, self.stack, self.stage = nc, stack, 0

    def open(self, stack=None):
        self.stage += 1
        nc, stack, n, sems = self.nc, stack or ExitStack(), self.stage, []

        def clear():
            if sems:
                nc.clear_and_free_semaphores(sems)
                nc.all_engine_barrier()
        stack.callback(clear)

        def sb(name, shape, dt=F32):
            return stack.enter_context(self.nc.sbuf_tensor(f"{name}_{n}", shape, dt))

        def sem(name):
            sems.append(nc.alloc_semaphore(f"{name}_{n}"))
            return sems[-1]
        return stack, sb, sem


def load_and_modulation(m, d):
    nc, ps = m.nc, m.ps
    stack, sb, sem = m.open()
    N_AB = 6 * D // 512
    with stack:
        w = [sb(f"w_ada{s}", [P, KT, 512]) for s in range(2)]
        cs = sb("silu_c", [P, KT, 2])
        row = [sb(f"row{s}", [2, 512]) for s in range(2)]
        small_in, x_in, w_in = sem("small_in"), m.x_in, [sem("w_in0"), sem("w_in1")]
        silu_done, w_used, row_copied, turned, added, seen = (
            sem(s) for s in ("silu_done", "w_used", "row_copied", "turned", "added", "seen"))
        with nc.Block() as block:
            @block.sync
            def _(sp):
                sp.dma_start(m.vec[:], d["vec"]).then_inc(small_in, 16)
                for s in range(2):
                    sp.dma_start(w[s][:].rearrange("p k n -> p (k n)"), d["w_ada"][s]).then_inc(w_in[s], 16)
                sp.dma_start(m.const[:], d["const"]).then_inc(small_in, 16)
                sp.dma_start(m.rowv[:], d["rowv"]).then_inc(small_in, 16)
                sp.dma_start(m.x[:].rearrange("p k t -> p (k t)"), d["x"]).then_inc(x_in, 16)
                with sp.Fori(1, N_AB // 2) as g:
                    for s in range(2):
                        sp.wait_ge(w_used, 2 * g - 1 + s)
                        sp.dma_start(w[s][:].rearrange("p k n -> p (k n)"), d["w_ada"][2 * g + s]).then_inc(w_in[s], 16)
                sp.wait_ge(small_in, 48)
                sp.wait_ge(x_in, 16)

            @block.tensor
            def _(pe):
                ident = CONST.of(m.const, "ident")[0:2, 0:2]

                def product(n, s, loads):
                    pe.wait_ge(w_in[s], loads)
                    pe.wait_ge(row_copied, n + 1)
                    for k in range(KT):
                        mm = pe.matmul(ps[0:2, s, :], cs[:, k, :], w[s][:, k, :], start=(k == 0), stop=(k == KT - 1))
                    mm.then_inc(w_used, 1)

                def turn(n, s):
                    pe.wait_ge(row_copied, n + 3)
                    pe.wait_ge(added, n + 1)
                    pe.sem_inc(seen, 1)
                    for a in range(4):
                        mm = pe.transpose(ps[:, 2 + s, 2 * a:2 * a + 2], row[s][:, a * P:(a + 1) * P], ident)
                    mm.then_inc(turned, 1)

                pe.wait_ge(silu_done, 1)
                product(0, 0, 16)
                with pe.Fori(0, N_AB // 2 - 1) as g:
                    product(2 * g + 1, 1, 16 * g + 16)
                    turn(2 * g, 0)
                    product(2 * g + 2, 0, 16 * g + 32)
                    turn(2 * g + 1, 1)
                product(N_AB - 1, 1, 8 * N_AB)
                turn(N_AB - 2, 0)
                turn(N_AB - 1, 1)

            @block.scalar
            def _(act):
                act.wait_ge(small_in, 48)
                act.activation(cs[:].rearrange("p k c -> p (k c)"), VEC.of(m.vec, "c"), ACT.Silu).then_inc(silu_done, 1)
                act.sem_inc(row_copied, 2)
                with act.Fori(0, N_AB // 2) as g:
                    for s in range(2):
                        act.wait_ge(w_used, 2 * g + s + 1)
                        act.wait_ge(added, 2 * g + s + 1)
                        act.activation(row[s][:], ps[0:2, s, :], ACT.Copy).then_inc(row_copied, 1)

            @block.vector
            def _(dve):
                dve.sem_inc(added, 2)
                dve.wait_ge(small_in, 48)
                b_ada = VEC.of(m.vec, "b_ada")
                with dve.Fori(0, N_AB // 2) as g:
                    for s in range(2):
                        dve.wait_ge(turned, 2 * g + s + 1)
                        at = bass.ds(16 * g + 8 * s, 8)
                        dve.tensor_tensor(m.mod[:, at], ps[:, 2 + s, 0:8], b_ada[:, at], ALU.add).then_inc(added, 1)


class Split:

    def __init__(self, sb, name, shape):
        self.high, self.low = sb(name + "_high", shape, F32R), sb(name + "_low", shape, F32R)

    def passes(self, other):
        return (self.high, other.high), (self.high, other.low), (self.low, other.high)


def rms_norm(m, src, dst, groups, gain, shift=None, out=None, whole=None):
    nc, ps, eps = m.nc, m.ps, CONST.of(m.const, "eps")
    inv_d = CONST.of(m.const, "inv_d")
    tokens = sum(n for _, n in groups)
    stack, sb, sem = m.open()
    with stack:
        sq = sb("sq", [P, KT, tokens])
        std, rstd = sb("std", [P, tokens]), sb("rstd", [P, tokens])
        sq_done, ms_done, std_done, rstd_done, scaled, shifted, rounded, stored = (
            sem(s) for s in ("sq_done", "ms_done", "std_done", "rstd_done", "scaled", "shifted", "rounded", "stored"))
        split = isinstance(dst, Split)
        in_sq = shift or split
        result = sq if whole is None else whole
        with nc.Block() as block:
            @block.scalar
            def _(act):
                for k in range(KT):
                    act.activation(sq[:, k, :], src[:, k, 0:tokens], ACT.Square).then_inc(sq_done, 1)
                for g, (t, n) in enumerate(groups):
                    act.wait_ge(ms_done, g + 1)
                    act.activation(std[:, t:t + n], ps[:, g, 0:n], ACT.Sqrt, bias=eps).then_inc(std_done, 1)
                if shift:
                    for g, (t, n) in enumerate(groups):
                        for k in range(KT):
                            act.wait_ge(scaled, g * KT + k + 1)
                            to = result if split else dst
                            act.activation(to[:, k, t:t + n], sq[:, k, t:t + n], ACT.Identity, bias=shift(k, g)).then_inc(shifted, 1)
                if split:
                    for g, (t, n) in enumerate(groups):
                        for k in range(KT):
                            act.wait_ge(shifted if shift else scaled, g * KT + k + 1)
                            act.activation(dst.high[:, k, t:t + n], result[:, k, t:t + n], ACT.Copy).then_inc(rounded, 1)

            @block.tensor
            def _(pe):
                for k in range(KT):
                    pe.wait_ge(sq_done, k + 1)
                    for g, (t, n) in enumerate(groups):
                        mm = pe.matmul(ps[:, g, 0:n], inv_d, sq[:, k, t:t + n], start=(k == 0), stop=(k == KT - 1))
                        if k == KT - 1:
                            mm.then_inc(ms_done, 1)

            @block.vector
            def _(dve):
                for g, (t, n) in enumerate(groups):
                    dve.wait_ge(std_done, g + 1)
                    dve.reciprocal(rstd[:, t:t + n], std[:, t:t + n]).then_inc(rstd_done, 1)
                for g, (t, n) in enumerate(groups):
                    dve.wait_ge(rstd_done, g + 1)
                    dve.wait_ge(ms_done, g + 1)
                    for k in range(KT):
                        to = (sq if shift else result) if in_sq else dst
                        dve.scalar_tensor_tensor(to[:, k, t:t + n], src[:, k, t:t + n], gain(k, g), rstd[:, t:t + n],
                                                 ALU.mult, ALU.mult).then_inc(scaled, 1)
                if split:
                    for g, (t, n) in enumerate(groups):
                        for k in range(KT):
                            dve.wait_ge(rounded, g * KT + k + 1)
                            dve.tensor_tensor(dst.low[:, k, t:t + n], result[:, k, t:t + n], dst.high[:, k, t:t + n].bitcast(F32),
                                              ALU.subtract)

            @block.sync
            def _(sp):
                if out is not None:
                    for k in range(KT):
                        sp.wait_ge(scaled, k + 1)
                        sp.dma_start(out[:, k, :], dst[:, k, 0:tokens]).then_inc(stored, 16)
                    sp.wait_ge(stored, 16 * KT)


def add_normed(m, y, gain):
    nc, ps = m.nc, m.ps
    stack, sb, sem = m.open()
    with stack:
        sq = sb("sq", [P, KT, SEQ])
        std, rstd = sb("std", [P, SEQ]), sb("rstd", [P, SEQ])
        sq_done, ms_done, std_done, rstd_done, scaled = (
            sem(s) for s in ("sq_done", "ms_done", "std_done", "rstd_done", "scaled"))
        with nc.Block() as block:
            @block.scalar
            def _(act):
                for k in range(KT):
                    act.activation(sq[:, k, :], y[:, k, :], ACT.Square).then_inc(sq_done, 1)
                act.wait_ge(ms_done, 1)
                act.activation(std[:], ps[:, 0, :], ACT.Sqrt, bias=CONST.of(m.const, "eps")).then_inc(std_done, 1)

            @block.tensor
            def _(pe):
                for k in range(KT):
                    pe.wait_ge(sq_done, k + 1)
                    mm = pe.matmul(ps[:, 0, :], CONST.of(m.const, "inv_d"), sq[:, k, :], start=(k == 0), stop=(k == KT - 1))
                mm.then_inc(ms_done, 1)

            @block.vector
            def _(dve):
                dve.wait_ge(std_done, 1)
                dve.reciprocal(rstd[:], std[:]).then_inc(rstd_done, 1)
                dve.wait_ge(rstd_done, 1)
                for k in range(KT):
                    dve.scalar_tensor_tensor(sq[:, k, :], y[:, k, :], gain(k), rstd[:], ALU.mult, ALU.mult).then_inc(scaled, 1)
                for k in range(KT):
                    dve.wait_ge(scaled, k + 1)
                    dve.tensor_tensor(m.x[:, k, 0:SEQ], sq[:, k, :], m.x[:, k, 0:SEQ], ALU.add)


def modulation_gain(m, name, part):
    nc = m.nc
    stack, sb, sem = m.open()
    with stack:
        with nc.Block() as block:
            @block.vector
            def _(dve):
                mod = m.mod[:].rearrange("p (j c) -> p j c", c=2)
                for c in range(2):
                    dve.scalar_tensor_tensor(m.gain[:, :, c], mod[:, KT * part:KT * part + KT, c], 1.0,
                                             VEC.of(m.vec, name), ALU.add, ALU.mult)


def gate_gain(m, name, part):
    nc = m.nc
    with nc.Block() as block:
        @block.vector
        def _(dve):
            mod = m.mod[:].rearrange("p (j c) -> p j c", c=2)
            dve.tensor_tensor(m.gain[:, :, 0], mod[:, KT * part:KT * part + KT, 0], VEC.of(m.vec, name), ALU.mult)


def project_in(m, d, mix):
    nc, ps = m.nc, m.ps
    stack, sb, sem = m.open()
    with stack:
        w_first = W_IN.n - 2 * KT * D_ML
        w = sb("w_in", [P, w_first])
        gb, u = sb("gate_b", [P, 4, SEQ]), sb("u", [P, 4, ROWS, GRID + 2 * HALO])
        acc = mix[:, 4:8, :]
        centre = u[:].rearrange("p j r t -> p (j r t)")[:, 0:4 * SEQ].rearrange("p (j t) -> p j t", j=4)
        stat = sb("conv_stat", [P, 2, SEQ])
        w_in = [sem(f"w_in_{n}") for n, _ in W_IN_TILES]
        bank_full, act_free, dve_free, sig, u_ready, dve_own, conv_sq, mean_done, centred, var_done, std_done, normed = (
            sem(s) for s in ("bank_full", "act_free", "dve_free", "sig", "u_ready", "dve_own", "conv_sq", "mean_done",
                             "centred", "var_done", "std_done", "normed"))

        def wt(name):
            a, n = W_IN.at[name]
            a -= w_first if name in ("v", "o") else 0
            return w[:, a:a + n].rearrange("p (k n) -> p k n", k=KT)

        x_, c_ = (0, SEQ), (SEQ, CTX)
        jobs = [("gb", j, x_, "act") for j in range(4)] + [("ga", j, x_, "dve") for j in range(4)]
        jobs += [("q", j, x_, "dve") for j in range(2)]
        jobs += [("k", j, t, "dve") for j in range(2) for t in (x_, c_)]
        jobs += [("gates", 0, t, "dve") for t in (x_, c_)]
        jobs += [("v", None, i, "act") for i in range(ALLT // P)] + [("o", None, i, "act") for i in range(TT)]
        NB = 6
        CB, VB = 6, 7
        mean_at, var_at = len(jobs) - 3, len(jobs) - 2

        def done_before(n, reader):
            return sum(1 for j in jobs[:n] if j[3] == reader)

        with nc.Block() as block:
            @block.sync
            def _(sp):
                for i, (name, _) in enumerate(W_IN_TILES):
                    a, n = W_IN.at[name]
                    if name in ("v", "o"):
                        sp.wait_ge(bank_full, 4 if name == "v" else 8)
                    sp.dma_start(wt(name).rearrange("p k n -> p (k n)"), d["w_in"][:, a:a + n]).then_inc(w_in[i], 16)

            @block.tensor
            def _(pe):
                seen, inv_c = set(), CONST.of(m.const, "inv_c")
                for n, (name, j, t, reader) in enumerate(jobs):
                    if n == mean_at:
                        pe.wait_ge(u_ready, 1)
                        for c in range(4):
                            mm = pe.matmul(ps[:, CB, :], inv_c, acc[:, c, :], start=(c == 0), stop=(c == 3))
                        mm.then_inc(mean_done, 1)
                    if n == var_at:
                        for c in range(4):
                            pe.wait_ge(conv_sq, c + 1)
                            mm = pe.matmul(ps[:, VB, :], inv_c, gb[:, c, :], start=(c == 0), stop=(c == 3))
                        mm.then_inc(var_done, 1)
                    if n >= NB:
                        pe.wait_ge(act_free if jobs[n - NB][3] == "act" else dve_free,
                                   done_before(n - NB + 1, jobs[n - NB][3]))
                    i = [x for x, _ in W_IN_TILES].index(name)
                    if name not in seen:
                        pe.wait_ge(w_in[i], 16)
                        seen.add(name)
                    bank = ps[:, n % NB, :]
                    for k in range(KT):
                        if j is None:
                            mm = pe.matmul(bank, m.h[:, k, t * P:t * P + P], wt(name)[:, k, :], start=(k == 0), stop=False)
                        else:
                            cols = min(P, W_IN.at[name][1] // KT)
                            mm = pe.matmul(bank[0:cols, 0:t[1]], wt(name)[:, k, j * P:j * P + cols],
                                           m.h[:, k, t[0]:t[0] + t[1]], start=(k == 0), stop=(k == KT - 1))
                    if j is None:
                        mm = pe.matmul(bank, CONST.of(m.const, "ones")[0:1, :], ROWV.of(m.rowv, "b_" + name)[0:1, :],
                                       start=False, stop=True)
                    mm.then_inc(bank_full, 1)

            @block.scalar
            def _(act):
                for n, (name, j, t, reader) in enumerate(jobs):
                    if n == var_at:
                        for c in range(4):
                            act.wait_ge(centred, c + 1)
                            act.activation(gb[:, c, :], centre[:, c, :], ACT.Square).then_inc(conv_sq, 1)
                        act.wait_ge(var_done, 1)
                        act.activation(stat[:, 0, :], ps[:, VB, :], ACT.Sqrt, bias=CONST.of(m.const, "eps")).then_inc(std_done, 1)
                    if reader != "act":
                        continue
                    act.wait_ge(bank_full, n + 1)
                    bank = ps[:, n % NB, :]
                    if name == "gb":
                        act.activation(gb[:, j, :], bank, ACT.Sigmoid, bias=VEC.of(m.vec, "b_gb", j, 1)).then_inc(act_free, 1)
                    elif name == "o":
                        act.activation(m.so[:, t, :], bank, ACT.Sigmoid).then_inc(act_free, 1)
                    else:
                        act.activation(m.v[:, t, :], bank, ACT.Copy).then_inc(act_free, 1)
                for j in range(4):
                    act.wait_ge(normed, j + 1)
                    act.activation(acc[:, j, :], acc[:, j, :], ACT.Silu, scale=VEC.of(m.vec, "ln_g", j, 1),
                                   bias=VEC.of(m.vec, "ln_b", j, 1))

            @block.vector
            def _(dve):
                own = Steps(dve_own)
                own(dve, dve.memset(u[:], 0.0))

                def read(n):
                    name, j, t, _ = jobs[n]
                    dve.wait_ge(bank_full, n + 1)
                    bank = ps[:, n % NB, :]
                    if name == "ga":
                        if j == 0:
                            dve.wait_ge(act_free, 4)
                        dve.scalar_tensor_tensor(
                            u[:, j, :, HALO:HALO + GRID], bank.rearrange("p (r t) -> p r t", t=GRID),
                            VEC.of(m.vec, "b_ga", j, 1), gb[:, j, :].rearrange("p (r t) -> p r t", t=GRID),
                            ALU.add, ALU.mult).then_inc(dve_free, 1)
                    elif name == "q":
                        dve.tensor_scalar(m.q[:, j, :], bank, VEC.of(m.vec, "b_q", j, 1), None, ALU.add).then_inc(dve_free, 1)
                    elif name == "k":
                        scale = QK ** -0.5
                        b = VEC.of(m.vec, "b_k", j, 1)
                        if t is x_:
                            dve.tensor_scalar(m.k[:, j, CTX:CTX + SEQ], bank, b, scale, ALU.add, ALU.mult).then_inc(dve_free, 1)
                        else:
                            dve.tensor_scalar(m.k[:, j, 0:CTX], bank[:, 0:CTX], b, scale, ALU.add, ALU.mult)
                            dve.tensor_scalar(m.k[:, j, CTX + SEQ:], bank[:, 0:CTX], b, scale, ALU.add, ALU.mult).then_inc(dve_free, 1)
                    else:
                        dve.tensor_scalar(m.gates[:, t[0]:t[0] + t[1]], bank[0:16, 0:t[1]],
                                          VEC.of(m.vec, "b_gates", 0, 1)[0:16], VEC.of(m.vec, "b_gates", 1, 1)[0:16],
                                          ALU.add, ALU.add).then_inc(dve_free, 1)
                def taps(tap):
                    for j in range(4):
                        src = u[:, j, :, tap:tap + GRID]
                        to = acc[:, j, :].rearrange("p (r t) -> p r t", t=GRID)
                        w_tap = VEC.of(m.vec, "conv_w", j * CW + tap, 1)
                        if tap == 0:
                            ins = dve.tensor_scalar(to, src, w_tap, VEC.of(m.vec, "conv_b", j, 1), ALU.mult, ALU.add)
                        else:
                            ins = dve.scalar_tensor_tensor(to, src, w_tap, to, ALU.mult, ALU.add)
                    own(dve, ins)

                mine = [n for n, job in enumerate(jobs) if job[3] == "dve"]
                for n in mine[:4]:
                    read(n)
                dve.wait_ge(dve_free, 4)
                for tap in range(CW):
                    taps(tap)
                    if tap % 2 == 1 and 4 + tap // 2 < len(mine):
                        read(mine[4 + tap // 2])
                dve.tensor_copy(m.scratch1[:, 0:1], acc[:, 0, 0:1]).then_inc(u_ready, 1)
                dve.wait_ge(mean_done, 1)
                for j in range(4):
                    dve.tensor_tensor(centre[:, j, :], acc[:, j, :], ps[:, CB, :], ALU.subtract).then_inc(centred, 1)
                dve.wait_ge(std_done, 1)
                own(dve, dve.reciprocal(stat[:, 1, :], stat[:, 0, :]))
                dve.wait_ge(centred, 4)
                for j in range(4):
                    dve.tensor_tensor(acc[:, j, :], centre[:, j, :], stat[:, 1, :], ALU.mult).then_inc(normed, 1)


def mlstm(m, d, mix):
    nc, ps = m.nc, m.ps
    M_LEAST = -60.0
    stack, sb, sem = m.open()
    L = CTX + SEQ + CTX
    with stack:
        sel = sb("sel", [64, 2, H_M, P])
        lsig, tmp, zero = sb("lsig", [16, ALLT]), sb("lsig_tmp", [16, ALLT]), sb("zero", [16, SEQ])
        sums = [sb(f"run{i}", [64, ALLT]) for i in range(2)]
        run = [t[0:16] for t in sums]
        a_col = sb("a_col", [P, TT, 2, 16])
        r_row = sb("r_row", [P, 2, H_M, ALLT])
        t_sb = [sb(f"logits{i}", [P, ALLT]) for i in range(2)]
        p_sb = [sb(f"decay{i}", [P, ALLT]) for i in range(2)]
        s_sb = [sb(f"scores{i}", [P, ALLT]) for i in range(2)]
        st_sb = [sb(f"scores_t{i}", [P, ALLT]) for i in range(2)]
        cols = [sb(f"row_cols{i}", [P, 8, 2]) for i in range(4)]
        hout = sb("hout", [P, TT, D_ML])
        ss, rs = sb("ss", [P, TT * H_M]), sb("rs", [P, 2, TT * H_M])
        (sel_in, l_abs, l_exp, l_ln, own_s, run_done, rr_done, rr_copied, ac_done, ac_copied, qk_done, qk_free, t_done,
         p_done, s_done, tr_done, st_done, pv_done, h_done, thr_done, ss_done, rs_done, mixed, mt_done) = (
            sem(s) for s in ("sel_in", "l_abs", "l_exp", "l_ln", "own", "run_done", "rr_done", "rr_copied", "ac_done",
                             "ac_copied", "qk_done", "qk_free", "t_done", "p_done", "s_done", "tr_done", "st_done",
                             "pv_done", "h_done", "thr_done", "ss_done", "rs_done", "mixed", "mt_done"))
        units = [(h, i) for h in range(H_M) for i in range(TT)]
        subs = [(h, i, r) for h, i in units for r in range(2)]

        def keys(i, r):
            return (0, CTX + P * (i + 1)) if r == 0 else (CTX + P * i, SEQ - P * i + CTX)

        with nc.Block() as block:
            @block.sync
            def _(sp):
                sp.dma_start(sel[:].rearrange("p a b n -> p (a b n)"), d["sel"]).then_inc(sel_in, 16)

            @block.scalar
            def _(act):
                act.wait_ge(l_abs, 1)
                act.activation(tmp[:], tmp[:], ACT.Exp, scale=-1.0).then_inc(l_exp, 1)
                act.wait_ge(l_exp, 1)
                act.activation(tmp[:], tmp[:], ACT.Ln, bias=1.0).then_inc(l_ln, 1)
                for n in range(2 * H_M):
                    r, h = divmod(n, H_M)
                    act.wait_ge(rr_done, n + 1)
                    b = 2 * (n % 2)
                    act.activation(r_row[:, r, h, 0:SEQ], ps[:, b, :], ACT.Copy)
                    act.activation(r_row[:, r, h, SEQ:], ps[:, b + 1, 0:CTX], ACT.Copy).then_inc(rr_copied, 1)
                act.wait_ge(ac_done, 1)
                act.activation(a_col[:].rearrange("p i r g -> p (i r g)"), ps[:, 4, 0:TT * 32], ACT.Copy).then_inc(ac_copied, 1)

                def copy_t(n):
                    h, i, r = subs[n]
                    k0, w = keys(i, r)
                    act.wait_ge(tr_done, n + 1)
                    if n >= 2:
                        act.wait_ge(pv_done, n - 1)
                    act.activation(st_sb[n % 2][:, 0:min(w, SEQ)], ps[:, 4, 0:min(w, SEQ)], ACT.Copy)
                    if w > SEQ:
                        act.activation(st_sb[n % 2][:, SEQ:w], ps[:, 5, 0:w - SEQ], ACT.Copy)
                    act.activation(m.scratch2[:, 0:1], m.scratch2[:, 1:2], ACT.Copy).then_inc(st_done, 1)

                for n, (h, i, r) in enumerate(subs):
                    k0, w = keys(i, r)
                    act.wait_ge(t_done, n + 1)
                    c = cols[n % 4]
                    if n >= 2:
                        act.wait_ge(s_done, n - 1)
                    if n >= 4:
                        act.wait_ge(h_done, n - 3)
                    act.activation(p_sb[n % 2][:, 0:w], t_sb[n % 2][:, 0:w], ACT.Exp, bias=c[:, 2, 0:1]).then_inc(p_done, 1)
                    act.activation(c[:, 3, 0:1], c[:, 1, 0:1], ACT.Exp, scale=-1.0).then_inc(thr_done, 1)
                    if n >= 1:
                        copy_t(n - 1)
                copy_t(len(subs) - 1)
                act.wait_ge(ss_done, 1)
                act.activation(rs[:, 0, :], ss[:], ACT.Sqrt, scale=1.0 / DV, bias=CONST.of(m.const, "eps")).then_inc(rs_done, 1)
                for j in range(4):
                    act.wait_ge(mt_done, j + 1)
                    act.activation(mix[:, j, :], ps[:, j, :], ACT.Copy)

            @block.vector
            def _(dve):
                own = Steps(own_s)
                dve.memset(zero[:], 0.0)
                for t in sums:
                    ins = dve.memset(t[:], 0.0)
                own(dve, ins)
                dve.memset(m.scratch2[:, 0:2], 0.0)
                own(dve, dve.tensor_scalar(lsig[:], m.gates[:], -1.0, None, ALU.mult))
                dve.tensor_tensor(tmp[:], lsig[:], m.gates[:], ALU.max).then_inc(l_abs, 1)
                dve.wait_ge(l_ln, 1)
                own(dve, dve.scalar_tensor_tensor(lsig[:], m.gates[:], 0.0, tmp[:], ALU.min, ALU.subtract))
                x, c = slice(0, SEQ), slice(SEQ, ALLT)
                own(dve, dve.tensor_tensor_scan(run[0][:, c], lsig[:, c], zero[:, 0:CTX], 0.0, ALU.add, ALU.add))
                own(dve, dve.tensor_tensor_scan(run[0][:, x], lsig[:, x], zero[:], run[0][:, ALLT - 1:ALLT], ALU.add, ALU.add))
                own(dve, dve.tensor_tensor_scan(tmp[:, x], lsig[:, x], zero[:], 0.0, ALU.add, ALU.add))
                own(dve, dve.tensor_tensor_scan(tmp[:, c], lsig[:, c], zero[:, 0:CTX], tmp[:, SEQ - 1:SEQ], ALU.add, ALU.add))
                for t in sums:
                    dve.tensor_copy(t[32:48], m.gates[:])
                dve.tensor_tensor(run[1][:], tmp[:], lsig[:], ALU.subtract).then_inc(run_done, 1)
                dve.wait_ge(rr_copied, 2 * H_M)
                dve.wait_ge(ac_copied, 1)

                def finish(n):
                    h, i, r = subs[n]
                    c = cols[n % 4]
                    dve.wait_ge(thr_done, n + 1)
                    own(dve, dve.scalar_tensor_tensor(c[:, 5, 0:1], c[:, 4, 0:1], -1.0, c[:, 3, 0:1], ALU.mult, ALU.max))
                    own(dve, dve.tensor_tensor(c[:, 5, 0:1], c[:, 5, 0:1], c[:, 4, 0:1], ALU.max))
                    own(dve, dve.reciprocal(c[:, 6, 0:1], c[:, 5, 0:1]))
                    dve.wait_ge(pv_done, n + 1)
                    to, pv = hout[:, i, h * DV:(h + 1) * DV], ps[:, 6 + n % 2, 0:DV]
                    if r == 0:
                        ins = dve.tensor_scalar(to, pv, c[:, 6, 0:1], None, ALU.mult)
                    else:
                        ins = dve.scalar_tensor_tensor(to, pv, c[:, 6, 0:1], to, ALU.mult, ALU.add)
                    ins.then_inc(h_done, 1)
                    dve.wait_ge(h_done, n + 1)

                def scores(n):
                    h, i, r = subs[n]
                    k0, w = keys(i, r)
                    dve.wait_ge(p_done, n + 1)
                    dve.wait_ge(qk_done, n // 2 + 1)
                    if n >= 2:
                        dve.wait_ge(tr_done, n - 1)
                    b = 2 * ((n // 2) % 2)
                    qk = ps[:, b:b + 2, :].rearrange("p b n -> p (b n)")[:, k0:k0 + w]
                    dve.tensor_tensor_reduce(s_sb[n % 2][:, 0:w], p_sb[n % 2][:, 0:w], qk, 1.0, 0.0, ALU.mult, ALU.add,
                                             cols[n % 4][:, 4, 0:1]).then_inc(s_done, 1)
                    dve.wait_ge(s_done, n + 1)

                for n, (h, i, r) in enumerate(subs):
                    k0, w = keys(i, r)
                    c = cols[n % 4]
                    row = r_row[:, r, h, :]
                    mask = CONST.of(m.const, "mask_fwd")[:, ALLT - w:] if r == 0 else CONST.of(m.const, "mask_bwd")[:, 0:w]
                    src = row[:, 0:w] if r == 0 else row[:, k0 - CTX:]
                    own(dve, dve.tensor_tensor_reduce(t_sb[n % 2][:, 0:w], src, mask, 1.0, NEG, ALU.add, ALU.max, c[:, 0, 0:1]))
                    gate = (4 + h) if r == 0 else (12 + h)
                    a = a_col[:, i, r, gate:gate + 1]
                    if r == 0:
                        own(dve, dve.tensor_scalar(c[:, 1, 0:1], c[:, 0, 0:1], a, M_LEAST, ALU.add, ALU.max))
                        dve.tensor_tensor(c[:, 2, 0:1], a, c[:, 1, 0:1], ALU.subtract).then_inc(t_done, 1)
                    else:
                        own(dve, dve.tensor_scalar(c[:, 1, 0:1], c[:, 0, 0:1], a, M_LEAST, ALU.subtract, ALU.max))
                        dve.scalar_tensor_tensor(c[:, 2, 0:1], a, -1.0, c[:, 1, 0:1], ALU.mult, ALU.subtract).then_inc(t_done, 1)
                    if n >= 1:
                        scores(n - 1)
                    if n >= 3:
                        finish(n - 3)
                last = len(subs) - 1
                scores(last)
                finish(last - 2)
                finish(last - 1)
                finish(last)
                for i in range(TT):
                    for h in range(H_M):
                        hh = hout[:, i, h * DV:(h + 1) * DV]
                        ins = dve.tensor_tensor_reduce(t_sb[0][:, 0:DV], hh, hh, 1.0, 0.0, ALU.mult, ALU.add,
                                                       ss[:, i * H_M + h:i * H_M + h + 1])
                        own(dve, ins)
                dve.tensor_copy(m.scratch1[:, 0:1], m.scratch1[:, 0:1]).then_inc(ss_done, 1)
                dve.wait_ge(rs_done, 1)
                own(dve, dve.reciprocal(rs[:, 1, :], rs[:, 0, :]))
                for i in range(TT):
                    for h in range(H_M):
                        hh = hout[:, i, h * DV:(h + 1) * DV]
                        ins = dve.scalar_tensor_tensor(hh, hh, rs[:, 1, i * H_M + h:i * H_M + h + 1],
                                                       ROWV.of(m.rowv, "norm_g", h * DV, DV), ALU.mult, ALU.mult)
                    own(dve, ins)
                    dve.tensor_tensor(hout[:, i, :], hout[:, i, :], m.so[:, i, :], ALU.mult).then_inc(mixed, 1)

            @block.tensor
            def _(pe):
                pe.wait_ge(sel_in, 16)
                pe.wait_ge(run_done, 1)
                for n in range(2 * H_M):
                    r, h = divmod(n, H_M)
                    if n >= 2:
                        pe.wait_ge(rr_copied, n - 1)
                    b = 2 * (n % 2)
                    order = [(SEQ, CTX, 0), (0, CTX, CTX), (CTX, CTX, SEQ)] if r == 0 else [(0, SEQ, 0), (SEQ, CTX, SEQ)]
                    for t, w, at in order:
                        to = ps[:, b + at // SEQ, at % SEQ:at % SEQ + w]
                        mm = pe.matmul(to, sel[:, r, h, :], sums[r][:, t:t + w], start=True, stop=True)
                    mm.then_inc(rr_done, 1)
                for i in range(TT):
                    for r in range(2):
                        at = (2 * i + r) * 16
                        mm = pe.transpose(ps[:, 4, at:at + 16], run[r][:, i * P:(i + 1) * P], CONST.of(m.const, "ident")[0:16, 0:16])
                mm.then_inc(ac_done, 1)
                pe.wait_ge(rr_copied, 2 * H_M)
                pe.wait_ge(ac_copied, 1)
                ident = CONST.of(m.const, "ident")

                def qk(u):
                    h, i = units[u]
                    if u >= 2:
                        pe.wait_ge(s_done, 2 * (u - 1))
                    rows = slice(QK * (h % 2), QK * (h % 2) + QK)
                    b = 2 * (u % 2)
                    for c in range(2):
                        mm = pe.matmul(ps[:, b + c, :], m.q[rows, h // 2, i * P:(i + 1) * P],
                                       m.k[rows, h // 2, c * SEQ:(c + 1) * SEQ], start=True, stop=True)
                    mm.then_inc(qk_done, 1)

                def turn(n):
                    h, i, r = subs[n]
                    k0, w = keys(i, r)
                    pe.wait_ge(s_done, n + 1)
                    if n >= 1:
                        pe.wait_ge(st_done, n)
                    for t in range(w // P):
                        mm = pe.transpose(ps[:, 4 + t // 4, (t % 4) * P:(t % 4 + 1) * P],
                                          s_sb[n % 2][:, t * P:(t + 1) * P], ident)
                    mm.then_inc(tr_done, 1)

                def pv(n):
                    h, i, r = subs[n]
                    k0, w = keys(i, r)
                    pe.wait_ge(st_done, n + 1)
                    if n >= 2:
                        pe.wait_ge(h_done, n - 1)
                    for t in range(w // P):
                        tile = (k0 // P + t + 4) % 6
                        mm = pe.matmul(ps[:, 6 + n % 2, 0:DV], st_sb[n % 2][:, t * P:(t + 1) * P],
                                       m.v[:, tile, h * DV:(h + 1) * DV], start=(t == 0), stop=(t == w // P - 1))
                    mm.then_inc(pv_done, 1)

                qk(0)
                for n in range(len(subs)):
                    if n % 2 == 0 and n // 2 + 1 < len(units):
                        qk(n // 2 + 1)
                    turn(n)
                    if n >= 1:
                        pv(n - 1)
                pv(len(subs) - 1)
                for i in range(TT):
                    pe.wait_ge(mixed, i + 1)
                for j in range(4):
                    for i in range(TT):
                        mm = pe.transpose(ps[:, j, i * P:(i + 1) * P], hout[:, i, j * P:(j + 1) * P], ident)
                    mm.then_inc(mt_done, 1)


def project_out(m, w_dram, src, bias=None, dst=None):
    nc, ps = m.nc, m.ps
    stack, sb, sem = m.open()
    with stack:
        raw = sb("w_out", [P, KT, D])
        w = [Split(sb, f"w{s}", [P, D]) for s in range(2)]
        h = [Split(sb, f"h{s}", [P, SEQ]) for s in range(2)]
        raw_in = [sem(f"raw_in{k}") for k in range(KT)]
        high_done, low_done, used, done = (sem(n) for n in ("high_done", "low_done", "used", "done"))
        with nc.Block() as block:
            @block.sync
            def _(sp):
                for k in range(KT):
                    sp.dma_start(raw[:, k, :], w_dram[:, k * D:(k + 1) * D]).then_inc(raw_in[k], 16)

            @block.scalar
            def _(act):
                for k in range(KT):
                    s = k % 2
                    if k >= 2:
                        act.wait_ge(used, k - 1)
                    act.activation(h[s].high[:], src[:, k, 0:SEQ], ACT.Copy).then_inc(high_done, 1)
                    act.wait_ge(raw_in[k], 16)
                    act.activation(w[s].high[:], raw[:, k, :], ACT.Copy).then_inc(high_done, 1)

            @block.vector
            def _(dve):
                for k in range(KT):
                    s = k % 2
                    dve.wait_ge(high_done, 2 * k + 1)
                    dve.tensor_tensor(h[s].low[:], src[:, k, 0:SEQ], h[s].high[:].bitcast(F32), ALU.subtract).then_inc(low_done, 1)
                    dve.wait_ge(high_done, 2 * k + 2)
                    dve.tensor_tensor(w[s].low[:], raw[:, k, :], w[s].high[:].bitcast(F32), ALU.subtract).then_inc(low_done, 1)
                for j in range(KT):
                    dve.wait_ge(done, j + 1)
                    if dst is None:
                        dve.tensor_tensor(m.x[:, j, 0:SEQ], ps[:, j, :], m.x[:, j, 0:SEQ], ALU.add)
                    else:
                        dve.tensor_scalar(dst[:, j, :], ps[:, j, :], VEC.of(m.vec, bias, j, 1), None, ALU.add)

            @block.tensor
            def _(pe):
                for k in range(KT):
                    s = k % 2
                    pe.wait_ge(high_done, 2 * k + 2)
                    for j in range(KT):
                        pe.matmul(ps[:, j, :], w[s].high[:, j * P:(j + 1) * P], h[s].high[:], start=(k == 0), stop=False)
                    pe.wait_ge(low_done, 2 * k + 2)
                    for j in range(KT):
                        pe.matmul(ps[:, j, :], w[s].high[:, j * P:(j + 1) * P], h[s].low[:], start=False, stop=False)
                        mm = pe.matmul(ps[:, j, :], w[s].low[:, j * P:(j + 1) * P], h[s].high[:], start=False, stop=(k == KT - 1))
                        if k == KT - 1:
                            mm.then_inc(done, 1)
                    if k < KT - 1:
                        mm.then_inc(used, 1)


def route(m, d, scratch, y):
    nc, ps = m.nc, m.ps
    stack, sb, sem = m.open()
    TE = TT * N_EXP
    with stack:
        wr, wgu, wdn = sb("w_router", [P, KT, N_EXP]), sb("ws_gu", [P, KT, 2 * D_EXP]), sb("ws_dn", [P, 2, D])
        rows = [sb(f"rows{i}", [P, D]) for i in range(2)]
        s, biased, rest = sb("s", [P, TT, N_EXP]), sb("biased", [P, TT, N_EXP]), sb("rest", [P, TT, N_EXP])
        mask, top, sums = sb("mask", [P, TT, N_EXP]), sb("top", [P, TT, 8]), sb("sums", [P, 2, TT])
        held, nblk = sb("held", [P, TT, N_EXP]), sb("nblk", [P, 2, N_EXP])
        ends, base, zero = sb("ends", [P, N_EXP]), sb("base", [P, N_EXP]), sb("zero", [P, N_EXP])
        owner, owner_i, pairs = sb("owner", [P, 3]), sb("owner_i", [P, 1], I32), sb("pairs", [P, 2])
        sg, hs = sb("shared_gate", [P, 2, SEQ]), sb("shared_h", [P, 2, SEQ])
        stored = [sem("stored0"), sem("stored1")]
        (w_in, logits, s_done, own_s, tr_done, tr_copied, mask_done, rank_done, owner_done, owner_out,
         gu_done, sg_done, hs_done, y_done) = (
            sem(n) for n in ("w_in", "logits", "s_done", "own", "tr_done", "tr_copied", "mask_done", "rank_done",
                             "owner_done", "owner_out", "gu_done", "sg_done", "hs_done", "y_done"))
        with nc.Block() as block:
            @block.sync
            def _(sp):
                for to, name in ((wr, "w_router"), (wgu, "ws_gu"), (wdn, "ws_dn")):
                    sp.dma_start(to[:].rearrange("p k n -> p (k n)"), d[name]).then_inc(w_in, 16)
                for i in range(TT):
                    sp.wait_ge(tr_copied, i + 1)
                    sp.dma_start(scratch["h_rows"][i * P:(i + 1) * P, :], rows[i % 2][:]).then_inc(stored[i % 2], 16)
                sp.wait_ge(owner_done, 1)
                sp.dma_start(scratch["block_expert"], owner_i[:]).then_inc(owner_out, 16)
                sp.wait_ge(owner_out, 16)
                sp.dma_start(m.owner_row[:], scratch["block_expert"].rearrange("p o -> o p")).then_inc(owner_out, 16)
                sp.wait_ge(owner_out, 32)
                for q in stored:
                    sp.wait_ge(q, 16 * (TT // 2))

            @block.tensor
            def _(pe):
                ident = CONST.of(m.const, "ident")
                pe.wait_ge(w_in, 48)
                for i in range(TT):
                    for k in range(KT):
                        mm = pe.matmul(ps[:, 0, i * N_EXP:(i + 1) * N_EXP], m.h[:, k, i * P:(i + 1) * P], wr[:, k, :],
                                       start=(k == 0), stop=(k == KT - 1))
                mm.then_inc(logits, 1)
                for i in range(TT):
                    if i >= 1:
                        pe.wait_ge(tr_copied, i)
                    for k in range(KT):
                        mm = pe.transpose(ps[:, 1 + k // 4, (k % 4) * P:(k % 4 + 1) * P], m.h[:, k, i * P:(i + 1) * P], ident)
                    mm.then_inc(tr_done, 1)
                for j in range(4):
                    for k in range(KT):
                        mm = pe.matmul(ps[:, 3 + j, :], wgu[:, k, j * P:(j + 1) * P], m.h[:, k, 0:SEQ],
                                       start=(k == 0), stop=(k == KT - 1))
                    mm.then_inc(gu_done, 1)
                pe.wait_ge(mask_done, 1)
                for i in range(TT):
                    to = ps[:, 0, i * N_EXP:(i + 1) * N_EXP]
                    pe.matmul(to, CONST.of(m.const, "before"), mask[:, i, :], start=True, stop=(i == 0))
                    for j in range(i):
                        pe.matmul(to, CONST.of(m.const, "ones"), mask[:, j, :], start=False, stop=(j == i - 1))
                for i in range(TT):
                    mm = pe.matmul(ps[:, 0, TE:TE + N_EXP], CONST.of(m.const, "ones"), mask[:, i, :],
                                   start=(i == 0), stop=(i == TT - 1))
                mm.then_inc(rank_done, 1)
                for j in range(KT):
                    if j == 0:
                        pe.wait_ge(hs_done, 2)
                        pe.wait_ge(tr_copied, TT)
                    if j >= 2:
                        pe.wait_ge(y_done, j - 1)
                    for k in range(2):
                        mm = pe.matmul(ps[:, 1 + j % 2, :], wdn[:, k, j * P:(j + 1) * P], hs[:, k, :], start=(k == 0), stop=(k == 1))
                    mm.then_inc(gu_done, 1)

            @block.scalar
            def _(act):
                act.wait_ge(logits, 1)
                act.activation(s[:].rearrange("p i e -> p (i e)"), ps[:, 0, 0:TE], ACT.Sigmoid).then_inc(s_done, 1)
                for i in range(TT):
                    act.wait_ge(tr_done, i + 1)
                    if i >= 2:
                        act.wait_ge(stored[i % 2], 16 * (i // 2))
                    act.activation(rows[i % 2][:, 0:512], ps[:, 1, :], ACT.Copy)
                    act.activation(rows[i % 2][:, 512:], ps[:, 2, :], ACT.Copy).then_inc(tr_copied, 1)
                for j in range(2):
                    act.wait_ge(gu_done, j + 1)
                    act.activation(sg[:, j, :], ps[:, 3 + j, :], ACT.Silu).then_inc(sg_done, 1)
                for j in range(KT):
                    act.wait_ge(gu_done, 5 + j)
                    act.activation(y[:, j, :], ps[:, 1 + j % 2, :], ACT.Copy).then_inc(y_done, 1)

            @block.vector
            def _(dve):
                own = Steps(own_s)
                own(dve, dve.memset(zero[:], 0.0))
                dve.wait_ge(s_done, 1)
                for i in range(TT):
                    ins = dve.tensor_tensor(biased[:, i, :], s[:, i, :], ROWV.of(m.rowv, "b_router"), ALU.add)
                own(dve, ins)
                for i in range(TT):
                    ins = dve.max(top[:, i, :], biased[:, i, :])
                own(dve, ins)
                for i in range(TT):
                    ins = dve.match_replace(rest[:, i, :], top[:, i, :], biased[:, i, :], NEG)
                own(dve, ins)
                ins = dve.tensor_tensor(mask[:], rest[:], biased[:], ALU.not_equal)
                ins.then_inc(mask_done, 1)
                dve.wait_ge(mask_done, 1)
                for i in range(TT):
                    ins = dve.tensor_tensor_reduce(biased[:, i, :], s[:, i, :], mask[:, i, :], 1.0, 0.0, ALU.mult, ALU.add,
                                                   sums[:, 0, i:i + 1])
                own(dve, ins)
                own(dve, dve.reciprocal(sums[:, 1, :], sums[:, 0, :]))
                token = CONST.of(m.const, "token")
                for i in range(TT):
                    dve.tensor_scalar(m.moved[:, i, :, 1], biased[:, i, :], sums[:, 1, i:i + 1], ROUTE_SCALE, ALU.mult, ALU.mult)
                    dve.tensor_scalar(m.moved[:, i, :, 0], mask[:, i, :], 0.0, token[:, i:i + 1], ALU.mult, ALU.add)
                    ins = dve.tensor_tensor_scan(held[:, i, :], mask[:, i, :], zero[:], 0.0, ALU.add, ALU.add)
                own(dve, ins)
                for i in range(TT):
                    ins = dve.tensor_scalar(rest[:, i, :], held[:, i, :], float(SEQ), token[:, i:i + 1], ALU.mult, ALU.add)
                own(dve, ins)
                for i in range(TT):
                    dve.tensor_scalar(m.moved[:, i, :, 2], rest[:, i, :], float(1 - SEQ), None, ALU.add)
                dve.wait_ge(rank_done, 1)
                count = ps[:, 0, TE:TE + N_EXP]
                own(dve, dve.tensor_scalar(nblk[:, 0, :], count, 0.0, None, ALU.is_gt))
                for j in range(1, TT):
                    own(dve, dve.scalar_tensor_tensor(nblk[:, j % 2, :], count, float(P * j), nblk[:, (j + 1) % 2, :],
                                                      ALU.is_gt, ALU.add))
                n_of = nblk[:, (TT - 1) % 2, :]
                own(dve, dve.tensor_tensor_scan(ends[:], n_of, zero[:], 0.0, ALU.add, ALU.add))
                own(dve, dve.tensor_tensor(base[:], ends[:], n_of, ALU.subtract))
                own(dve, dve.tensor_scalar(base[:], base[:], float(P), 1.0, ALU.mult, ALU.add))
                for i in range(TT):
                    ins = dve.tensor_tensor(rest[:, i, :], ps[:, 0, i * N_EXP:(i + 1) * N_EXP], base[:], ALU.add)
                own(dve, ins)
                own(dve, dve.tensor_tensor(held[:], rest[:], mask[:], ALU.mult))
                dve.tensor_scalar(m.dest[:], held[:], 1.0, None, ALU.subtract)
                own(dve, dve.tensor_scalar(nblk[:, 0, :], ends[:], CONST.of(m.const, "part"), None, ALU.is_le))
                own(dve, dve.reduce_sum(owner[:, 0:1], nblk[:, 0, :], mybir.AxisListType.X))
                own(dve, dve.tensor_scalar(owner[:, 1:2], owner[:, 0:1], float(N_EXP - 1), None, ALU.min))
                dve.tensor_copy(owner_i[:], owner[:, 1:2]).then_inc(owner_done, 1)
                own(dve, dve.tensor_scalar(nblk[:, 0, :], CONST.of(m.const, "slot", 0, N_EXP), 2.0, ends[:, N_EXP - 1:N_EXP],
                                           ALU.mult, ALU.is_lt))
                own(dve, dve.reduce_sum(pairs[:, 0:1], nblk[:, 0, :], mybir.AxisListType.X))
                dve.tensor_scalar(m.pairs_i[:], pairs[:, 0:1], 1.0, None, ALU.subtract)
                for j in range(2):
                    dve.wait_ge(sg_done, j + 1)
                    dve.wait_ge(gu_done, 3 + j)
                    dve.tensor_tensor(hs[:, j, :], sg[:, j, :], ps[:, 5 + j, :], ALU.mult).then_inc(hs_done, 1)


def experts(m, d, scratch):
    nc, ps = m.nc, m.ps
    stack, sb, sem = m.open()
    GU, BI, BT, BG, BU, BA, BY = KT * 2 * D_EXP, 0, 1, 3, 4, 5, 6
    with stack:
        gu = [sb(f"w_gu{s}", [P, KT, 2 * D_EXP]) for s in range(2)]
        dn = [sb(f"w_dn{s}", [P, 2, D]) for s in range(2)]
        pick, cols = sb("pick", [P, TT, P]), sb("cols", [P, TT, 3])
        raw = [sb(f"raw{s}", [P, 3]) for s in range(2)]
        token_i, target = sb("token_i", [P, 1], I32), sb("target", [P, 2])
        target_i = [sb(f"target_i{s}", [P, 1], I32) for s in range(2)]
        xg, xt = sb("x_rows", [P, D]), sb("x_t", [P, KT, P])
        sg, a, at = sb("silu_gate", [P, D_EXP]), sb("act", [P, D_EXP]), sb("act_t", [P, 2, P])
        yb, spare = sb("y_block", [P, D]), sb("spare", [P, 2])
        gu_in, dn_in = [sem("gu_in0"), sem("gu_in1")], [sem("dn_in0"), sem("dn_in1")]
        (picked, found, listed, gathered, xt_turned, xt_done, gate_done, up_done, sg_done,
         a_done, a_turned, at_done, y_made, y_out, scattered, target_done, own_s, issued) = (
            sem(n) for n in ("picked", "found", "listed", "gathered", "xt_turned", "xt_done",
                             "gate_done", "up_done", "sg_done", "a_done", "a_turned", "at_done", "y_made", "y_out",
                             "scattered", "target_done", "own", "issued"))
        least, last = SEQ * TOP_K // P // 2 - 1, (MAX_BLOCKS + 1) // 2 - 1

        with nc.Block() as block:
            @block.sync
            def _(sp):
                rest = sp.value_load(m.pairs_i[0:1, 0:1], min_val=least, max_val=last)

                def load(to, name, arrived, n, used=None, uses=None):
                    e = sp.value_load(m.owner_row[0:1, bass.ds(value(n), 1)], min_val=0, max_val=N_EXP - 1)
                    if used is not None:
                        sp.wait_ge(used, value(uses))
                    sp.dma_start(to[:].rearrange("p k n -> p (k n)"), d[name][e]).then_inc(arrived, 16)

                def load_gu(n, s):
                    load(gu[s], "w_gu", gu_in[s], n, up_done, n - 1)

                def load_dn(n, s):
                    load(dn[s], "w_dn", dn_in[s], n, y_made, 2 * n - 2)

                for s in range(2):
                    load(gu[s], "w_gu", gu_in[s], s)
                    load(dn[s], "w_dn", dn_in[s], s)
                load_gu(2, 0)
                load_gu(3, 1)
                load_dn(2, 0)
                with sp.Fori(2, rest + 1) as g:
                    for s in range(2):
                        load_gu(Count(g, 2, s), s)
                        load_dn(Count(g, 2, s - 1), 1 - s)
                load_dn(Count(rest, 2, 1), 1)

            @block.tensor
            def _(pe):
                ident = CONST.of(m.const, "ident")
                rest = pe.value_load(m.pairs_i[0:1, 0:1], min_val=least, max_val=last)

                def find(n):
                    pe.wait_ge(picked, value(n + 1))
                    for i in range(TT):
                        mm = pe.matmul(ps[:, BI, 0:3], pick[:, i, :], cols[:, i, :], start=(i == 0), stop=(i == TT - 1))
                    mm.then_inc(found, 1)

                def turn(half):
                    for k in range(4):
                        mm = pe.transpose(ps[:, BT + half, k * P:(k + 1) * P], xg[:, (4 * half + k) * P:(4 * half + k + 1) * P], ident)
                    mm.then_inc(xt_turned, 1)

                def gate_and_up(b, s, loaded):
                    pe.wait_ge(xt_done, value(2 * b + 2))
                    pe.wait_ge(gu_in[s], loaded)
                    pe.wait_ge(sg_done, value(b + 1))
                    for k in range(KT):
                        mm = pe.matmul(ps[:, BG, 0:D_EXP], xt[:, k, :], gu[s][:, k, 0:D_EXP], start=(k == 0), stop=(k == KT - 1))
                    mm.then_inc(gate_done, 1)
                    pe.wait_ge(a_done, value(b + 1))
                    for k in range(KT):
                        mm = pe.matmul(ps[:, BU, 0:D_EXP], xt[:, k, :], gu[s][:, k, D_EXP:], start=(k == 0), stop=(k == KT - 1))
                    mm.then_inc(up_done, 1)

                def down(c, s, loaded):
                    pe.wait_ge(at_done, value(c + 1))
                    pe.wait_ge(dn_in[s], loaded)
                    for n in range(2):
                        pe.wait_ge(y_out, value(2 * c + n + 1))
                        for j in range(2):
                            mm = pe.matmul(ps[:, BY + n, :], at[:, j, :], dn[s][:, j, n * 512:(n + 1) * 512],
                                           start=(j == 0), stop=(j == 1))
                        mm.then_inc(y_made, 1)

                def step(b, s, gu_loaded, dn_loaded):
                    gate_and_up(b, s, gu_loaded)
                    pe.wait_ge(gathered, value(16 * b + 32))
                    turn(0)
                    turn(1)
                    find(b + 2)
                    if dn_loaded is not None:
                        down(b - 1, 1 - s, dn_loaded)
                    pe.wait_ge(a_done, value(b + 2))
                    for j in range(2):
                        mm = pe.transpose(ps[:, BA, j * P:(j + 1) * P], a[:, j * P:(j + 1) * P], ident)
                    mm.then_inc(a_turned, 1)

                find(0)
                pe.wait_ge(gathered, 16)
                turn(0)
                turn(1)
                find(1)
                step(0, 0, 16, None)
                with pe.Fori(0, rest) as g:
                    step(Count(g, 2, 1), 1, 16 * g + 16, 16 * g + 16)
                    step(Count(g, 2, 2), 0, 16 * g + 32, 16 * g + 16)
                step(Count(rest, 2, 1), 1, 16 * rest + 16, 16 * rest + 16)
                down(Count(rest, 2, 1), 1, 16 * rest + 16)

            @block.scalar
            def _(act):
                rest = act.value_load(m.pairs_i[0:1, 0:1], min_val=least, max_val=last)
                act.sem_inc(sg_done, 1)
                act.sem_inc(y_out, 2)

                def copy_x(n):
                    for half in range(2):
                        act.wait_ge(xt_turned, value(n + (half + 1)))
                        act.activation(xt[:, 4 * half:4 * half + 4, :].rearrange("p k t -> p (k t)"), ps[:, BT + half, :],
                                       ACT.Copy).then_inc(xt_done, 1)

                def copy_y(c):
                    for n in range(2):
                        act.wait_ge(scattered, value(16 * c + 16))
                        act.wait_ge(y_made, value(2 * c + n + 1))
                        act.activation(yb[:, n * 512:(n + 1) * 512], ps[:, BY + n, :], ACT.Copy).then_inc(y_out, 1)

                def step(b, first=False):
                    act.wait_ge(a_done, value(b + 1))
                    act.wait_ge(gate_done, value(b + 1))
                    act.activation(sg[:], ps[:, BG, 0:D_EXP], ACT.Silu).then_inc(sg_done, 1)
                    act.wait_ge(up_done, value(b + 1))
                    copy_x(2 * b + 2)
                    if not first:
                        copy_y(b - 1)
                    act.wait_ge(a_turned, value(b + 1))
                    act.activation(at[:].rearrange("p j t -> p (j t)"), ps[:, BA, 0:2 * P], ACT.Copy).then_inc(at_done, 1)

                copy_x(0)
                step(0, True)
                with act.Fori(0, rest) as g:
                    for s in range(2):
                        step(Count(g, 2, s + 1))
                step(Count(rest, 2, 1))
                copy_y(Count(rest, 2, 1))

            @block.vector
            def _(dve):
                rest = dve.value_load(m.pairs_i[0:1, 0:1], min_val=least, max_val=last)
                dve.sem_inc(a_done, 1)
                slot, neg_block = CONST.of(m.const, "slot"), CONST.of(m.const, "neg_block")

                def choose(n):
                    e = dve.value_load(m.owner_row[0:1, bass.ds(n, 1)], min_val=0, max_val=N_EXP - 1)
                    for i in range(TT):
                        dve.tensor_scalar(pick[:, i, :], slot, m.dest[:, i, bass.ds(e, 1)], neg_block[:, bass.ds(n, 1)],
                                          ALU.subtract, ALU.is_equal)
                    dve.tensor_copy(cols[:], m.moved[:, :, bass.ds(e, 1), :].rearrange("p i o c -> p i (o c)")).then_inc(picked, 1)

                def read_tokens(n, s):
                    dve.wait_ge(found, n + 1)
                    dve.tensor_copy(token_i[:], ps[:, BI, 0:1])
                    dve.tensor_copy(raw[s][:], ps[:, BI, 0:3]).then_inc(listed, 1)

                choose(0)
                read_tokens(0, 0)
                choose(1)
                dve.wait_ge(gathered, 16)
                read_tokens(1, 1)
                choose(2)
                with dve.Fori(0, rest + 1) as g:
                    for s in range(2):
                        b = 2 * g + s
                        dve.wait_ge(up_done, b + 1)
                        dve.wait_ge(sg_done, b + 2)
                        dve.wait_ge(listed, b + 1)
                        dve.scalar_tensor_tensor(a[:], ps[:, BU, 0:D_EXP], raw[s][:, 1:2], sg[:], ALU.mult, ALU.mult).then_inc(a_done, 1)
                        dve.tensor_scalar(target[:, 0:1], raw[s][:, 2:3], 0.0, 1.0e6, ALU.is_equal, ALU.mult).then_inc(own_s, 1)
                        dve.wait_ge(own_s, 2 * b + 1)
                        dve.tensor_tensor(target[:, 1:2], target[:, 0:1], raw[s][:, 2:3], ALU.add).then_inc(own_s, 1)
                        dve.wait_ge(own_s, 2 * b + 2)
                        dve.wait_ge(gathered, 16 * b + 32)
                        read_tokens(b + 2, s)
                        choose(b + 3)
                        dve.wait_ge(y_out, 2 * b + 2)
                        dve.tensor_scalar(target_i[s][:], target[:, 1:2], 1.0, None, ALU.subtract).then_inc(target_done, 1)

            @block.gpsimd
            def _(pool):
                rest = pool.value_load(m.pairs_i[0:1, 0:1], min_val=least, max_val=last)

                def gather():
                    pool.indirect_dma_start(xg[:], None, scratch["h_rows"], bass.IndirectOffsetOnAxis(ap=token_i[:, 0:1], axis=0),
                                            bounds_check=SEQ - 1, oob_is_err=False).then_inc(gathered, 16)

                pool.dma_start(spare[:], d["const"][:, 0:2]).then_inc(scattered, 16)
                def next_rows(n):
                    pool.wait_ge(listed, value(n + 1))
                    pool.wait_ge(xt_turned, value(2 * n))
                    pool.sem_inc(issued, 1)
                    gather()

                def store(c, s):
                    pool.wait_ge(target_done, value(c + 1))
                    pool.wait_ge(y_out, value(2 * c + 4))
                    pool.sem_inc(issued, 1)
                    pool.indirect_dma_start(scratch["y_rows"], bass.IndirectOffsetOnAxis(ap=target_i[s][:, 0:1], axis=0), yb[:], None,
                                            bounds_check=TOP_K * SEQ - 1, oob_is_err=False).then_inc(scattered, 16)

                pool.wait_ge(listed, 1)
                gather()
                next_rows(1)
                next_rows(2)
                with pool.Fori(0, rest) as g:
                    for s in range(2):
                        next_rows(Count(g, 2, s + 3))
                        store(Count(g, 2, s), s)
                next_rows(Count(rest, 2, 3))
                store(Count(rest, 2, 0), 0)
                store(Count(rest, 2, 1), 1)
                pool.wait_ge(gathered, 32 * rest + 64)
                pool.sem_inc(issued, 1)
                pool.wait_ge(scattered, 32 * rest + 48)
                pool.sem_inc(issued, 1)


def combine(m, scratch, y):
    nc, ps = m.nc, m.ps
    stack, sb, sem = m.open()
    with stack:
        rows = [sb(f"expert_rows{i}", [P, TOP_K, D]) for i in range(2)]
        rows_in = [sem("rows_in0"), sem("rows_in1")]
        turned, added = sem("turned"), sem("added")
        src = scratch["y_rows"].rearrange("(c i p) n -> i p c n", c=TOP_K, p=P)
        with nc.Block() as block:
            @block.sync
            def _(sp):
                for i in range(TT):
                    if i >= 2:
                        sp.wait_ge(turned, 2 * (i - 1))
                    sp.dma_start(rows[i % 2][:], src[i]).then_inc(rows_in[i % 2], 16)

            @block.tensor
            def _(pe):
                for i in range(TT):
                    pe.wait_ge(rows_in[i % 2], 16 * (i // 2) + 16)
                    for half in range(2):
                        n = 2 * i + half
                        if n >= 4:
                            pe.wait_ge(added, n - 3)
                        for k in range(4):
                            at = (4 * half + k) * P
                            for c in range(TOP_K):
                                mm = pe.matmul(ps[:, n % 4, k * P:(k + 1) * P], rows[i % 2][:, c, at:at + P],
                                               CONST.of(m.const, "ident"), start=(c == 0), stop=(c == TOP_K - 1), is_transpose=True)
                        mm.then_inc(turned, 1)

            @block.vector
            def _(dve):
                for i in range(TT):
                    for half in range(2):
                        n = 2 * i + half
                        to = y[:, 4 * half:4 * half + 4, i * P:(i + 1) * P]
                        dve.wait_ge(turned, n + 1)
                        dve.tensor_tensor(to, ps[:, n % 4, :].rearrange("p (k t) -> p k t", k=4), to, ALU.add).then_inc(added, 1)


def attention(m, d, w_name, o, diff):
    nc, ps = m.nc, m.ps
    stack, sb, sem = m.open()
    BT, BO, BP = 4, 6, 7
    U = 1 if diff else 2
    with stack:
        w = [sb(f"w_qkv{s}", [P, 3, KT, P]) for s in range(2)]
        ws = [Split(sb, n, [P, KT, P]) for n in ("w_q", "w_k")]
        rope, amask = sb("rope", [P, 2, SEQ]), sb("amask", [P, 4, SEQ])
        q, k = [sb(f"q{s}", [P, SEQ]) for s in range(2)], [sb(f"k{s}", [P, SEQ]) for s in range(2)]
        v = [sb(f"v{s}", [P, TT, P]) for s in range(2)]
        mask_now = sb("mask_now", [P, SEQ])
        straight, crossed = sb("straight", [P, SEQ]), sb("crossed", [P, SEQ])
        sm = [sb(f"scores{u}", [P, TT, SEQ]) for u in range(2)]
        pt = sb("scores_t", [P, TT, SEQ])
        low = [sb(f"least{u}", [P, TT]) for u in range(2)]
        den = [sb(f"den{u}", [P, 3, TT]) for u in range(2)]
        w_in, tables_in = [sem("w_in0"), sem("w_in1")], sem("tables_in")
        (q_made, k_made, v_made, q_ready, k_ready, v_ready, s_made, masked, e_done, p_ready, turned, pt_done, o_made,
         o_copied, own_s, own_p, own_rope, seen, mask_set, high_done, low_done) = (
            sem(n) for n in ("q_made", "k_made", "v_made", "q_ready", "k_ready", "v_ready", "s_made", "masked", "e_done",
                             "p_ready", "turned", "pt_done", "o_made", "o_copied", "own", "own_p", "own_rope", "seen", "mask_set", "high_done", "low_done"))

        def weights(s):
            return w[s][:].rearrange("p c k n -> p (c k n)")

        def steps(eng, emit):
            with eng.Fori(0, 3) as g:
                for s in range(2):
                    emit(2 * g + s, s, g, True)
            for s in range(2):
                emit(6 + s, s, None, s == 0)

        def width(i):
            return P * (i + 1)

        with nc.Block() as block:
            @block.sync
            def _(sp):
                for s in range(2):
                    sp.dma_start(weights(s), d[w_name][s]).then_inc(w_in[s], 16)
                sp.dma_start(rope[:].rearrange("p a t -> p (a t)"), d["rope"]).then_inc(tables_in, 16)
                sp.dma_start(amask[:].rearrange("p a t -> p (a t)"), d["amask"]).then_inc(tables_in, 16)
                with sp.Fori(1, 4) as g:
                    for s in range(2):
                        sp.wait_ge(v_made, 2 * g - 1 + s)
                        sp.dma_start(weights(s), d[w_name][2 * g + s]).then_inc(w_in[s], 16)

            @block.tensor
            def _(pe):
                ident = CONST.of(m.const, "ident")

                def project(j, s, part, first=False):
                    if part < 2:
                        pe.wait_ge(low_done, 2 * j + part + 1)
                    if part == 0:
                        if not first:
                            pe.wait_ge(v_ready, j)
                    else:
                        pe.wait_ge(q_ready if part == 1 else k_ready, j + 1)
                    if part < 2:
                        for kk in range(KT):
                            for i, (wp, hp) in enumerate(ws[part].passes(m.hs)):
                                mm = pe.matmul(ps[:, BP, :], wp[:, kk, :], hp[:, kk, :], start=(kk == 0 and i == 0),
                                               stop=(kk == KT - 1 and i == 2))
                    else:
                        for i in range(TT):
                            for kk in range(KT):
                                mm = pe.matmul(ps[:, BP, i * P:(i + 1) * P], m.h[:, kk, i * P:(i + 1) * P], w[s][:, 2, kk, :],
                                               start=(kk == 0), stop=(kk == KT - 1))
                    mm.then_inc((q_made, k_made, v_made)[part], 1)

                def scores(j, s, u):
                    if u == 0:
                        pe.wait_ge(k_ready, j + 1)
                    pe.wait_ge(masked, 8 * j + 4 * u + 4)
                    rows = slice(HD * u, HD * u + HD)
                    for i in range(TT):
                        mm = pe.matmul(ps[:, i, 0:width(i)], q[s][rows, i * P:(i + 1) * P], k[s][rows, 0:width(i)],
                                       start=True, stop=True)
                    mm.then_inc(s_made, 1)

                def turn(n, of):
                    pe.wait_ge(p_ready, n + 1)
                    for t in range(TT):
                        pe.wait_ge(pt_done, 4 * n + t + 1)
                        for i in range(t, TT):
                            mm = pe.transpose(ps[:, BT + t % 2, (i - t) * P:(i - t + 1) * P], sm[of][:, i, t * P:(t + 1) * P], ident)
                        mm.then_inc(turned, 1)

                def product(j, n, s, u):
                    rows = slice(0, P) if diff else slice(HD * u, HD * u + HD)
                    if u == 0:
                        pe.wait_ge(o_copied, j + 1)
                        pe.wait_ge(v_ready, j + 1)
                    for t in range(TT):
                        pe.wait_ge(pt_done, 4 * n + t + 3)
                        mm = pe.matmul(ps[rows, BO, t * P:], v[s][:, t, rows], pt[:, t, 0:SEQ - t * P], start=(t == 0), stop=(t == TT - 1))
                    mm.then_inc(o_made, 1)

                def step(j, s, g, more):
                    scores(j, s, 0)
                    if more:
                        project(j + 1, 1 - s, 0)
                    scores(j, s, 1)
                    if not diff:
                        turn(2 * j, 0)
                    if more:
                        project(j + 1, 1 - s, 1)
                    if not diff:
                        product(j, 2 * j, s, 0)
                        turn(2 * j + 1, 1)
                    else:
                        turn(j, 0)
                    if more:
                        project(j + 1, 1 - s, 2)
                    product(j, 2 * j + 1 if not diff else j, s, 1 if not diff else 0)

                pe.sem_inc(turned, 8)
                pe.sem_inc(o_made, 1)
                for part in range(3):
                    project(0, 0, part, True)
                steps(pe, step)

            @block.scalar
            def _(act):
                act.sem_inc(pt_done, 2)

                def exps(j, u):
                    for i in range(TT):
                        act.wait_ge(masked, 8 * j + 4 * u + i + 5)
                        act.activation(sm[u][:, i, 0:width(i)], sm[u][:, i, 0:width(i)], ACT.Exp, scale=-1.0,
                                       bias=low[u][:, i:i + 1], accum_out=den[u][:, 0, i:i + 1]).then_inc(e_done, 1)

                def copy_t(n):
                    act.wait_ge(o_made, n + 1)
                    for t in range(TT):
                        act.wait_ge(turned, 4 * n + t + 9)
                        act.activation(pt[:, t, 0:SEQ - t * P], ps[:, BT + t % 2, 0:SEQ - t * P], ACT.Copy).then_inc(pt_done, 1)

                def copy_v(j, s):
                    act.wait_ge(v_made, j + 1)
                    act.activation(v[s][:].rearrange("p i n -> p (i n)"), ps[:, BP, :], ACT.Copy).then_inc(v_ready, 1)

                def high_parts(n, s, loads):
                    act.wait_ge(w_in[s], loads)
                    for part in range(2):
                        if not isinstance(n, int) or n > 0:
                            act.wait_ge((q_made, k_made)[part], n)
                        act.activation(ws[part].high[:], w[s][:, part], ACT.Copy).then_inc(high_done, 1)

                def step(j, s, g, more):
                    exps(j, 0)
                    if not diff:
                        copy_t(2 * j)
                    exps(j, 1)
                    copy_t(j if diff else 2 * j + 1)
                    if more:
                        copy_v(j + 1, 1 - s)
                    if g is not None:
                        high_parts(j + 2, s, 16 * g + 32)

                high_parts(0, 0, 16)
                high_parts(1, 1, 16)
                copy_v(0, 0)
                steps(act, step)

            @block.vector
            def _(dve):
                dve.sem_inc(masked, 4)
                dve.sem_inc(o_copied, 1)

                def rotate(j, s, part):
                    dve.wait_ge((q_made, k_made)[part], j + 1)
                    src, to, ready = ps[:, BP, :], (q, k)[part][s], (q_ready, k_ready)[part]
                    dve.tensor_tensor(straight[:], src, rope[:, 0, :], ALU.mult)
                    for a in range(4):
                        b = a ^ 1
                        ins = dve.tensor_tensor(crossed[32 * b:32 * b + 32, :], src[32 * a:32 * a + 32, :],
                                                rope[32 * a:32 * a + 32, 1, :], ALU.mult)
                    ins.then_inc(own_rope, 1)
                    dve.wait_ge(own_rope, 2 * j + part + 1)
                    dve.tensor_tensor(to[:], straight[:], crossed[:], ALU.add).then_inc(ready, 1)
                    dve.wait_ge(ready, j + 1)

                def mask(j, g, u):
                    if diff:
                        dve.wait_ge(*((turned, 4 * j + 8) if u == 0 else (own_p, j + 1)))
                    else:
                        dve.wait_ge(turned, 8 * j + 4 * u + 4)
                    dve.wait_ge(s_made, 2 * j + u + 1)
                    dve.sem_inc(seen, 1)
                    for i in range(TT):
                        dve.tensor_tensor_reduce(sm[u][:, i, 0:width(i)], ps[:, i, 0:width(i)], mask_now[:, SEQ - width(i):],
                                                 -HD ** -0.5, 3.0e38, ALU.add, ALU.min, low[u][:, i:i + 1]).then_inc(masked, 1)

                def normalise(j, u):
                    dve.wait_ge(e_done, 8 * j + 4 * u + 4)
                    dve.reciprocal(den[u][:, 1, :], den[u][:, 0, :]).then_inc(own_s, 1)
                    n = (3 if diff else 2) * j + u + 1
                    dve.wait_ge(own_s, n)
                    if diff and u == 1:
                        dve.tensor_scalar(den[1][:, 2, :], den[1][:, 1, :], m.neg_lambda[:, 0:1], None, ALU.mult).then_inc(own_s, 1)
                        dve.wait_ge(own_s, n + 1)
                    for i in range(TT):
                        p0 = sm[0][:, i, 0:width(i)]
                        if diff and u == 1:
                            ins = dve.scalar_tensor_tensor(p0, sm[1][:, i, 0:width(i)], den[1][:, 2, i:i + 1], p0, ALU.mult, ALU.add)
                        else:
                            pu = sm[u][:, i, 0:width(i)]
                            ins = dve.tensor_scalar(pu, pu, den[u][:, 1, i:i + 1], None, ALU.mult)
                    if not diff or u == 1:
                        ins.then_inc(p_ready, 1)
                    else:
                        ins.then_inc(own_p, 1)
                        dve.wait_ge(own_p, j + 1)

                def low_parts(n, s, part):
                    dve.wait_ge(high_done, 2 * n + part + 1)
                    dve.tensor_tensor(ws[part].low[:], w[s][:, part], ws[part].high[:].bitcast(F32), ALU.subtract).then_inc(low_done, 1)

                def step(j, s, g, more):
                    if s == 0 and not diff:
                        dve.wait_ge(masked, 8 * j + 4)
                        dve.tensor_copy(mask_now[:], amask[:, bass.ds(3 if g is None else g, 1), :].rearrange("p a t -> p (a t)")).then_inc(mask_set, 1)
                        dve.wait_ge(mask_set, 4 if g is None else g + 1)
                    mask(j, g, 0)
                    normalise(j, 0)
                    if more:
                        rotate(j + 1, 1 - s, 0)
                    mask(j, g, 1)
                    normalise(j, 1)
                    if more:
                        rotate(j + 1, 1 - s, 1)
                    dve.wait_ge(o_made, U * (j + 1) + 1)
                    dve.tensor_copy(o[:, bass.ds(j, 1), :].rearrange("p a t -> p (a t)"), ps[:, BO, :]).then_inc(o_copied, 1)
                    if g is not None:
                        low_parts(j + 2, s, 0)
                        low_parts(j + 2, s, 1)

                low_parts(0, 0, 0)
                low_parts(0, 0, 1)
                dve.wait_ge(tables_in, 32)
                if diff:
                    dve.tensor_copy(mask_now[:], amask[:, 0, :]).then_inc(mask_set, 1)
                    dve.wait_ge(mask_set, 1)
                rotate(0, 0, 0)
                low_parts(1, 1, 0)
                rotate(0, 0, 1)
                low_parts(1, 1, 1)
                steps(dve, step)


def lambda_value(m):
    nc, ps = m.nc, m.ps
    stack, sb, sem = m.open()
    with stack:
        prod, e = sb("prod", [P, 2]), sb("e", [P, 2])
        prod_done, dot_done, e_done, own_s = sem("prod_done"), sem("dot_done"), sem("e_done"), sem("own")
        with nc.Block() as block:
            @block.vector
            def _(dve):
                own = Steps(own_s)
                vec = VEC.of(m.vec, "lambda")
                dve.tensor_tensor(prod[:], vec[:, 0::2], vec[:, 1::2], ALU.mult).then_inc(prod_done, 1)
                dve.wait_ge(e_done, 1)
                own(dve, dve.tensor_tensor(prod[:, 0:1], e[:, 1:2], e[:, 0:1], ALU.subtract))
                dve.tensor_scalar(m.neg_lambda[:], prod[:, 0:1], LAMBDA_INIT, None, ALU.subtract)

            @block.tensor
            def _(pe):
                pe.wait_ge(prod_done, 1)
                pe.matmul(ps[:, 0, 0:2], CONST.of(m.const, "ones"), prod[:], start=True, stop=True).then_inc(dot_done, 1)

            @block.scalar
            def _(act):
                act.wait_ge(dot_done, 1)
                act.activation(e[:], ps[:, 0, 0:2], ACT.Exp).then_inc(e_done, 1)


def head_norm(m, o):
    nc, ps = m.nc, m.ps
    stack, sb, sem = m.open()
    with stack:
        sq = [sb(f"sq{i}", [P, SEQ]) for i in range(2)]
        std = [sb(f"std{i}", [P, SEQ]) for i in range(2)]
        g = sb("g", [P, 1])
        sq_done, ms_done, std_done, rstd_done, out_done = (
            sem(n) for n in ("sq_done", "ms_done", "std_done", "rstd_done", "out_done"))
        with nc.Block() as block:
            @block.scalar
            def _(act):
                for j in range(N_PAIR + 1):
                    if j < N_PAIR:
                        if j >= 2:
                            act.wait_ge(ms_done, j - 1)
                        act.activation(sq[j % 2][:], o[:, j, :], ACT.Square).then_inc(sq_done, 1)
                    if j >= 1:
                        i = j - 1
                        act.wait_ge(ms_done, i + 1)
                        if i >= 2:
                            act.wait_ge(out_done, i - 1)
                        act.activation(std[i % 2][:], ps[:, i % 4, :], ACT.Sqrt, bias=CONST.of(m.const, "diff_eps")).then_inc(std_done, 1)

            @block.tensor
            def _(pe):
                for j in range(N_PAIR):
                    pe.wait_ge(sq_done, j + 1)
                    if j >= 4:
                        pe.wait_ge(std_done, j - 3)
                    pe.matmul(ps[:, j % 4, :], CONST.of(m.const, "inv_v"), sq[j % 2][:], start=True, stop=True).then_inc(ms_done, 1)

            @block.vector
            def _(dve):
                dve.tensor_scalar(g[:], VEC.of(m.vec, "subln"), 1.0 - LAMBDA_INIT, None, ALU.mult).then_inc(rstd_done, 1)
                for j in range(N_PAIR):
                    dve.wait_ge(std_done, j + 1)
                    dve.reciprocal(std[j % 2][:], std[j % 2][:]).then_inc(rstd_done, 1)
                    dve.wait_ge(rstd_done, j + 2)
                    dve.scalar_tensor_tensor(o[:, j, :], o[:, j, :], g[:, 0:1], std[j % 2][:], ALU.mult, ALU.mult).then_inc(out_done, 1)


def conv_ffn(m, d, layer):
    nc, ps = m.nc, m.ps
    stack, sb, sem = m.open()
    base = VEC.at["ffn_conv"][0] + layer * FT * 8
    PARTS = [(0, 12), (12, FT)]
    W = 2 * KT * P
    with stack:
        raw = [sb(f"raw{s}", [P, W]) for s in range(2)]
        w = [Split(sb, f"w{s}", [P, W]) for s in range(2)]
        hid = Split(sb, "hidden", [P, 12, SEQ])
        y = [sb(f"conv{s}", [P, 2, SEQ]) for s in range(2)]
        gate = [sb(f"gate{s}", [P, SEQ]) for s in range(2)]
        raw_in = [sem("raw_in0"), sem("raw_in1")]
        (high_done, low_done, used, up_made, tap0, tap1, conv_done, gate_done, gate_free, prod_done, hid_high, hid_low,
         down_made, added) = (
            sem(n) for n in ("high_done", "low_done", "used", "up_made", "tap0", "tap1", "conv_done", "gate_done", "gate_free",
                             "prod_done", "hid_high", "hid_low", "down_made", "added"))
        n0 = [0, PARTS[0][1] + KT]
        JOBS = n0[1] + PARTS[1][1] - PARTS[1][0] + KT

        def tap(j, which, c):
            return m.vec[:, bass.ds(base + 8 * j + 4 * which + c, 1)]

        def loads(part):
            a, b = PARTS[part]
            return [(n0[part], b - a, W), (n0[part] + b - a, KT, (b - a) * P)]

        def size_after(n):
            for part in range(2):
                for first, count, cols in loads(part):
                    if first <= n < first + count:
                        return cols
            return 0

        def in_pairs(eng, emit):
            for part in range(2):
                for down, (first, count, cols) in enumerate(loads(part)):
                    with eng.Fori(0, count // 2 - 1) as g:
                        for s in range(2):
                            emit(part, down, first + 2 * g + s, 2 * g + s, s, cols)
                    for s in range(2):
                        n = first + count - 2 + s
                        emit(part, down, n, count - 2 + s, s, size_after(n + 1))

        with nc.Block() as block:
            @block.sync
            def _(sp):
                def load(part, down, n, j, s, first=False):
                    a, b = PARTS[part]
                    src = d["w_down"][layer][j][:, a * P:b * P] if down else d["w_up"][layer][a + j]
                    if not first:
                        sp.wait_ge(low_done, n - 1)
                    sp.dma_start(raw[s][:, 0:(b - a) * P] if down else raw[s][:], src).then_inc(raw_in[s], 16)

                for part in range(2):
                    for down, (first, count, _) in enumerate(loads(part)):
                        start = 1 if first == 0 else 0
                        if start:
                            load(0, 0, 0, 0, 0, True)
                            load(0, 0, 1, 1, 1, True)
                        with sp.Fori(start, count // 2) as g:
                            for s in range(2):
                                load(part, down, first + 2 * g + s, 2 * g + s, s)

            @block.tensor
            def _(pe):
                def job(part, down, n, j, s, _):
                    a, b = PARTS[part]
                    pe.wait_ge(low_done, n + 1)
                    if not down:
                        pe.wait_ge(conv_done, 2 * (PARTS[part][0] + j) + 2)
                        for c in range(2):
                            for k in range(KT):
                                at = (c * KT + k) * P
                                for i, (wp, hp) in enumerate(w[s].passes(m.hs)):
                                    mm = pe.matmul(ps[:, 2 * s + c, :], wp[:, at:at + P], hp[:, k, :],
                                                   start=(k == 0 and i == 0), stop=(k == KT - 1 and i == 2))
                            mm.then_inc(up_made if c == 0 else used, 1)
                    else:
                        pe.wait_ge(hid_low, b - 1)
                        pe.wait_ge(added, KT * part + j + 1)
                        for k in range(b - a):
                            if k == b - a - 1:
                                pe.wait_ge(hid_low, b)
                            for i, (wp, hp) in enumerate(w[s].passes(hid)):
                                mm = pe.matmul(ps[:, 4 + s, :], wp[:, k * P:(k + 1) * P], hp[:, k, :],
                                               start=(k == 0 and i == 0), stop=(k == b - a - 1 and i == 2))
                        mm.then_inc(used, 1)
                pe.sem_inc(used, 1)
                in_pairs(pe, job)

            @block.scalar
            def _(act):
                def high(n, s, cols, first=False):
                    if cols == 0:
                        return
                    act.wait_ge(raw_in[s], 8 * (n - s) + 16)
                    if not first:
                        act.wait_ge(used, n)
                    act.activation(w[s].high[:, 0:cols], raw[s][:, 0:cols], ACT.Copy).then_inc(high_done, 1)

                def job(part, down, n, j, s, cols):
                    high(n + 1, 1 - s, cols)
                    if down:
                        return
                    t = PARTS[part][0] + j
                    for c in range(2):
                        act.wait_ge(*((up_made, t + 1) if c == 0 else (used, n + 2)))
                        act.wait_ge(gate_free, t + 1)
                        act.activation(y[s][:, c, :], ps[:, 2 * s + c, :], ACT.Identity, scale=tap(t, c, 2),
                                       bias=tap(t, c, 3)).then_inc(tap0, 1)
                    act.wait_ge(conv_done, 2 * t + 5)
                    act.activation(gate[s][:], y[s][:, 0, :], ACT.Silu).then_inc(gate_done, 1)
                    act.wait_ge(prod_done, t + 1)
                    act.activation(hid.high[:, bass.ds(j, 1), :].rearrange("p a t -> p (a t)"), gate[s][:], ACT.Copy).then_inc(hid_high, 1)

                high(0, 0, W, True)
                in_pairs(act, job)

            @block.vector
            def _(dve):
                dve.sem_inc(conv_done, 4)
                dve.sem_inc(gate_free, 2)
                dve.sem_inc(added, 2)

                def low(n, s, cols):
                    if cols == 0:
                        return
                    dve.wait_ge(high_done, n + 1)
                    dve.tensor_tensor(w[s].low[:, 0:cols], raw[s][:, 0:cols], w[s].high[:, 0:cols].bitcast(F32),
                                      ALU.subtract).then_inc(low_done, 1)

                def job(part, down, n, j, s, cols):
                    low(n + 1, 1 - s, cols)
                    if down:
                        to = m.x[:, bass.ds(j, 1), 0:SEQ].rearrange("p a t -> p (a t)")
                        dve.wait_ge(used, n + 2)
                        dve.tensor_tensor(to, ps[:, 4 + s, :], to, ALU.add).then_inc(added, 1)
                        return
                    t = PARTS[part][0] + j
                    for c in range(2):
                        dve.wait_ge(tap0, 2 * t + c + 1)
                        src = ps[:, 2 * s + c, :]
                        dve.scalar_tensor_tensor(y[s][:, c, 1:], src[:, 0:SEQ - 1], tap(t, c, 1), y[s][:, c, 1:],
                                                 ALU.mult, ALU.add).then_inc(tap1, 1)
                        dve.wait_ge(tap1, 2 * t + c + 1)
                        dve.scalar_tensor_tensor(y[s][:, c, 2:], src[:, 0:SEQ - 2], tap(t, c, 0), y[s][:, c, 2:],
                                                 ALU.mult, ALU.add).then_inc(conv_done, 1)
                    dve.wait_ge(gate_done, t + 1)
                    dve.wait_ge(conv_done, 2 * t + 6)
                    dve.tensor_tensor(gate[s][:], gate[s][:], y[s][:, 1, :], ALU.mult).then_inc(prod_done, 1)
                    dve.wait_ge(hid_high, t + 1)
                    slot = bass.ds(j, 1)
                    dve.tensor_tensor(hid.low[:, slot, :].rearrange("p a t -> p (a t)"), gate[s][:],
                                      hid.high[:, slot, :].rearrange("p a t -> p (a t)").bitcast(F32), ALU.subtract).then_inc(hid_low, 1)
                    dve.wait_ge(hid_low, t + 1)
                    dve.sem_inc(gate_free, 1)

                low(0, 0, W)
                in_pairs(dve, job)


def program(nc, d, out, scratch):
    stack = ExitStack()
    m = Machine(nc, stack)
    with stack:
        _, sb, sem = m.open(stack)
        m.x_in = sem("x_in")
        m.ps = stack.enter_context(nc.psum_tensor("banks", [P, 8, 512], F32))
        m.vec, m.rowv, m.const = sb("vec", [P, VEC.n]), sb("rowv", [P, ROWV.n]), sb("const", [P, CONST.n])
        m.x = sb("x", [P, KT, ALLT])
        m.mod, m.gain = sb("mod", [P, 96]), sb("gain", [P, KT, 2])
        m.neg_lambda = sb("neg_lambda", [P, 1])
        m.scratch1, m.scratch2 = sb("scratch1", [P, 2]), sb("scratch2", [P, 2])

        def mod(part):
            return lambda k, g: m.mod[:, 2 * (KT * part + k) + g:2 * (KT * part + k) + g + 1]

        def gain(k, g=0):
            return m.gain[:, k, g:g + 1]

        def norm_gain(name, at):
            return lambda k, g: VEC.of(m.vec, name, at + k, 1)

        load_and_modulation(m, d)
        modulation_gain(m, "g_pre_mix", 1)
        s1, sb1, _ = m.open()
        with s1:
            mix = sb1("mix", [P, KT, SEQ])
            s2, sb2, _ = m.open()
            with s2:
                m.q, m.k = sb2("q", [P, 2, SEQ]), sb2("k", [P, 2, CTX + SEQ + CTX])
                m.v, m.so, m.gates = sb2("v", [P, ALLT // P, D_ML]), sb2("so", [P, TT, D_ML]), sb2("gates", [16, ALLT])
                s3, sb3, _ = m.open()
                with s3:
                    m.h = sb3("h", [P, KT, ALLT])
                    rms_norm(m, m.x, m.h, [(0, SEQ), (SEQ, CTX)], gain, mod(0))
                    project_in(m, d, mix)
                mlstm(m, d, mix)
            y = sb1("y", [P, KT, SEQ])
            project_out(m, d["w_out"], mix, "b_out", y)
            gate_gain(m, "g_post_mix", 2)
            add_normed(m, y, gain)
        modulation_gain(m, "g_pre_ffn", 4)
        s1, sb1, _ = m.open()
        with s1:
            y = sb1("y", [P, KT, SEQ])
            m.dest, m.moved = sb1("dest", [P, TT, N_EXP]), sb1("moved", [P, TT, N_EXP, 3])
            m.owner_row, m.pairs_i = sb1("owner_row", [1, P], I32), sb1("pairs_i", [P, 1], I32)
            s2, sb2, _ = m.open()
            with s2:
                m.h = sb2("h", [P, KT, SEQ])
                rms_norm(m, m.x, m.h, [(0, SEQ)], gain, mod(3))
                route(m, d, scratch, y)
            experts(m, d, scratch)
            combine(m, scratch, y)
            gate_gain(m, "g_post_ffn", 5)
            add_normed(m, y, gain)
        lambda_value(m)
        for layer in range(2):
            s1, sb1, _ = m.open()
            with s1:
                o = sb1("o", [P, KT, SEQ])
                s2, sb2, _ = m.open()
                with s2:
                    m.h, m.hs = sb2("h", [P, KT, SEQ]), Split(sb2, "h", [P, KT, SEQ])
                    rms_norm(m, m.x, m.hs, [(0, SEQ)], norm_gain(("even_norm", "odd_norm")[layer], 0), whole=m.h)
                    attention(m, d, ("w_even", "w_odd")[layer], o, layer == 1)
                if layer == 1:
                    head_norm(m, o)
                project_out(m, d[("w_eo", "w_oo")[layer]], o)
            s1, sb1, _ = m.open()
            with s1:
                m.hs = Split(sb1, "h", [P, KT, SEQ])
                rms_norm(m, m.x, m.hs, [(0, SEQ)], norm_gain("ffn_norm", layer * KT))
                conv_ffn(m, d, layer)
        s1, sb1, _ = m.open()
        with s1:
            y = sb1("y", [P, KT, SEQ])
            rms_norm(m, m.x, y, [(0, SEQ)], norm_gain("final_norm", 0), out=out)


def kernel(**inputs):
    import concourse.bacc as bacc
    from concourse.bass_utils import run_bass_kernel_spmd as run

    nc = bacc.Bacc("TRN2", target_bir_lowering=False, num_devices=1)
    arrays = {**constants(), **layouts(**{k: np.asarray(v) for k, v in inputs.items()})}
    d = {name: nc.dram_tensor(f"in_{name}", a.shape, F32, kind="ExternalInput").ap() for name, a in arrays.items()}
    out = nc.dram_tensor("out", (P, KT, SEQ), F32, kind="ExternalOutput").ap()
    scratch = {
        "h_rows": nc.dram_tensor("h_rows", (SEQ, D), F32).ap(),
        "y_rows": nc.dram_tensor("y_rows", (TOP_K * SEQ, D), F32).ap(),
        "block_expert": nc.dram_tensor("block_expert", (P, 1), I32).ap(),
    }
    program(nc, d, out, scratch)
    r = run(nc, [{f"in_{name}": a for name, a in arrays.items()}], core_ids=[0])
    y = r.results[0]["out"]
    return np.ascontiguousarray(y.transpose(2, 1, 0)).reshape(1, SEQ, D)
```
